# Optimizing a Trainium2 kernel written in Bass

```python
import math
import jax, jax.numpy as jnp
from jax import lax
import numpy as np

D_MODEL = 1024
BATCH = 1
SEQ = 256
DEPTH = 1

N_DIFF_HEADS = 4
DIFF_HEAD_DIM = 64
DIFF_V_DIM = 2 * DIFF_HEAD_DIM
DIFF_WIDTH = N_DIFF_HEADS * DIFF_V_DIM
N_MLSTM_HEADS = 4
MLSTM_QK_DIM = 64
MLSTM_V_DIM = 128
MLSTM_WIDTH = N_MLSTM_HEADS * MLSTM_V_DIM
MIX_WIDTH = DIFF_WIDTH + MLSTM_WIDTH
CONV_WIDTH = 4
CHUNK = 64
Q_BLOCK = 128
D_FF = 4 * D_MODEL
ROPE_THETA = 10000.0
EPS = 1e-6

IN_SIZES = (
    N_DIFF_HEADS * 2 * DIFF_HEAD_DIM,
    N_DIFF_HEADS * 2 * DIFF_HEAD_DIM,
    DIFF_WIDTH,
    N_MLSTM_HEADS * MLSTM_QK_DIM,
    N_MLSTM_HEADS * MLSTM_QK_DIM,
    MLSTM_WIDTH,
    MLSTM_WIDTH,
    N_MLSTM_HEADS,
    N_MLSTM_HEADS,
)
IN_WIDTH = sum(IN_SIZES)
IN_OFFSETS = tuple(int(o) for o in np.cumsum(IN_SIZES)[:-1])
CONV_CH = 2 * N_MLSTM_HEADS * MLSTM_QK_DIM


def lambda_init(layer):
    return 0.8 - 0.6 * math.exp(-0.3 * layer)

def rmsnorm(x, g):
    xf = x.astype(jnp.float32)
    y = xf * lax.rsqrt(jnp.mean(xf * xf, axis=-1, keepdims=True) + EPS)
    return (y * g.astype(jnp.float32)).astype(x.dtype)

def rope(x, pos):
    d = x.shape[-1]
    inv = ROPE_THETA ** (-jnp.arange(0, d, 2, dtype=jnp.float32) / d)
    ang = pos.astype(jnp.float32)[:, None] * inv[None, :]
    cos = jnp.cos(ang)[None, :, None, :]
    sin = jnp.sin(ang)[None, :, None, :]
    xf = x.astype(jnp.float32)
    x1, x2 = xf[..., : d // 2], xf[..., d // 2:]
    out = jnp.concatenate([x1 * cos - x2 * sin, x2 * cos + x1 * sin], axis=-1)
    return out.astype(x.dtype)

def diff_attention(q, k, v, lam):
    S = q.shape[3]
    scale = DIFF_HEAD_DIM ** -0.5
    outs = []
    for blk in range(S // Q_BLOCK):
        lo, hi = blk * Q_BLOCK, (blk + 1) * Q_BLOCK
        qb = q[:, :, :, lo:hi]
        kb = k[:, :, :, :hi]
        s = jnp.einsum('bhcqd,bhckd->bhcqk', qb, kb).astype(jnp.float32) * scale
        mask = (lo + jnp.arange(Q_BLOCK))[:, None] >= jnp.arange(hi)[None, :]
        s = jnp.where(mask, s, -jnp.inf)
        p = jax.nn.softmax(s, axis=-1)
        p_diff = p[:, :, 0] - lam * p[:, :, 1]
        outs.append(jnp.einsum('bhqk,bhkv->bhqv', p_diff.astype(v.dtype), v[:, :, :hi]))
    return jnp.concatenate(outs, axis=2)

def mlstm_chunkwise(q, k, v, i_pre, logf):
    B, H, S, dqk = q.shape
    dv = v.shape[-1]
    nc = S // CHUNK
    q = q * (dqk ** -0.5)

    def chunked(t):
        t = t.reshape(t.shape[:2] + (nc, CHUNK) + t.shape[3:])
        return jnp.moveaxis(t, 2, 0)

    xs = (chunked(q), chunked(k), chunked(v), chunked(i_pre), chunked(logf))
    causal = jnp.tril(jnp.ones((CHUNK, CHUNK), dtype=bool))

    def step(carry, inp):
        C, n, m = carry
        qc, kc, vc, ic, fc = inp
        b = jnp.cumsum(fc, axis=-1)
        g = b[..., -1]
        logD = b[..., :, None] - b[..., None, :] + ic[..., None, :]
        logD = jnp.where(causal, logD, -jnp.inf)
        inter = b + m[..., None]
        m_comb = jnp.maximum(inter, jnp.max(logD, axis=-1))
        scores = jnp.einsum('bhjd,bhsd->bhjs', qc, kc) * jnp.exp(logD - m_comb[..., None])
        w_inter = jnp.exp(inter - m_comb)
        num = (w_inter[..., None] * jnp.einsum('bhjd,bhdv->bhjv', qc, C)
               + jnp.einsum('bhjs,bhsv->bhjv', scores, vc))
        den = w_inter * jnp.einsum('bhjd,bhd->bhj', qc, n) + jnp.sum(scores, axis=-1)
        h = num / jnp.maximum(jnp.abs(den), jnp.exp(-m_comb))[..., None]
        log_w = g[..., None] - b + ic
        m_new = jnp.maximum(g + m, jnp.max(log_w, axis=-1))
        decay = jnp.exp(g + m - m_new)
        w = jnp.exp(log_w - m_new[..., None])
        C_new = decay[..., None, None] * C + jnp.einsum('bhs,bhsd,bhsv->bhdv', w, kc, vc)
        n_new = decay[..., None] * n + jnp.einsum('bhs,bhsd->bhd', w, kc)
        return (C_new, n_new, m_new), h

    init = (jnp.zeros((B, H, dqk, dv), jnp.float32),
            jnp.zeros((B, H, dqk), jnp.float32),
            jnp.zeros((B, H), jnp.float32))
    _, hs = lax.scan(step, init, xs)
    return jnp.moveaxis(hs, 0, 2).reshape(B, H, S, dv)

def causal_dwconv(x, w, b):
    S = x.shape[1]
    xp = jnp.pad(x, ((0, 0), (CONV_WIDTH - 1, 0), (0, 0)))
    y = b
    for j in range(CONV_WIDTH):
        y = y + w[j] * xp[:, j:j + S]
    return y

def first_inputs(seed: int = 0) -> dict:
    key = jax.random.key(seed)
    ks = jax.random.split(key, 20)
    f32 = jnp.float32
    nrm = lambda k, shape, s: jax.random.normal(k, shape, f32) * s
    gain = lambda k, shape: 1.0 + 0.05 * jax.random.normal(k, shape, f32)
    return {
        "x": jax.random.normal(ks[0], (BATCH, SEQ, D_MODEL), f32),
        "norm_mix_pre": gain(ks[1], (DEPTH, D_MODEL)),
        "w_in": nrm(ks[2], (DEPTH, D_MODEL, IN_WIDTH), D_MODEL ** -0.5),
        "conv_w": nrm(ks[3], (DEPTH, CONV_WIDTH, CONV_CH), CONV_WIDTH ** -0.5),
        "conv_b": nrm(ks[4], (DEPTH, CONV_CH), 0.01),
        "b_igate": nrm(ks[5], (DEPTH, N_MLSTM_HEADS), 0.1),
        "b_fgate": 3.0 + nrm(ks[6], (DEPTH, N_MLSTM_HEADS), 0.5),
        "lambda_q1": nrm(ks[7], (DEPTH, DIFF_HEAD_DIM), 0.1),
        "lambda_k1": nrm(ks[8], (DEPTH, DIFF_HEAD_DIM), 0.1),
        "lambda_q2": nrm(ks[9], (DEPTH, DIFF_HEAD_DIM), 0.1),
        "lambda_k2": nrm(ks[10], (DEPTH, DIFF_HEAD_DIM), 0.1),
        "diff_norm": gain(ks[11], (DEPTH, DIFF_V_DIM)),
        "mlstm_norm": gain(ks[12], (DEPTH, N_MLSTM_HEADS, MLSTM_V_DIM)),
        "w_out": nrm(ks[13], (DEPTH, MIX_WIDTH, D_MODEL), MIX_WIDTH ** -0.5),
        "norm_mix_post": gain(ks[14], (DEPTH, D_MODEL)),
        "norm_mlp_pre": gain(ks[15], (DEPTH, D_MODEL)),
        "w_up": nrm(ks[16], (DEPTH, D_MODEL, D_FF), D_MODEL ** -0.5),
        "w_down": nrm(ks[17], (DEPTH, D_FF, D_MODEL), D_FF ** -0.5),
        "norm_mlp_post": gain(ks[18], (DEPTH, D_MODEL)),
    }

def first_block(x, norm_mix_pre, w_in, conv_w, conv_b, b_igate, b_fgate,
              lambda_q1, lambda_k1, lambda_q2, lambda_k2, diff_norm, mlstm_norm,
              w_out, norm_mix_post, norm_mlp_pre, w_up, w_down, norm_mlp_post):
    B, S, _ = x.shape
    pos = jnp.arange(S, dtype=jnp.int32)
    for l in range(DEPTH):
        lam_init = lambda_init(l)
        h = rmsnorm(x, norm_mix_pre[l])
        proj = h @ w_in[l]
        dq, dk, dvv, mq, mk, mv, mo, mi, mf = jnp.split(proj, IN_OFFSETS, axis=-1)

        dq = rope(dq.reshape(B, S, 2 * N_DIFF_HEADS, DIFF_HEAD_DIM), pos)
        dk = rope(dk.reshape(B, S, 2 * N_DIFF_HEADS, DIFF_HEAD_DIM), pos)
        dq = dq.reshape(B, S, N_DIFF_HEADS, 2, DIFF_HEAD_DIM).transpose(0, 2, 3, 1, 4)
        dk = dk.reshape(B, S, N_DIFF_HEADS, 2, DIFF_HEAD_DIM).transpose(0, 2, 3, 1, 4)
        dvv = dvv.reshape(B, S, N_DIFF_HEADS, DIFF_V_DIM).transpose(0, 2, 1, 3)
        lam = (jnp.exp(jnp.sum(lambda_q1[l].astype(jnp.float32) * lambda_k1[l].astype(jnp.float32)))
               - jnp.exp(jnp.sum(lambda_q2[l].astype(jnp.float32) * lambda_k2[l].astype(jnp.float32)))
               + lam_init)
        o_diff = diff_attention(dq, dk, dvv, lam)
        o_diff = rmsnorm(o_diff, diff_norm[l]) * (1.0 - lam_init)
        o_diff = o_diff.transpose(0, 2, 1, 3).reshape(B, S, DIFF_WIDTH)

        qk = causal_dwconv(jnp.concatenate([mq, mk], axis=-1), conv_w[l], conv_b[l])
        qk = jax.nn.silu(qk)
        mq, mk = qk[..., :CONV_CH // 2], qk[..., CONV_CH // 2:]
        to_heads = lambda t, d: t.reshape(B, S, N_MLSTM_HEADS, d).transpose(0, 2, 1, 3).astype(jnp.float32)
        i_pre = (mi + b_igate[l]).astype(jnp.float32).transpose(0, 2, 1)
        logf = jax.nn.log_sigmoid((mf + b_fgate[l]).astype(jnp.float32)).transpose(0, 2, 1)
        hm = mlstm_chunkwise(to_heads(mq, MLSTM_QK_DIM), to_heads(mk, MLSTM_QK_DIM),
                             to_heads(mv, MLSTM_V_DIM), i_pre, logf)
        hm = rmsnorm(hm.transpose(0, 2, 1, 3), mlstm_norm[l]).astype(x.dtype)
        o_mlstm = hm.reshape(B, S, MLSTM_WIDTH) * jax.nn.sigmoid(mo)

        mixed = jnp.concatenate([o_diff.astype(x.dtype), o_mlstm], axis=-1) @ w_out[l]
        x = x + rmsnorm(mixed, norm_mix_post[l])

        h = rmsnorm(x, norm_mlp_pre[l])
        u = jnp.square(jax.nn.relu(h @ w_up[l]))
        x = x + rmsnorm(u @ w_down[l], norm_mlp_post[l])
    return x


DEPTH_2 = 2

N_HEADS = 16
HEAD_DIM = D_MODEL // N_HEADS
ROPE_DIM = HEAD_DIM // 4
ROPE_THETA_2 = 500000.0
ATTN_SCALE = HEAD_DIM ** -0.5
DILATED_PAIRS = ((128, 1), (512, 4), (2048, 16))
N_DIL = len(DILATED_PAIRS)
BAND_BLOCK = 128
MOBA_BLOCK = 256
MOBA_TOPK = 3
MOBA_QCHUNK = 128
D_FF_2 = 2816
CONV_WIDTH_2 = 3
RMS_EPS = 1e-6
N_LAYERS_A = (DEPTH_2 + 1) // 2
N_LAYERS_B = DEPTH_2 // 2


def rmsnorm_2(x, gain):
    xf = x.astype(jnp.float32)
    y = xf * lax.rsqrt(jnp.mean(xf * xf, axis=-1, keepdims=True) + RMS_EPS)
    return (y * gain.astype(jnp.float32)).astype(x.dtype)

def rope_tables(seq_len):
    pos = jnp.arange(seq_len, dtype=jnp.float32)
    inv_freq = ROPE_THETA_2 ** (-jnp.arange(0, ROPE_DIM, 2, dtype=jnp.float32) / ROPE_DIM)
    ang = pos[:, None] * inv_freq[None, :]
    return jnp.cos(ang), jnp.sin(ang)

def apply_partial_rope(x, cos, sin):
    extra = x.ndim - 3
    c = cos.reshape((cos.shape[0],) + (1,) * extra + (cos.shape[1],)).astype(x.dtype)
    s = sin.reshape((sin.shape[0],) + (1,) * extra + (sin.shape[1],)).astype(x.dtype)
    half = ROPE_DIM // 2
    x1, x2, xp = x[..., :half], x[..., half:ROPE_DIM], x[..., ROPE_DIM:]
    return jnp.concatenate([x1 * c - x2 * s, x2 * c + x1 * s, xp], axis=-1)

def band_attention(q, k, v, dil, window):
    S, H, hd = q.shape
    reach = window // dil
    assert reach <= BAND_BLOCK
    span = dil * BAND_BLOCK
    s_pad = -(-S // span) * span
    L = s_pad // dil
    nb = L // BAND_BLOCK

    def to_res(t):
        t = jnp.pad(t, ((0, s_pad - S), (0, 0), (0, 0)))
        return t.reshape(L, dil, H, hd).transpose(1, 0, 2, 3).reshape(dil, nb, BAND_BLOCK, H, hd)

    qr, kr, vr = to_res(q), to_res(k), to_res(v)

    def with_prev(t):
        prev = jnp.concatenate([jnp.zeros_like(t[:, :1]), t[:, :-1]], axis=1)
        return jnp.concatenate([prev, t], axis=2)

    kc, vc = with_prev(kr), with_prev(vr)
    scores = jnp.einsum('rnqhd,rnkhd->rnhqk', qr, kc).astype(jnp.float32) * ATTN_SCALE
    qi = jnp.arange(BAND_BLOCK)
    kj = jnp.arange(2 * BAND_BLOCK)
    dist = qi[:, None] + BAND_BLOCK - kj[None, :]
    kpos = jnp.arange(nb)[:, None] * BAND_BLOCK - BAND_BLOCK + kj[None, :]
    mask = ((dist >= 0) & (dist <= reach))[None] & (kpos >= 0)[:, None, :]
    scores = jnp.where(mask[None, :, None], scores, -jnp.inf)
    m = scores.max(axis=-1)
    p = jnp.exp(scores - m[..., None])
    den = p.sum(axis=-1)
    num = jnp.einsum('rnhqk,rnkhd->rnqhd', p, vc.astype(jnp.float32))
    m_t = m.transpose(0, 1, 3, 2)
    den_t = den.transpose(0, 1, 3, 2)
    o = num / den_t[..., None]

    def from_res(t):
        t = t.reshape((dil, L) + t.shape[3:])
        t = jnp.swapaxes(t, 0, 1)
        return t.reshape((s_pad,) + t.shape[2:])[:S]

    return from_res(o), from_res(m_t), from_res(den_t)

def mixer_dilated(h, w_qkv, q_gain, k_gain, w_o, cos, sin):
    B, S, _ = h.shape
    qkv = (h @ w_qkv).reshape(B, S, 3, N_DIL, N_HEADS, HEAD_DIM)
    q = apply_partial_rope(rmsnorm_2(qkv[:, :, 0], q_gain[:, None, :]), cos, sin)
    k = apply_partial_rope(rmsnorm_2(qkv[:, :, 1], k_gain[:, None, :]), cos, sin)
    v = qkv[:, :, 2]

    def one_sequence(args):
        qb, kb, vb = args
        outs, maxes, dens = [], [], []
        for g, (window, dil) in enumerate(DILATED_PAIRS):
            o, m, d = band_attention(qb[:, g], kb[:, g], vb[:, g], dil, window)
            outs.append(o)
            maxes.append(m)
            dens.append(d)
        o = jnp.stack(outs)
        m = jnp.stack(maxes)
        d = jnp.stack(dens)
        wgt = d * jnp.exp(m - m.max(axis=0, keepdims=True))
        wgt = wgt / wgt.sum(axis=0, keepdims=True)
        return jnp.einsum('gsh,gshd->shd', wgt, o)

    attn = lax.map(one_sequence, (q, k, v))
    return attn.reshape(B, S, N_HEADS * HEAD_DIM).astype(h.dtype) @ w_o

def mixer_moba(h, w_qkv, q_gain, k_gain, w_o, cos, sin):
    B, S, _ = h.shape
    qkv = (h @ w_qkv).reshape(B, S, 3, N_HEADS, HEAD_DIM)
    q = apply_partial_rope(rmsnorm_2(qkv[:, :, 0], q_gain), cos, sin)
    k = apply_partial_rope(rmsnorm_2(qkv[:, :, 1], k_gain), cos, sin)
    v = qkv[:, :, 2]
    s_pad = -(-S // MOBA_BLOCK) * MOBA_BLOCK
    nblk = s_pad // MOBA_BLOCK
    n_chunk = s_pad // MOBA_QCHUNK
    topk = min(MOBA_TOPK, nblk)

    def to_bhsd(t):
        return jnp.pad(t, ((0, 0), (0, s_pad - S), (0, 0), (0, 0))).transpose(0, 2, 1, 3)

    q, k, v = to_bhsd(q), to_bhsd(k), to_bhsd(v)
    k_blocks = k.reshape(B, N_HEADS, nblk, MOBA_BLOCK, HEAD_DIM)
    v_blocks = v.reshape(B, N_HEADS, nblk, MOBA_BLOCK, HEAD_DIM)
    k_mean = k_blocks.astype(jnp.float32).mean(axis=3)
    gate = jnp.einsum('bhsd,bhnd->bhsn', q.astype(jnp.float32), k_mean)
    own_blk = jnp.arange(s_pad) // MOBA_BLOCK
    fully_past = jnp.arange(nblk)[None, :] < own_blk[:, None]
    gate = jnp.where(fully_past, gate, -jnp.inf)
    _, sel = lax.top_k(gate, topk)

    def to_chunks(t):
        t = t.reshape(B, N_HEADS, n_chunk, MOBA_QCHUNK, t.shape[-1])
        return t.transpose(0, 2, 1, 3, 4).reshape(B * n_chunk, N_HEADS, MOBA_QCHUNK, t.shape[-1])

    q_chunks = to_chunks(q)
    sel_chunks = to_chunks(sel)
    chunk_ids = jnp.arange(B * n_chunk, dtype=jnp.int32)
    n_sel = topk * MOBA_BLOCK

    def one_chunk(args):
        qc, selc, cid = args
        b = cid // n_chunk
        c = cid % n_chunk
        kb = k_blocks[b]
        vb = v_blocks[b]
        qpos = c * MOBA_QCHUNK + jnp.arange(MOBA_QCHUNK)
        ob = (c * MOBA_QCHUNK) // MOBA_BLOCK
        h_idx = jnp.arange(N_HEADS)[:, None, None]
        k_sel = kb[h_idx, selc]
        v_sel = vb[h_idx, selc]
        s_sel = jnp.einsum('hqd,hqnkd->hqnk', qc, k_sel).astype(jnp.float32) * ATTN_SCALE
        valid = jnp.arange(topk) < ob
        s_sel = jnp.where(valid[None, None, :, None], s_sel, -jnp.inf)
        s_sel = s_sel.reshape(N_HEADS, MOBA_QCHUNK, n_sel)
        k_own = lax.dynamic_index_in_dim(kb, ob, axis=1, keepdims=False)
        v_own = lax.dynamic_index_in_dim(vb, ob, axis=1, keepdims=False)
        s_own = jnp.einsum('hqd,hkd->hqk', qc, k_own).astype(jnp.float32) * ATTN_SCALE
        kpos = ob * MOBA_BLOCK + jnp.arange(MOBA_BLOCK)
        s_own = jnp.where((kpos[None, :] <= qpos[:, None])[None], s_own, -jnp.inf)
        p = jax.nn.softmax(jnp.concatenate([s_sel, s_own], axis=-1), axis=-1).astype(v_sel.dtype)
        o = jnp.einsum('hqn,hqnd->hqd', p[..., :n_sel],
                       v_sel.reshape(N_HEADS, MOBA_QCHUNK, n_sel, HEAD_DIM))
        return o + jnp.einsum('hqk,hkd->hqd', p[..., n_sel:], v_own)

    out = lax.map(one_chunk, (q_chunks, sel_chunks, chunk_ids))
    out = out.reshape(B, n_chunk, N_HEADS, MOBA_QCHUNK, HEAD_DIM).transpose(0, 1, 3, 2, 4)
    out = out.reshape(B, s_pad, N_HEADS * HEAD_DIM)[:, :S]
    return out.astype(h.dtype) @ w_o

def conv_ffn(h, w_up, conv_w, conv_b, w_down):
    S = h.shape[1]
    u = h @ w_up
    up = jnp.pad(u, ((0, 0), (CONV_WIDTH_2 - 1, 0), (0, 0)))
    uc = conv_b + sum(conv_w[j] * up[:, j:j + S] for j in range(CONV_WIDTH_2))
    gate, val = uc[..., :D_FF_2], uc[..., D_FF_2:]
    return (jax.nn.silu(gate) * val) @ w_down

def second_inputs(seed: int = 0) -> dict:
    key = jax.random.key(seed)
    ks = jax.random.split(key, 16)
    hd_all = N_HEADS * HEAD_DIM

    def w(k, shape, fan_in):
        return jax.random.normal(k, shape, jnp.float32) * fan_in ** -0.5

    def gain(k, shape):
        return 1.0 + 0.1 * jax.random.normal(k, shape, jnp.float32)

    return {
        'x': jax.random.normal(ks[0], (BATCH, SEQ, D_MODEL), jnp.float32),
        'attn_norm': gain(ks[1], (DEPTH_2, D_MODEL)),
        'a_w_qkv': w(ks[2], (N_LAYERS_A, D_MODEL, 3 * N_DIL * hd_all), D_MODEL),
        'a_q_norm': gain(ks[3], (N_LAYERS_A, N_DIL, HEAD_DIM)),
        'a_k_norm': gain(ks[4], (N_LAYERS_A, N_DIL, HEAD_DIM)),
        'a_w_o': w(ks[5], (N_LAYERS_A, hd_all, D_MODEL), hd_all),
        'b_w_qkv': w(ks[6], (N_LAYERS_B, D_MODEL, 3 * hd_all), D_MODEL),
        'b_q_norm': gain(ks[7], (N_LAYERS_B, HEAD_DIM)),
        'b_k_norm': gain(ks[8], (N_LAYERS_B, HEAD_DIM)),
        'b_w_o': w(ks[9], (N_LAYERS_B, hd_all, D_MODEL), hd_all),
        'ffn_norm': gain(ks[10], (DEPTH_2, D_MODEL)),
        'ffn_w_up': w(ks[11], (DEPTH_2, D_MODEL, 2 * D_FF_2), D_MODEL),
        'ffn_conv_w': w(ks[12], (DEPTH_2, CONV_WIDTH_2, 2 * D_FF_2), CONV_WIDTH_2),
        'ffn_conv_b': 0.01 * jax.random.normal(ks[13], (DEPTH_2, 2 * D_FF_2), jnp.float32),
        'ffn_w_down': w(ks[14], (DEPTH_2, D_FF_2, D_MODEL), D_FF_2),
    }

def second_block(x, attn_norm, a_w_qkv, a_q_norm, a_k_norm, a_w_o,
              b_w_qkv, b_q_norm, b_k_norm, b_w_o,
              ffn_norm, ffn_w_up, ffn_conv_w, ffn_conv_b, ffn_w_down):
    cos, sin = rope_tables(x.shape[1])
    for i in range(DEPTH_2):
        hn = rmsnorm_2(x, attn_norm[i])
        if i % 2 == 0:
            j = i // 2
            x = x + mixer_dilated(hn, a_w_qkv[j], a_q_norm[j], a_k_norm[j], a_w_o[j], cos, sin)
        else:
            j = i // 2
            x = x + mixer_moba(hn, b_w_qkv[j], b_q_norm[j], b_k_norm[j], b_w_o[j], cos, sin)
        hn = rmsnorm_2(x, ffn_norm[i])
        x = x + conv_ffn(hn, ffn_w_up[i], ffn_conv_w[i], ffn_conv_b[i], ffn_w_down[i])
    return x


def setup_inputs(seed=0):
    out = dict(first_inputs(seed))
    for name, value in second_inputs(seed + 1).items():
        if name != "x":
            out[name + "_2"] = value
    return out


def reference(
    x, norm_mix_pre, w_in, conv_w, conv_b, b_igate, b_fgate, lambda_q1, lambda_k1, lambda_q2,
    lambda_k2, diff_norm, mlstm_norm, w_out, norm_mix_post, norm_mlp_pre, w_up, w_down,
    norm_mlp_post, attn_norm_2, a_w_qkv_2, a_q_norm_2, a_k_norm_2, a_w_o_2, b_w_qkv_2,
    b_q_norm_2, b_k_norm_2, b_w_o_2, ffn_norm_2, ffn_w_up_2, ffn_conv_w_2, ffn_conv_b_2,
    ffn_w_down_2,
):
    x = first_block(
        x, norm_mix_pre, w_in, conv_w, conv_b, b_igate, b_fgate, lambda_q1, lambda_k1,
        lambda_q2, lambda_k2, diff_norm, mlstm_norm, w_out, norm_mix_post, norm_mlp_pre, w_up,
        w_down, norm_mlp_post,
    )
    return second_block(
        x, attn_norm_2, a_w_qkv_2, a_q_norm_2, a_k_norm_2, a_w_o_2, b_w_qkv_2, b_q_norm_2,
        b_k_norm_2, b_w_o_2, ffn_norm_2, ffn_w_up_2, ffn_conv_w_2, ffn_conv_b_2, ffn_w_down_2,
    )


_drawn_inputs = setup_inputs


def setup_inputs(seed=0):
    import zlib

    import numpy as np

    out = dict(_drawn_inputs(seed))
    spreads = {}
    factors = {'conv_b': 5.146,
     'b_igate': 8.0,
     'lambda_q2': 5.863,
     'lambda_k2': 8.0,
     'a_q_norm_2': 5.524,
     'a_k_norm_2': 6.022,
     'b_q_norm_2': 7.272,
     'b_k_norm_2': 7.165,
     'ffn_conv_b_2': 8.0,
     'lambda_q1': 8.0,
     'lambda_k1': 8.0}
    for name, (base, spread) in spreads.items():
        noise = np.random.default_rng([zlib.crc32(name.encode()), seed]).standard_normal(out[name].shape)
        drawn = base * np.exp(spread * noise) if base else spread * noise
        out[name] = __import__('jax').numpy.asarray(drawn.astype(out[name].dtype))
    for name, factor in factors.items():
        out[name] = (out[name] * factor).astype(out[name].dtype)
    return out
```

```python
from contextlib import ExitStack, contextmanager

import numpy as np

import concourse.bass as bass
import concourse.mybir as mybir

F32 = mybir.dt.float32
F32R = mybir.dt.float32r
ALU = mybir.AluOpType
ACT = mybir.ActivationFunctionType
AX = mybir.AxisListType

P = 128
S = 256
TOK = S // P
D = 1024
KT = D // P
HD = 64
SLOTS = 4
QW = 1024
EPS = 1e-6
BIG = 1e30
LAMBDA_INIT = 0.8 - 0.6 * 1.0

NH1 = 4
VD = 128
CONV1 = 4
FF1 = 4096
U1 = FF1 // 512
NH = 16
NG = 3
ROT = 16
FF2 = 2816
U2 = FF2 // 256
DILS = ((128, 1), (512, 4), (2048, 16))


def residue_order():
    t = np.arange(S)
    return (t % 4) * 64 + (t // 4 % 4) * 16 + t // 16


def constant_tables():
    c = {}
    c["ident"] = np.eye(P)
    pos = residue_order()
    token_at = np.argsort(pos)
    src = np.arange(P)
    perm_in = np.zeros((P, P))
    perm_in[src, (src % 4) * 32 + (src // 4 % 4) * 8 + src // 16] = 1
    perm_out = np.zeros((P, P))
    perm_out[src, (src % 16) * 8 + (src // 16 % 4) * 2 + src // 64] = 1
    c["perm_in"], c["perm_out"] = perm_in, perm_out
    mask_a = np.zeros((P, TOK, 512))
    for qt in range(TOK):
        tq = token_at[qt * P:(qt + 1) * P][:, None]
        own = token_at[qt * P:(qt + 1) * P][None, :]
        for g, ks in ((0, token_at[None, :]), (1, own), (2, own)):
            window, dil = DILS[g]
            ok = (tq >= ks) & (tq - ks <= window) & ((tq - ks) % dil == 0)
            col = (0, 256, 384)[g]
            mask_a[:, qt, col:col + ks.shape[1]] = np.where(ok, 0.0, BIG)
    c["mask_a"] = mask_a
    row, col = np.arange(P)[:, None], np.arange(P)[None, :]
    c["causal"] = np.concatenate([np.zeros((P, P)), np.where(row >= col, 0.0, BIG)], 1)
    c["causal_t"] = np.concatenate([np.where(col >= row, 0.0, BIG), np.zeros((P, P))], 1)

    def rope(theta, dim, tokens):
        inv = np.float32(theta) ** (-np.arange(0, dim, 2, dtype=np.float32) / np.float32(dim))
        ang = tokens.astype(np.float32)[:, None] * inv[None, :].astype(np.float32)
        both = np.stack([np.cos(ang), np.sin(ang)])
        return both.reshape(2, TOK, P, dim // 2).transpose(2, 0, 1, 3)
    c["rope1"] = rope(10000.0, HD, np.arange(S))
    c["rope_a"] = rope(500000.0, ROT, token_at)
    c["rope_b"] = rope(500000.0, ROT, np.arange(S))
    sel = np.zeros((P, NH1, P))
    for h in range(NH1):
        sel[h, h, :] = 1
    c["sel"] = sel
    c["rotated"] = (np.arange(P) % HD < ROT).astype(np.float32)[:, None]
    return c


def pack(parts):
    where, cols, n = {}, [], 0
    for name, a in parts.items():
        flat = np.asarray(a).reshape(P, -1)
        where[name] = (n, flat.shape[1])
        cols.append(flat)
        n += flat.shape[1]
    return np.ascontiguousarray(np.concatenate(cols, 1), dtype=np.float32), where


class Stage:

    def __init__(self, name, trips=1, uses=(), quarters=(), counts=None):
        self.name, self.trips, self.uses, self.quarters = name, trips, list(uses), list(quarters)
        self.counts = dict(counts or {})
        assert trips == 1 or len(self.quarters) % SLOTS == 0


class Plan:

    def __init__(self, stages):
        self.stage, tally, self.nq = {}, {}, 0
        for s in stages:
            s.base = dict(tally)
            s.q0 = self.nq
            per = dict(s.counts)
            s.use = {}
            for name, bank in s.uses:
                s.use[name] = (bank, per.get(("bank", bank), 0))
                per[("bank", bank)] = per.get(("bank", bank), 0) + 1
            s.released = []
            for n, by in enumerate(s.quarters):
                slot = (s.q0 + n) % SLOTS
                if by is None:
                    per[("used", slot)] = per.get(("used", slot), 0) + 1
                    s.released.append((("used", slot), per[("used", slot)]))
                else:
                    s.released.append(by)
            s.per = per
            for k, v in per.items():
                tally[k] = tally.get(k, 0) + v * s.trips
            self.nq += len(s.quarters) * s.trips
            self.stage[s.name] = s
        self.total = tally

    def at(self, s, key, k, i=0):
        per = s.per.get(key, 0) if s.trips > 1 else 0
        v = s.base.get(key, 0) + k
        return v if per == 0 else i * per + v

    def filled(self, s, name, i=0):
        bank, n = s.use[name]
        return self.at(s, ("bank", bank), n + 1, i)

    def free(self, s, name, i=0):
        bank, n = s.use[name]
        return self.at(s, ("bank", bank), n, i)

    def slot(self, s, n):
        return (s.q0 + n) % SLOTS

    def turn(self, s, n, i=0, ahead=0):
        v = (s.q0 + n + ahead) // SLOTS
        return v if s.trips == 1 else i * (len(s.quarters) // SLOTS) + v


def up_names(tag):
    return [(f"{tag}{f}", 4 + f) for f in range(4)]


def norm_stage(name, **more):
    return Stage(name, uses=[(f"t{k}", k) for k in range(8)],
                 counts={"hiT": 8, "ms": 2, "rstd": 1, "xn": 2, "act_step": 1, **more})


def turn_stage(name, **more):
    return Stage(name, uses=[(f"t{k}", k) for k in range(8)], counts={"hiT": 8, **more})


def row_out_quarters():
    return [None] * 3 + ["r2"] + [None] * 3 + ["r3"]


def row_out_uses():
    return [("r0", 0), ("r2", 2), ("r1", 1), ("r3", 3)]


def attention_uses(n):
    out = []
    for u in range(n):
        out += [(f"s{u}", u % 2), (f"p{u}", 2 + u % 2), (f"o{u}", 4 + u % 2)]
    return out


def make_plan():
    in1 = Stage(
        "in1",
        uses=[("gate", 7), ("dq0", 0), ("dq1", 1), ("gate_t", 7), ("dk0", 2), ("dk1", 3)]
        + [("mqk0", 4), ("mqk1", 5), ("mqk2", 6), ("gate_m", 7), ("mqk3", 7)]
        + [("dv0", 0), ("dv1", 1), ("qt0", 6), ("qt1", 7), ("mv0", 2), ("mv1", 3)]
        + [("kt0", 6), ("kt1", 7), ("mo0", 4), ("mo1", 5)],
        quarters=[None] * 3 + ["dq1"] + [None] * 3 + ["dk1"] + [None] * 3 + ["mqk3"]
        + [None] * 3 + ["dv1"] + [None] * 3 + ["mv1"] + [None] * 3 + ["mo1"],
        counts={"gates": 5, "lnf": 2, "gate_w": 2, "rot": 4, "cv": 4, "ecv": 1, "mqk": 2, "sig": 1, "dve_step": 16})
    diff_s = Stage("diff", uses=attention_uses(8),
                   counts={"prob": 8, "pd": 8, "dve_step": 24, "oms": 8})
    mls_uses = []
    for h in range(NH1):
        mls_uses += [(f"m{h}", 6), (f"s{h}", 7), (f"o{h}", 4 + h % 2)]
    mls = Stage("mlstm", uses=mls_uses, counts={"wm": 4, "oms": 4, "dve_step": 17, "act_step": 1, "orstd": 1, "osq": 1})

    proj_a = []
    q_a = []
    for g in range(NG):
        proj_a += [(f"q{g}0", 0), (f"q{g}1", 1), (f"k{g}0", 2), (f"k{g}1", 3)]
        proj_a += [(f"qt{g}0", 6), (f"qt{g}1", 7), (f"v{g}0", 4), (f"v{g}1", 5), (f"kt{g}0", 6), (f"kt{g}1", 7)]
        q_a += [None] * 3 + [f"q{g}1"] + [None] * 3 + [f"k{g}1"] + [None] * 3 + [f"v{g}1"]
    half_a = Stage("half_a", trips=2, uses=proj_a + attention_uses(16), quarters=q_a,
                   counts={"sq": 12, "ms8": 12, "rs8": 12, "rot": 12, "act_step": 12, "prob": 16, "dve_step": 12 + 16})
    proj_b = [("q00", 0), ("q01", 1), ("k00", 2), ("k01", 3), ("qt00", 6), ("qt01", 7),
              ("v00", 4), ("v01", 5), ("kt00", 6), ("kt01", 7)]
    half_b = Stage("half_b", trips=2, uses=proj_b + attention_uses(8),
                   quarters=[None] * 3 + ["q01"] + [None] * 3 + ["k01"] + [None] * 3 + ["v01"],
                   counts={"sq": 4, "ms8": 4, "rs8": 4, "rot": 4, "act_step": 4, "prob": 8, "dve_step": 4 + 8})
    acc = [(f"acc{b}", b) for b in range(4)]

    def ffn(tag):
        up = {"cv": 4, "silu": 1, "u": 1, "uhi": 1, "ulo": 1, "dve_step": 4}
        return [
            Stage(f"ffn_{tag}_head", uses=up_names("a") + up_names("b"),
                  quarters=[None] * 3 + ["a3"] + [None] * 3 + ["b3"] + [None] * 2,
                  counts={k: 2 * v for k, v in up.items()}),
            Stage(f"ffn_{tag}_loop", trips=(U2 - 3) // 2, uses=up_names("a") + up_names("b"),
                  quarters=[None] * 3 + ["a3"] + [None] * 5 + ["b3"] + [None] * 2,
                  counts={k: 2 * v for k, v in up.items()}),
            Stage(f"ffn_{tag}_tail", uses=up_names("a") + acc,
                  quarters=[None] * 3 + ["a3"] + [None] * 3 + ["acc3"], counts=up),
        ]
    mlp_up = {"u": 1, "uhi": 1, "ulo": 1}
    stages = [
        Stage("load", counts={"dve_step": 5}),
        norm_stage("norm_in1"), in1, diff_s, mls,
        turn_stage("turn_mix"),
        Stage("out1", uses=row_out_uses(), quarters=row_out_quarters()),
        Stage("post_mix", counts={"msq": 4, "pms": 1, "rstd": 1, "act_step": 1, "x_new": 2}),
        norm_stage("norm_mlp"),
        Stage("mlp_head", uses=up_names("a") + up_names("b"),
              quarters=[None] * 3 + ["a3"] + [None] * 3 + ["b3"] + [None] * 4, counts={k: 2 * v for k, v in mlp_up.items()}),
        Stage("mlp_loop", trips=U1 - 2, uses=up_names("a"), quarters=[None] * 3 + ["a3"] + [None] * 4, counts=mlp_up),
        Stage("mlp_tail", uses=acc, quarters=[None] * 3 + ["acc3"]),
        Stage("post_mlp", counts={"msq": 4, "pms": 1, "rstd": 1, "act_step": 1, "x_new": 2}),
        norm_stage("norm_a"), half_a,
        turn_stage("turn_a"),
        Stage("out_a", uses=row_out_uses(), quarters=row_out_quarters()),
        norm_stage("norm_ffn_a"), *ffn("a"),
        norm_stage("norm_b"), half_b,
        turn_stage("turn_b"),
        Stage("out_b", uses=row_out_uses(), quarters=row_out_quarters()),
        norm_stage("norm_ffn_b"), *ffn("b"),
    ]
    return Plan(stages)


def rope_view(ap, heads, halves, dim):
    return ap.rearrange("p (h s d) -> p h s d", h=heads, s=halves, d=dim)


def blocks_kernel(nc, ins, out, at_const, at_col, at_row):
    plan = make_plan()
    st = plan.stage
    at, filled, free = plan.at, plan.filled, plan.free
    with ExitStack() as ctx:
        def sb(name, shape, dt=F32):
            return ctx.enter_context(nc.sbuf_tensor(name, shape, dt))

        def sem(name):
            return ctx.enter_context(nc.semaphore(name))

        ps = ctx.enter_context(nc.psum_tensor("ps", [P, 8, 512], F32))
        w_in = sb("w_stage", [P, SLOTS, QW])
        w_hi = sb("w_hi", [P, SLOTS, QW], F32R)
        w_lo = sb("w_lo", [P, SLOTS, QW], F32R)
        x = sb("x", [P, TOK, D])
        xn = sb("xn", [P, TOK, D])
        o_sb = sb("o_sb", [P, TOK, D])
        aT_hi = sb("aT_hi", [P, KT, S], F32R)
        aT_lo = sb("aT_lo", [P, KT, S], F32R)
        u32 = sb("u32", [P, 4 * S])
        u_hi = sb("u_hi", [P, 4 * S], F32R)
        u_lo = sb("u_lo", [P, 4 * S], F32R)
        hid = sb("hid", [P, 4, S])
        qz = sb("qz", [P, 12, 2, S])
        kT = sb("kT", [P, 12, S])
        vv = sb("vv", [P, TOK, 1536])
        sm = sb("sm", [P, 2, 512])
        prob = sb("prob", [P, 2, 512])
        pdf = sb("pdf", [P, 2, S])
        pts = sb("pts", [P, 2, 512])
        xq = sb("xq", [P, TOK, 512])
        sqb = sb("sqb", [P, TOK, 512])
        rt = sb("rt", [P, 2, P])
        consts = sb("consts", [P, sum(n for _, n in at_const.values())])
        cols = sb("cols", [P, sum(n for _, n in at_col.values())])
        rows = sb("rows", [P, sum(n for _, n in at_row.values())])
        small = sb("small", [P, 256])
        gt_in = sb("gt_in", [P, KT * 8])
        gt_hi = sb("gt_hi", [P, KT * 8], F32R)
        gt_lo = sb("gt_lo", [P, KT * 8], F32R)
        gtok = sb("gtok", [P, TOK, 8])
        gi = sb("gi", [4, S])
        atok = sb("atok", [P, 2, TOK, 4])
        tabs = sb("tabs", [P, 8, TOK, 2, ROT])
        gq = sb("gq", [P, 8])

        def const(name, *shape):
            a, n = at_const[name]
            v = consts[:, a:a + n]
            return v.rearrange(*shape[:1], **shape[1]) if shape else v

        def col(name, j=None, n=1):
            a, w = at_col[name]
            return cols[:, a:a + w] if j is None else cols[:, a + j:a + j + n]

        def row(name):
            a, n = at_row[name]
            return rows[:, a:a + n]
        ident = const("ident")
        gm = xn[0:4, :, :].rearrange("p t (r s) -> p (t r) s", s=S)
        cell = {}

        def stat(name, n=1):
            if name not in cell:
                cell[name] = (sum(m for _, m in cell.values()), n)
            a, m = cell[name]
            return small[:, a:a + m]

        mqkT = kT[:, 4:8, :]

        def vm(tok):
            return vv[:, tok, 512:512 + 4 * 132].rearrange("p (h c) -> p h c", c=132)

        full = [sem(f"full{b}") for b in range(8)]
        drained = [sem(f"drained{b}") for b in range(8)]
        loaded = [sem(f"loaded{q}") for q in range(SLOTS)]
        hi_done = [sem(f"hi_done{q}") for q in range(SLOTS)]
        lo_done = [sem(f"lo_done{q}") for q in range(SLOTS)]
        used = [sem(f"used{q}") for q in range(SLOTS)]
        s = {n: sem(n) for n in (
            "x_in", "const_in", "gate_in", "stored", "hiT", "ms", "rstd", "xn", "act_step", "dve_step",
            "gates", "lnf", "rot", "cv", "ecv", "mqk", "sig", "prob", "pd", "oms", "wm",
            "orstd", "osq", "sq", "ms8", "rs8", "silu", "u", "uhi", "ulo", "msq", "pms", "x_new", 
            "lam", "const_ready", "gate_w", "unit")}

        def is_full(stg, name, i=0):
            return full[stg.use[name][0]], filled(stg, name, i)

        def is_drained(stg, name, i=0):
            return drained[stg.use[name][0]], filled(stg, name, i)

        def is_free(stg, name, i=0):
            return drained[stg.use[name][0]], free(stg, name, i)

        def bank(stg, name):
            return stg.use[name][0]

        def was_read(stg, n, i):
            by = stg.released[n]
            if isinstance(by, str):
                return is_full(stg, by, i)
            return used[by[0][1]], at(stg, by[0], by[1], i)

        def after_post(name):
            return [(s["x_new"], at(st[name], "x_new", t + 1)) for t in range(TOK)]

        def after_sum(name, last):
            return [is_drained(st[name], last[t]) for t in range(TOK)]

        @contextmanager
        def trips(eng, stg):
            if stg.trips == 1:
                yield 0
            else:
                with eng.Fori(0, stg.trips) as i:
                    yield i

        class Chain:

            def __init__(self, eng, key):
                self.eng, self.key, self.n = eng, key, 0

            def enter(self, stg, i):
                self.stg, self.i, self.n = stg, i, 0

            def link(self, ins):
                self.n += 1
                ins.then_inc(s[self.key], 1)
                self.eng.wait_ge(s[self.key], at(self.stg, self.key, self.n, self.i))

            def leave(self):
                want = self.stg.per.get(self.key, 0)
                assert self.n == want, f"{self.stg.name} {self.key}: {self.n} increments, {want} in the plan"

        block = ctx.enter_context(nc.Block())

        @block.sync
        def _(sp):
            sp.dma_start(x[:], ins["x"].rearrange("b (t p) d -> p (b t) d", p=P)).then_inc(s["x_in"], 16)
            sp.dma_start(consts[:], ins["consts"]).then_inc(s["const_in"], 16)
            sp.dma_start(cols[:], ins["cols"]).then_inc(s["const_in"], 16)
            sp.dma_start(rows[:], ins["rows"].partition_broadcast(P)).then_inc(s["const_in"], 16)

            def k_rows(w):
                return w.rearrange("(k p) n -> p k n", p=P)

            def load_cols(stg, i, n0, w, c0):
                for q in range(4):
                    sl = slice(c0, c0 + 512) if isinstance(c0, int) else bass.ds(c0, 512)
                    slot = plan.slot(stg, n0 + q)
                    if stg.q0 + n0 + q >= SLOTS:
                        sp.wait_ge(lo_done[slot], plan.turn(stg, n0 + q, i))
                    sp.dma_start(w_in[:, slot, :].rearrange("p (k n) -> p k n", k=2),
                                 k_rows(w)[:, 2 * q:2 * q + 2, sl]).then_inc(loaded[slot], 16)

            def load_pair(stg, i, n0, w, j):
                load_cols(stg, i, n0, w, j * 512)

            def load_rows(stg, i, n0, nq, w, t0):
                for q in range(nq):
                    slot = plan.slot(stg, n0 + q)
                    if stg.q0 + n0 + q >= SLOTS:
                        sp.wait_ge(lo_done[slot], plan.turn(stg, n0 + q, i))
                    r0 = (t0 + q) * P
                    sl = slice(r0, r0 + P) if isinstance(r0, int) else bass.ds(r0, P)
                    sp.dma_start(w_in[:, slot, :], w[sl, :]).then_inc(loaded[slot], 16)

            S_ = st["in1"]
            w = ins["w_in"][0]
            for n, c0 in enumerate((0, 512, 1536, 1024, 2048, 2560)):
                load_cols(S_, 0, 4 * n, w, c0)
                if n == 0:
                    sp.dma_start(gt_in[:].rearrange("p (k n) -> p k n", k=KT),
                                 k_rows(w)[:, :, 3072:3080]).then_inc(s["gate_in"], 16)
            for n in range(2):
                load_cols(st["out1"], 0, 4 * n, ins["w_out"][0], 512 * n)
            up, down = ins["w_up"][0], ins["w_down"][0]
            S_ = st["mlp_head"]
            load_cols(S_, 0, 0, up, 0)
            load_cols(S_, 0, 4, up, 512)
            load_rows(S_, 0, 8, 4, down, 0)
            S_ = st["mlp_loop"]
            with trips(sp, S_) as i:
                load_cols(S_, i, 0, up, i * 512 + 1024)
                load_rows(S_, i, 4, 4, down, i * 4 + 4)
            load_rows(st["mlp_tail"], 0, 0, 4, down, 4 * (U1 - 1))

            def attention_weights(S_, w, groups):
                with trips(sp, S_) as i:
                    for g in range(groups):
                        for kind in range(3):
                            load_cols(S_, i, (g * 3 + kind) * 4, w, i * 512 + (kind * groups + g) * D)

            def ffn_weights(tag, layer):
                up, down = ins["ffn_w_up"][layer], ins["ffn_w_down"][layer]
                S_ = st[f"ffn_{tag}_head"]
                load_pair(S_, 0, 0, up, 0)
                load_pair(S_, 0, 4, up, 1)
                load_rows(S_, 0, 8, 2, down, 0)
                S_ = st[f"ffn_{tag}_loop"]
                with trips(sp, S_) as i:
                    load_pair(S_, i, 0, up, i * 2 + 2)
                    load_rows(S_, i, 4, 2, down, i * 4 + 2)
                    load_pair(S_, i, 6, up, i * 2 + 3)
                    load_rows(S_, i, 10, 2, down, i * 4 + 4)
                S_ = st[f"ffn_{tag}_tail"]
                load_pair(S_, 0, 0, up, U2 - 1)
                load_rows(S_, 0, 4, 4, down, 2 * (U2 - 2))

            attention_weights(st["half_a"], ins["a_w_qkv"][0], NG)
            for n in range(2):
                load_cols(st["out_a"], 0, 4 * n, ins["a_w_o"][0], 512 * n)
            ffn_weights("a", 0)
            attention_weights(st["half_b"], ins["b_w_qkv"][0], 1)
            for n in range(2):
                load_cols(st["out_b"], 0, 4 * n, ins["b_w_o"][0], 512 * n)
            ffn_weights("b", 1)
            for b, (t, h) in enumerate(((0, 0), (0, 1), (1, 0), (1, 1))):
                sp.wait_ge(*is_drained(st["ffn_b_tail"], f"acc{2 * t + h}"))
                sp.dma_start(out[0, t * P:(t + 1) * P, h * 512:(h + 1) * 512],
                             x[:, t, h * 512:(h + 1) * 512]).then_inc(s["stored"], 16)
            sp.wait_ge(s["stored"], 64)

        def units_a():
            mask = const("mask_a", "p (t c) -> p t c", dict(t=TOK))
            for pr in range(4):
                for h in range(2):
                    for qt in range(TOK):
                        q = [qz[:, g * 4 + pr, h, qt * P:(qt + 1) * P] for g in range(NG)]
                        own = slice(qt * P, (qt + 1) * P)
                        yield dict(
                            tok=qt,
                            scores=[(0, 256, q[0], kT[:, pr, :]), (256, 128, q[1], kT[:, 4 + pr, own]),
                                    (384, 128, q[2], kT[:, 8 + pr, own])],
                            segments=[(0, 512, mask[:, qt, :])],
                            tiles=4,
                            values=[(0, [(0, vv[:, 0, pr * P:(pr + 1) * P]), (1, vv[:, 1, pr * P:(pr + 1) * P]),
                                         (2, vv[:, qt, 512 + pr * P:512 + (pr + 1) * P]),
                                         (3, vv[:, qt, 1024 + pr * P:1024 + (pr + 1) * P])])],
                            outs=[(0, h * HD, pr * P + h * HD)])

        def units_pair(heads, kof, vof):
            mask = const("causal")
            for pr in range(heads):
                for qt in range(TOK):
                    W = (qt + 1) * P
                    yield dict(
                        tok=qt, head=pr,
                        scores=[(c * W, W, qz[:, pr, c, qt * P:(qt + 1) * P], kof(pr)[:, 0:W]) for c in range(2)],
                        segments=[(c * W, W, mask[:, 2 * P - W:2 * P]) for c in range(2)],
                        tiles=2 * (qt + 1),
                        values=[(c * P, [(c * (qt + 1) + t, vof(t, pr)) for t in range(qt + 1)]) for c in range(2)],
                        outs=[(c, c * P + c * HD, pr * P + c * HD) for c in range(2)])

        def units_diff():
            for u in units_pair(NH1, lambda h: kT[:, h, :], lambda t, h: vv[:, t, h * P:(h + 1) * P]):
                u["tiles"] = u["tok"] + 1
                u["values"] = u["values"][:1]
                yield u

        def units_b():
            return units_pair(4, lambda p_: kT[:, p_, :], lambda t, p_: vv[:, t, p_ * P:(p_ + 1) * P])

        @block.tensor
        def _(pe):
            def await_weights(stg, n, i):
                slot = plan.slot(stg, n)
                pe.wait_ge(lo_done[slot], plan.turn(stg, n, i) + 1)
                return slot

            def signal(stg, n, ins_):
                by = stg.released[n]
                if not isinstance(by, str):
                    ins_.then_inc(used[by[0][1]], 1)

            def dense_rows(stg, i, n0, names):
                for q in range(4):
                    slot = await_weights(stg, n0 + q, i)
                    for kk in range(2):
                        k = 2 * q + kk
                        wh, wl = (w[:, slot, kk * 512:(kk + 1) * 512] for w in (w_hi, w_lo))
                        for t in range(TOK):
                            o = ps[:, bank(stg, names[t]), :]
                            if k == 0:
                                pe.wait_ge(*is_free(stg, names[t], i))
                            ah, al = (a[:, k, t * P:(t + 1) * P] for a in (aT_hi, aT_lo))
                            pe.matmul(o, ah, wh, start=(k == 0), stop=False)
                            pe.matmul(o, ah, wl, start=False, stop=False)
                            last = pe.matmul(o, al, wh, start=False, stop=(k == KT - 1))
                            if k == KT - 1:
                                last.then_inc(full[bank(stg, names[t])], 1)
                    if q < 3:
                        signal(stg, n0 + q, last)

            def dense_cols(stg, i, n0, names):
                for q in range(4):
                    slot = await_weights(stg, n0 + q, i)
                    for kk in range(2):
                        k = 2 * q + kk
                        for f in range(4):
                            c0 = kk * 512 + f * P
                            wh, wl = (w[:, slot, c0:c0 + P] for w in (w_hi, w_lo))
                            o = ps[:, bank(stg, names[f]), 0:S]
                            if k == 0:
                                pe.wait_ge(*is_free(stg, names[f], i))
                            pe.matmul(o, wh, aT_hi[:, k, :], start=(k == 0), stop=False)
                            pe.matmul(o, wh, aT_lo[:, k, :], start=False, stop=False)
                            last = pe.matmul(o, wl, aT_hi[:, k, :], start=False, stop=(k == KT - 1))
                            if k == KT - 1:
                                last.then_inc(full[bank(stg, names[f])], 1)
                    if q < 3:
                        signal(stg, n0 + q, last)

            def down(stg, i, n0, tiles, first=False, final=False):
                for f in tiles:
                    slot = await_weights(stg, n0 + f, i)
                    for t in range(TOK):
                        ah, al = (u[:, f * S + t * P:f * S + (t + 1) * P] for u in (u_hi, u_lo))
                        for h in range(2):
                            wh, wl = (w[:, slot, h * 512:(h + 1) * 512] for w in (w_hi, w_lo))
                            o = ps[:, 2 * t + h, :]
                            b0 = first and f == tiles[0]
                            e0 = final and f == tiles[-1]
                            pe.matmul(o, ah, wh, start=b0, stop=False)
                            pe.matmul(o, ah, wl, start=False, stop=False)
                            last = pe.matmul(o, al, wh, start=False, stop=e0)
                            if e0:
                                last.then_inc(full[2 * t + h], 1)
                    if not e0:
                        signal(stg, n0 + f, last)

            def turn(stg, src, order):
                for k in range(KT):
                    if stg is not st["norm_in1"]:
                        pe.wait_ge(*is_free(stg, f"t{k}"))
                    for t in range(TOK):
                        o = ps[:, k, 0:S]
                        if order is None:
                            m, o = ident, o[:, t * P:(t + 1) * P]
                        elif order == "in":
                            m = const("perm_in")
                            o = o.rearrange("p (r t c) -> p r t c", t=TOK, c=8)[:, :, t, :]
                        else:
                            m = const("perm_out")
                            o = o.rearrange("p (r t c) -> p r t c", t=TOK, c=2)[:, :, t, :]
                        last = pe.transpose(o, src[:, t, k * P:(k + 1) * P], m)
                    last.then_inc(full[k], 1)

            def norm(stg, order=None):
                pe.wait_ge(s["xn"], at(stg, "xn", 2))
                turn(stg, xn, order)

            def attention(stg, units, i, probs, ready=None, prefix=""):
                units = list(units)
                n = len(units)
                for u in range(n + 2):
                    if u < n:
                        un = units[u]
                        b = bank(stg, f"s{u}")
                        pe.wait_ge(*is_free(stg, f"s{u}", i))
                        for c, W, q, k in un["scores"]:
                            last = pe.matmul(ps[:, b, c:c + W], q, k, start=True, stop=True)
                        last.then_inc(full[b], 1)
                    if 1 <= u <= n:
                        v = u - 1
                        b = bank(stg, f"p{v}")
                        pe.wait_ge(*is_free(stg, f"p{v}", i))
                        pe.wait_ge(s[ready], at(stg, ready, v + 1, i))
                        for t in range(units[v]["tiles"]):
                            last = pe.transpose(ps[:, b, t * P:(t + 1) * P], probs[:, v % 2, t * P:(t + 1) * P], ident)
                        last.then_inc(full[b], 1)
                    if u >= 2:
                        v = u - 2
                        b = bank(stg, f"o{v}")
                        pe.wait_ge(*is_free(stg, f"o{v}", i))
                        pe.wait_ge(*is_drained(stg, f"p{v}", i))
                        for c, pairs in units[v]["values"]:
                            for j, (t, val) in enumerate(pairs):
                                last = pe.matmul(ps[:, b, c:c + P], pts[:, v % 2, t * P:(t + 1) * P], val,
                                                 start=(j == 0), stop=(j == len(pairs) - 1))
                        last.then_inc(full[b], 1)

            def turn_heads(stg, names, i, n_rot):
                pe.wait_ge(s["rot"], at(stg, "rot", n_rot, i))
                for h in range(2):
                    b = bank(stg, names[h])
                    pe.wait_ge(*is_free(stg, names[h], i))
                    for j in range(2):
                        for t in range(TOK):
                            last = pe.transpose(ps[:, b, j * S + t * P:j * S + (t + 1) * P],
                                                xq[:, t, (2 * h + j) * P:(2 * h + j + 1) * P], ident)
                    last.then_inc(full[b], 1)

            pe.wait_ge(s["const_in"], 48)
            norm(st["norm_in1"])
            S_ = st["in1"]
            for k in range(KT):
                pe.wait_ge(*is_drained(st["norm_in1"], f"t{k}"))
            pe.wait_ge(s["gate_w"], at(S_, "gate_w", 2))
            pe.wait_ge(*is_free(S_, "gate"))
            for t in range(TOK):
                for k in range(KT):
                    o = ps[:, 7, t * 8:(t + 1) * 8]
                    ah, al = (a[:, k, t * P:(t + 1) * P] for a in (aT_hi, aT_lo))
                    gh, gl = (g_[:, k * 8:(k + 1) * 8] for g_ in (gt_hi, gt_lo))
                    pe.matmul(o, ah, gh, start=(k == 0), stop=False)
                    pe.matmul(o, ah, gl, start=False, stop=False)
                    last = pe.matmul(o, al, gh, start=False, stop=(k == KT - 1))
            last.then_inc(full[7], 1)
            dense_rows(S_, 0, 0, ("dq0", "dq1"))
            pe.wait_ge(*is_drained(S_, "gate"))
            for gi in range(2):
                for t in range(TOK):
                    last = pe.transpose(ps[0:4, 7, gi * S + t * P:gi * S + (t + 1) * P],
                                        gtok[:, t, 4 * gi:4 * gi + 4], ident)
            last.then_inc(full[7], 1)
            dense_rows(S_, 0, 4, ("dk0", "dk1"))
            pe.wait_ge(s["gates"], at(S_, "gates", 5))
            pe.wait_ge(*is_free(S_, "gate_m"))
            for j, r in enumerate((5, 7)):
                for t in range(TOK):
                    last = pe.transpose(ps[:, 7, (j * 2 + t) * 4:(j * 2 + t) * 4 + 4],
                                        gm[0:4, r, t * P:(t + 1) * P], ident[0:4, 0:4])
            last.then_inc(full[7], 1)
            dense_cols(S_, 0, 8, ("mqk0", "mqk1", "mqk2", "mqk3"))
            dense_rows(S_, 0, 12, ("dv0", "dv1"))
            turn_heads(S_, ("qt0", "qt1"), 0, 2)
            dense_rows(S_, 0, 16, ("mv0", "mv1"))
            turn_heads(S_, ("kt0", "kt1"), 0, 4)
            dense_rows(S_, 0, 20, ("mo0", "mo1"))

            S_ = st["diff"]
            for nm in ("qt0", "qt1", "kt0", "kt1", "dv0", "dv1"):
                pe.wait_ge(*is_drained(st["in1"], nm))
            attention(S_, units_diff(), 0, pdf, "pd")

            S_ = st["mlstm"]
            pe.wait_ge(s["const_ready"], 2)
            pe.wait_ge(s["mqk"], at(st["in1"], "mqk", 2))
            for nm in ("mv0", "mv1"):
                pe.wait_ge(*is_drained(st["in1"], nm))
            sel = const("sel", "p (h c) -> p h c", dict(h=NH1))
            for h in range(NH1 + 1):
                if h < NH1:
                    pe.wait_ge(*is_free(S_, f"m{h}"))
                    pe.matmul(ps[:, 6, 0:S], sel[0:4, h, :], gm[0:4, 6, :], start=True, stop=True).then_inc(full[6], 1)
                    r0 = (h % 2) * HD
                    pe.wait_ge(*is_free(S_, f"s{h}"))
                    kk, qq = mqkT[r0:r0 + HD, 2 + h // 2, :], mqkT[r0:r0 + HD, h // 2, :]
                    pe.matmul(ps[:, 7, 0:S], kk[:, 0:P], qq, start=True, stop=True)
                    pe.matmul(ps[:, 7, S:S + P], kk[:, P:S], qq[:, P:S], start=True, stop=True).then_inc(full[7], 1)
                if h >= 1:
                    g = h - 1
                    b = bank(S_, f"o{g}")
                    pe.wait_ge(*is_free(S_, f"o{g}"))
                    pe.wait_ge(*is_drained(S_, f"s{g}"))
                    pe.matmul(ps[:, b, 0:129], pts[:, g % 2, 0:P], vm(0)[:, g, 0:129], start=True, stop=True)
                    pe.matmul(ps[:, b, 256:385], pts[:, g % 2, P:2 * P], vm(0)[:, g, 0:129], start=True, stop=False)
                    pe.matmul(ps[:, b, 256:385], pts[:, g % 2, 2 * P:3 * P], vm(1)[:, g, 0:129],
                              start=False, stop=True).then_inc(full[b], 1)

            pe.wait_ge(s["osq"], at(st["mlstm"], "osq", 1))
            turn(st["turn_mix"], o_sb, None)

            def project_out(name, turned):
                stg = st[name]
                for k in range(KT):
                    pe.wait_ge(*is_drained(st[turned], f"t{k}"))
                dense_rows(stg, 0, 0, ("r0", "r2"))
                dense_rows(stg, 0, 4, ("r1", "r3"))
            project_out("out1", "turn_mix")

            norm(st["norm_mlp"])
            for k in range(KT):
                pe.wait_ge(*is_drained(st["norm_mlp"], f"t{k}"))

            def await_hidden(stg, n, i):
                pe.wait_ge(s["ulo"], at(stg, "ulo", n, i))

            A4, B4 = [f"a{f}" for f in range(4)], [f"b{f}" for f in range(4)]
            S_ = st["mlp_head"]
            dense_cols(S_, 0, 0, A4)
            dense_cols(S_, 0, 4, B4)
            await_hidden(S_, 1, 0)
            down(S_, 0, 8, range(4), first=True)
            S_ = st["mlp_loop"]
            with trips(pe, S_) as i:
                dense_cols(S_, i, 0, A4)
                await_hidden(S_, 0, i)
                down(S_, i, 4, range(4))
            S_ = st["mlp_tail"]
            await_hidden(S_, 0, 0)
            down(S_, 0, 0, range(4), final=True)

            def project_heads(S_, i, groups):
                for g in range(groups):
                    n = g * 12
                    dense_rows(S_, i, n, (f"q{g}0", f"q{g}1"))
                    dense_rows(S_, i, n + 4, (f"k{g}0", f"k{g}1"))
                    turn_heads(S_, (f"qt{g}0", f"qt{g}1"), i, 4 * g + 2)
                    dense_rows(S_, i, n + 8, (f"v{g}0", f"v{g}1"))
                    turn_heads(S_, (f"kt{g}0", f"kt{g}1"), i, 4 * g + 4)
                g = groups - 1
                for nm in (f"v{g}0", f"v{g}1", f"kt{g}0", f"kt{g}1"):
                    pe.wait_ge(*is_drained(S_, nm, i))

            def ffn(tag):
                norm(st[f"norm_ffn_{tag}"])
                for k in range(KT):
                    pe.wait_ge(*is_drained(st[f"norm_ffn_{tag}"], f"t{k}"))
                S_ = st[f"ffn_{tag}_head"]
                dense_cols(S_, 0, 0, A4)
                dense_cols(S_, 0, 4, B4)
                await_hidden(S_, 1, 0)
                down(S_, 0, 8, range(2), first=True)
                S_ = st[f"ffn_{tag}_loop"]
                with trips(pe, S_) as i:
                    dense_cols(S_, i, 0, A4)
                    await_hidden(S_, 0, i)
                    down(S_, i, 4, range(2))
                    dense_cols(S_, i, 6, B4)
                    await_hidden(S_, 1, i)
                    down(S_, i, 10, range(2))
                S_ = st[f"ffn_{tag}_tail"]
                dense_cols(S_, 0, 0, A4)
                await_hidden(S_, 0, 0)
                down(S_, 0, 4, range(2))
                await_hidden(S_, 1, 0)
                down(S_, 0, 6, range(2), final=True)

            norm(st["norm_a"], "in")
            for k in range(KT):
                pe.wait_ge(*is_drained(st["norm_a"], f"t{k}"))
            S_ = st["half_a"]
            with trips(pe, S_) as i:
                project_heads(S_, i, NG)
                attention(S_, units_a(), i, prob, "prob")
            for b in (4, 5):
                pe.wait_ge(drained[b], at(st["turn_a"], ("bank", b), 0))
            turn(st["turn_a"], o_sb, "out")
            project_out("out_a", "turn_a")
            ffn("a")
            norm(st["norm_b"])
            for k in range(KT):
                pe.wait_ge(*is_drained(st["norm_b"], f"t{k}"))
            S_ = st["half_b"]
            with trips(pe, S_) as i:
                project_heads(S_, i, 1)
                attention(S_, units_b(), i, prob, "prob")
            for b in (4, 5):
                pe.wait_ge(drained[b], at(st["turn_b"], ("bank", b), 0))
            turn(st["turn_b"], o_sb, None)
            project_out("out_b", "turn_b")
            ffn("b")

        @block.scalar
        def _(act):
            chain = Chain(act, "act_step")
            LN_EXP = "natural_log_exp_and_others"

            def split(stg, n, i=0):
                if stg.q0 + n + SLOTS >= plan.nq:
                    return
                slot = plan.slot(stg, n)
                act.wait_ge(*was_read(stg, n, i))
                act.wait_ge(loaded[slot], (plan.turn(stg, n, i, SLOTS) + 1) * 16)
                act.activation(w_hi[:, slot, :], w_in[:, slot, :], ACT.Copy).then_inc(hi_done[slot], 1)

            def splits(stg, ns, i=0):
                for n in ns:
                    split(stg, n, i)

            def rsqrt(dst, src, tmp, key):
                chain.link(act.activation(tmp, src, ACT.Ln, bias=EPS))
                act.activation(dst, tmp, ACT.Exp, scale=-0.5).then_inc(s[key], 1)

            def turned(stg, gain):
                for k in range(KT):
                    act.wait_ge(*is_full(stg, f"t{k}"))
                    g = 1.0 if gain is None else gain[:, k:k + 1]
                    act.activation(aT_hi[:, k, :], ps[:, k, 0:S], ACT.Copy, scale=g).then_inc(s["hiT"], 1)

            def norm(stg, gain, x_ready):
                chain.enter(stg, 0)
                act.wait_ge(*x_ready[0])
                act.activation(hid[:].rearrange("p a b -> p (a b)"), x[:, 0, :], ACT.Square, scale=D ** -0.5,
                               accum_out=stat("ms", 2)[:, 0:1]).then_inc(s["ms"], 1)
                act.wait_ge(s["ms"], at(stg, "ms", 2))
                rsqrt(stat("rstd", 2), stat("ms", 2), stat("lnms", 2), "rstd")
                act.wait_ge(*x_ready[1])
                act.wait_ge(s["rstd"], at(stg, "rstd", 1))
                act.activation(xn[:, 1, :], x[:, 1, :], ACT.Copy, scale=stat("rstd", 2)[:, 1:2]).then_inc(s["xn"], 1)
                chain.leave()
                turned(stg, gain)

            def post_norm(name, out_stage, names):
                stg = st[name]
                chain.enter(stg, 0)
                for n, nm in enumerate(names):
                    act.wait_ge(*is_full(out_stage, nm))
                    act.activation(hid[:].rearrange("p a b -> p (a b)")[:, (n % 2) * 512:(n % 2 + 1) * 512],
                                   ps[:, n, :], ACT.Square, scale=D ** -0.5,
                                   accum_out=stat("msq", 4)[:, n:n + 1]).then_inc(s["msq"], 1)
                    act.wait_ge(s["msq"], at(stg, "msq", n + 1))
                act.wait_ge(s["pms"], at(stg, "pms", 1))
                rsqrt(stat("prstd", 2), stat("pms", 2), stat("lnms", 2), "rstd")
                chain.leave()

            def attention(stg, units, i, outs_raw=False):
                units = list(units)
                n = len(units)
                for u in range(n + 1 + (outs_raw and 1)):
                    if u < n:
                        un = units[u]
                        act.wait_ge(*is_drained(stg, f"s{u}", i))
                        if u >= 2 and not outs_raw:
                            act.wait_ge(*is_full(stg, f"p{u - 2}", i))
                        if u >= 2 and outs_raw:
                            act.wait_ge(s["pd"], at(stg, "pd", u - 1, i))
                        nseg = len(un["segments"])
                        for g, (c, W, _) in enumerate(un["segments"]):
                            last = act.activation(prob[:, u % 2, c:c + W], sm[:, u % 2, c:c + W], ACT.Exp, scale=-1.0,
                                                  bias=stat(f"nmax{u % 2}", 2)[:, g:g + 1],
                                                  accum_out=stat(f"den{u % 2}", 2)[:, g:g + 1])
                        last.then_inc(s["prob"], 1)
                    if 1 <= u <= n:
                        v = u - 1
                        act.wait_ge(*is_full(stg, f"p{v}", i))
                        if v >= 2:
                            act.wait_ge(*is_full(stg, f"o{v - 2}", i))
                        W = units[v]["tiles"] * P
                        b = bank(stg, f"p{v}")
                        act.activation(pts[:, v % 2, 0:W], ps[:, b, 0:W], ACT.Copy).then_inc(drained[b], 1)
                    if outs_raw and u >= 2:
                        v = u - 2
                        un = units[v]
                        b = bank(stg, f"o{v}")
                        act.wait_ge(*is_full(stg, f"o{v}", i))
                        o = o_sb[:, un["tok"], un["head"] * P:(un["head"] + 1) * P]
                        act.activation(o, ps[:, b, 0:P], ACT.Copy).then_inc(drained[b], 1)

            def evac_v(stg, name, i, dst, src=None):
                act.wait_ge(*is_full(stg, name, i))
                b = bank(stg, name)
                src = ps[:, b, :] if src is None else src
                act.activation(dst, src, ACT.Copy).then_inc(drained[b], 1)

            def evac_q(stg, name, i, j0, scale):
                act.wait_ge(*is_full(stg, name, i))
                b = bank(stg, name)
                v = ps[:, b, :].rearrange("p (j s) -> p j s", j=2)
                for h in range(2):
                    r = slice(h * HD, (h + 1) * HD)
                    sc = scale if isinstance(scale, float) else scale[r, :]
                    last = act.activation(qz[r, j0:j0 + 2, h, :], v[r, :, :], ACT.Copy, scale=sc)
                last.then_inc(drained[b], 1)

            def evac_k(stg, name, i, j0, scale):
                act.wait_ge(*is_full(stg, name, i))
                b = bank(stg, name)
                act.activation(kT[:, j0:j0 + 2, :], ps[:, b, :].rearrange("p (j s) -> p j s", j=2), ACT.Copy,
                               scale=scale).then_inc(drained[b], 1)

            act.preload_act_table_set(LN_EXP)
            S_ = st["norm_in1"]
            act.wait_ge(s["const_in"], 48)
            norm(S_, col("g_mix"), [(s["x_in"], 16)] * TOK)
            for slot in range(SLOTS):
                act.wait_ge(loaded[slot], 16)
                act.activation(w_hi[:, slot, :], w_in[:, slot, :], ACT.Copy).then_inc(hi_done[slot], 1)
                if slot == 0:
                    act.wait_ge(s["gate_in"], 16)
                    act.activation(gt_hi[:], gt_in[:], ACT.Copy).then_inc(s["gate_w"], 1)
            act.wait_ge(s["lam"], 1)
            act.activation(stat("elam", 2), stat("dots", 2), ACT.Exp).then_inc(s["lam"], 1)

            S_ = st["in1"]
            chain.enter(S_, 0)
            splits(S_, range(0, 4))
            act.wait_ge(s["gates"], at(S_, "gates", 2))
            act.activation(gm[0:4, 2, :], gm[0:4, 1, :], ACT.Exp).then_inc(s["lnf"], 1)
            act.wait_ge(s["lnf"], at(S_, "lnf", 1))
            act.activation(gm[0:4, 3, :], gm[0:4, 2, :], ACT.Ln, bias=1.0).then_inc(s["lnf"], 1)
            splits(S_, range(4, 8))
            act.wait_ge(*is_full(S_, "gate_m"))
            act.activation(atok[:, 0, :, :], ps[:, 7, 0:8].rearrange("p (t h) -> p t h", t=2), ACT.Copy)
            act.activation(atok[:, 1, :, :], ps[:, 7, 8:16].rearrange("p (t h) -> p t h", t=2), ACT.Exp,
                           scale=-1.0).then_inc(drained[7], 1)
            splits(S_, range(8, 12))
            for f in range(4):
                act.wait_ge(*is_full(S_, f"mqk{f}"))
                act.activation(hid[:, f, :], ps[:, 4 + f, 0:S], ACT.Identity, scale=col("cw1", f * 4 + 3),
                               bias=col("cb1", f)).then_inc(s["cv"], 1)
            splits(S_, range(12, 16))
            for t in range(TOK):
                evac_v(S_, f"dv{t}", 0, vv[:, t, 0:512])
            for f in range(4):
                act.wait_ge(*is_drained(S_, f"mqk{f}"))
            act.activation(u32[:], hid[:].rearrange("p a b -> p (a b)"), ACT.Exp, scale=-1.0).then_inc(s["ecv"], 1)
            act.wait_ge(s["const_ready"], 2)
            for j in range(2):
                evac_q(S_, f"qt{j}", 0, 2 * j, -(HD ** -0.5))
            splits(S_, range(16, 20))
            for t in range(TOK):
                evac_v(S_, f"mv{t}", 0, vm(t)[:, :, 0:VD], ps[:, 2 + t, :].rearrange("p (h c) -> p h c", h=NH1))
            for j in range(2):
                evac_k(S_, f"kt{j}", 0, 2 * j, 1.0)
            splits(S_, range(20, 24))
            for t in range(TOK):
                act.wait_ge(*is_full(S_, f"mo{t}"))
                act.activation(sqb[:, t, :], ps[:, 4 + t, :], ACT.Exp, scale=-1.0).then_inc(drained[4 + t], 1)
            chain.leave()

            S_ = st["diff"]
            chain.enter(S_, 0)
            attention(S_, units_diff(), 0, outs_raw=True)
            chain.leave()

            S_ = st["mlstm"]
            chain.enter(S_, 0)
            act.wait_ge(*is_drained(st["in1"], "gate_m"))
            for h in range(NH1):
                act.wait_ge(*is_drained(S_, f"m{h}"))
                for c, W, t in ((0, S, 0), (S, P, 1)):
                    last = act.activation(prob[:, h % 2, c:c + W], sm[:, h % 2, c:c + W], ACT.Exp, scale=-1.0,
                                          bias=atok[:, 0, t, h:h + 1])
                last.then_inc(s["wm"], 1)
            act.wait_ge(s["oms"], at(S_, "oms", 4))
            rsqrt(stat("orstd", 16), stat("oms", 16), stat("lno", 16), "orstd")
            chain.leave()
            turned(st["turn_mix"], col("g_heads"))
            splits(st["out1"], range(8))
            post_norm("post_mix", st["out1"], ("r0", "r1", "r2", "r3"))
            norm(st["norm_mlp"], col("g_mlp"), after_post("post_mix"))

            def relu_rows(stg, i, names, first):
                for f in range(4):
                    act.wait_ge(*is_full(stg, names[f], i))
                    act.activation(hid[:, f, :], ps[:, 4 + f, 0:S], ACT.Relu).then_inc(drained[4 + f], 1)

            def hidden_hi(stg, i, n, W=4 * S):
                act.wait_ge(s["u"], at(stg, "u", n, i))
                act.activation(u_hi[:, 0:W], u32[:, 0:W], ACT.Copy).then_inc(s["uhi"], 1)

            A4, B4 = [f"a{f}" for f in range(4)], [f"b{f}" for f in range(4)]
            S_ = st["mlp_head"]
            splits(S_, range(0, 4))
            relu_rows(S_, 0, A4, True)
            hidden_hi(S_, 0, 1)
            splits(S_, range(4, 8))
            relu_rows(S_, 0, B4, False)
            splits(S_, range(8, 12))
            hidden_hi(S_, 0, 2)
            S_ = st["mlp_loop"]
            with trips(act, S_) as i:
                splits(S_, range(0, 4), i)
                relu_rows(S_, i, A4, False)
                splits(S_, range(4, 8), i)
                hidden_hi(S_, i, 1)
            splits(st["mlp_tail"], range(4))
            post_norm("post_mlp", st["mlp_tail"], [f"acc{b}" for b in range(4)])

            def project_heads(S_, i, groups, layer):
                n = [0]

                def head_norms(names):
                    for t in range(TOK):
                        act.wait_ge(*is_full(S_, names[t], i))
                        if n[0] >= 2:
                            act.wait_ge(s["ms8"], at(S_, "ms8", n[0] - 1, i))
                        act.activation(sqb[:, t, :], ps[:, bank(S_, names[t]), :], ACT.Square,
                                       scale=HD ** -0.5).then_inc(s["sq"], 1)
                        n[0] += 1
                        act.wait_ge(s["ms8"], at(S_, "ms8", n[0], i))
                        rsqrt(stat(f"rs8{t}", 8), stat(f"ms8{t}", 8), stat(f"ln8{t}", 8), "rs8")
                for g in range(groups):
                    q0 = g * 12
                    splits(S_, range(q0, q0 + 4), i)
                    head_norms((f"q{g}0", f"q{g}1"))
                    splits(S_, range(q0 + 4, q0 + 8), i)
                    for j in range(2):
                        evac_q(S_, f"qt{g}{j}", i, g * 4 + 2 * j, gq[:, 2 * (layer * 3 + g):2 * (layer * 3 + g) + 1])
                    head_norms((f"k{g}0", f"k{g}1"))
                    splits(S_, range(q0 + 8, q0 + 12), i)
                    for t in range(TOK):
                        evac_v(S_, f"v{g}{t}", i, vv[:, t, g * 512:(g + 1) * 512])
                    for j in range(2):
                        evac_k(S_, f"kt{g}{j}", i, g * 4 + 2 * j, gq[:, 2 * (layer * 3 + g) + 1:2 * (layer * 3 + g) + 2])

            def ffn(tag, layer):
                W = 2 * S
                cw = col(f"cw2{tag}").rearrange("p (j c) -> p j c", c=16)

                def convolve(stg, i, names, j, n):
                    for f in range(4):
                        act.wait_ge(*is_full(stg, names[f], i))
                        sc = cw[:, bass.ds(j, 1), 4 * f + 2:4 * f + 3].rearrange("p a b -> p (a b)")
                        bi = cw[:, bass.ds(j, 1), 4 * f + 3:4 * f + 4].rearrange("p a b -> p (a b)")
                        act.activation(hid[:, f, :], ps[:, 4 + f, 0:S], ACT.Identity, scale=sc, bias=bi).then_inc(s["cv"], 1)
                    for f in range(2):
                        act.wait_ge(*is_drained(stg, names[f], i))
                    act.activation(u32[:, W:2 * W], hid[:, 0:2, :].rearrange("p a b -> p (a b)"), ACT.Silu)\
                        .then_inc(s["silu"], 1)
                act.preload_act_table(ACT.Silu)
                S_ = st[f"ffn_{tag}_head"]
                splits(S_, range(0, 4))
                convolve(S_, 0, A4, 0, 1)
                hidden_hi(S_, 0, 1, W)
                splits(S_, range(4, 8))
                convolve(S_, 0, B4, 1, 2)
                splits(S_, range(8, 10))
                hidden_hi(S_, 0, 2, W)
                S_ = st[f"ffn_{tag}_loop"]
                with trips(act, S_) as i:
                    splits(S_, range(0, 4), i)
                    convolve(S_, i, A4, i * 2 + 2, 1)
                    splits(S_, range(4, 6), i)
                    hidden_hi(S_, i, 1, W)
                    splits(S_, range(6, 10), i)
                    convolve(S_, i, B4, i * 2 + 3, 2)
                    splits(S_, range(10, 12), i)
                    hidden_hi(S_, i, 2, W)
                S_ = st[f"ffn_{tag}_tail"]
                splits(S_, range(0, 4))
                convolve(S_, 0, A4, U2 - 1, 1)
                splits(S_, range(4, 6))
                act.wait_ge(*was_read(S_, 5, 0))
                hidden_hi(S_, 0, 1, W)
                splits(S_, range(6, 8))
                act.preload_act_table_set(LN_EXP)

            norm(st["norm_a"], col("g_a"), after_post("post_mlp"))
            S_ = st["half_a"]
            with trips(act, S_) as i:
                chain.enter(S_, i)
                project_heads(S_, i, NG, 0)
                attention(S_, units_a(), i)
                chain.leave()
            turned(st["turn_a"], None)
            splits(st["out_a"], range(8))
            norm(st["norm_ffn_a"], col("g_fa"), after_sum("out_a", ("r1", "r3")))
            ffn("a", 0)
            norm(st["norm_b"], col("g_b"), after_sum("ffn_a_tail", ("acc1", "acc3")))
            S_ = st["half_b"]
            with trips(act, S_) as i:
                chain.enter(S_, i)
                project_heads(S_, i, 1, 1)
                attention(S_, units_b(), i)
                chain.leave()
            turned(st["turn_b"], None)
            splits(st["out_b"], range(8))
            norm(st["norm_ffn_b"], col("g_fb"), after_sum("out_b", ("r1", "r3")))
            ffn("b", 1)

        @block.gpsimd
        def _(pool):
            pool.memset(qz[:], 0.0).then_inc(s["const_ready"], 1)
            for t in range(TOK):
                last = pool.memset(vm(t)[:, :, VD:VD + 1], 1.0)
            last.then_inc(s["const_ready"], 1)

        @block.vector
        def _(dve):
            chain = Chain(dve, "dve_step")
            link = chain.link

            def split(stg, n, i=0):
                if stg.q0 + n + SLOTS >= plan.nq:
                    return
                slot = plan.slot(stg, n)
                dve.wait_ge(hi_done[slot], plan.turn(stg, n, i, SLOTS) + 1)
                dve.tensor_tensor(w_lo[:, slot, :], w_in[:, slot, :], w_hi[:, slot, :].bitcast(F32),
                                  ALU.subtract).then_inc(lo_done[slot], 1)

            def splits(stg, ns, i=0):
                for n in ns:
                    split(stg, n, i)

            def turned(stg, gain):
                for k in range(KT):
                    dve.wait_ge(s["hiT"], at(stg, "hiT", k + 1))
                    g = 1.0 if gain is None else gain[:, k:k + 1]
                    dve.scalar_tensor_tensor(out=aT_lo[:, k, :], in0=ps[:, k, 0:S], scalar=g,
                                             in1=aT_hi[:, k, :].bitcast(F32), op0=ALU.mult,
                                             op1=ALU.subtract).then_inc(drained[k], 1)

            def norm(stg, gain, x_ready):
                dve.wait_ge(*x_ready[1])
                dve.tensor_tensor_reduce(out=u32[:], in0=x[:, 1, :], in1=x[:, 1, :], scale=1.0 / D, scalar=0.0,
                                         op0=ALU.mult, op1=ALU.add,
                                         accum_out=stat("ms", 2)[:, 1:2]).then_inc(s["ms"], 1)
                dve.wait_ge(*x_ready[0])
                dve.wait_ge(s["rstd"], at(stg, "rstd", 1))
                dve.tensor_scalar(xn[:, 0, :], x[:, 0, :], stat("rstd", 2)[:, 0:1], None, ALU.mult).then_inc(s["xn"], 1)
                turned(stg, gain)

            def post_norm(name, gain):
                stg = st[name]
                dve.wait_ge(s["msq"], at(stg, "msq", 4))
                m = stat("msq", 4).rearrange("p (t h) -> p t h", h=2)
                dve.tensor_tensor(stat("pms", 2).rearrange("p (t h) -> p t h", h=1), m[:, :, 0:1], m[:, :, 1:2],
                                  ALU.add).then_inc(s["pms"], 1)
                dve.wait_ge(s["rstd"], at(stg, "rstd", 1))
                for b in range(4):
                    t, h = divmod(b, 2)
                    sl = slice(h * 512, (h + 1) * 512)
                    dve.scalar_tensor_tensor(out=xn[:, t, sl], in0=ps[:, b, :], scalar=stat("prstd", 2)[:, t:t + 1],
                                             in1=row(gain)[:, sl], op0=ALU.mult, op1=ALU.mult).then_inc(drained[b], 1)
                for t in range(TOK):
                    for h in range(2):
                        b = 2 * t + h
                        sl = slice(h * 512, (h + 1) * 512)
                        if h == 0:
                            dve.wait_ge(drained[b + 1], at(stg, ("bank", b + 1), 0))
                            last = dve.tensor_tensor(x[:, t, sl], x[:, t, sl], xn[:, t, sl], ALU.add)
                        else:
                            dve.tensor_tensor(x[:, t, sl], x[:, t, sl], xn[:, t, sl], ALU.add).then_inc(s["x_new"], 1)

            def add_rows(stg, names):
                for b in range(4):
                    t, h = divmod(b, 2)
                    dve.wait_ge(*is_full(stg, names[b]))
                    sl = slice(h * 512, (h + 1) * 512)
                    dve.tensor_tensor(x[:, t, sl], ps[:, b, :], x[:, t, sl], ALU.add).then_inc(drained[b], 1)

            def attention(stg, units, i, lag_out=2):
                units = list(units)
                n = len(units)
                diff = stg is st["diff"]
                for u in range(n + 2):
                    if u < n:
                        un = units[u]
                        dve.wait_ge(*is_full(stg, f"s{u}", i))
                        if u >= 2:
                            dve.wait_ge(s["prob"], at(stg, "prob", u - 1, i))
                        b = bank(stg, f"s{u}")
                        dve.sem_inc(s["unit"], 1)
                        for g, (c, W, mask) in enumerate(un["segments"]):
                            last = dve.tensor_tensor_reduce(
                                out=sm[:, u % 2, c:c + W], in0=ps[:, b, c:c + W], in1=mask, scale=1.0, scalar=BIG,
                                op0=ALU.add, op1=ALU.min, accum_out=stat(f"nmax{u % 2}", 2)[:, g:g + 1])
                        last.then_inc(drained[b], 1)
                    if 1 <= u <= n:
                        v = u - 1
                        nseg = len(units[v]["segments"])
                        dve.wait_ge(s["prob"], at(stg, "prob", v + 1, i))
                        if v >= 2 and not diff:
                            dve.wait_ge(*is_drained(stg, f"o{v - 2}", i))
                        link(dve.reciprocal(stat(f"rden{v % 2}", 2)[:, 0:nseg], stat(f"den{v % 2}", 2)[:, 0:nseg]))
                        if diff:
                            W = units[v]["segments"][0][1]
                            r = stat(f"rden{v % 2}", 2)
                            link(dve.tensor_scalar(stat("rlam"), r[:, 1:2], stat("neglam"), None, ALU.mult))
                            if v >= 2:
                                dve.wait_ge(*is_full(stg, f"p{v - 2}", i))
                            link(dve.tensor_scalar(rtmp[:, 0:W], prob[:, v % 2, W:2 * W],
                                                   stat("rlam"), None, ALU.mult))
                            dve.scalar_tensor_tensor(out=pdf[:, v % 2, 0:W], in0=prob[:, v % 2, 0:W], scalar=r[:, 0:1],
                                                     in1=rtmp[:, 0:W], op0=ALU.mult, op1=ALU.add)\
                                .then_inc(s["pd"], 1)
                    if u >= 2 and not diff:
                        v = u - 2
                        un = units[v]
                        dve.wait_ge(*is_full(stg, f"o{v}", i))
                        b = bank(stg, f"o{v}")
                        for g, c, oc in un["outs"]:
                            if stg.trips > 1:
                                dst = o_sb[:, un["tok"], bass.ds(i * 512 + oc, HD)]
                            last = dve.tensor_scalar(dst, ps[:, b, c:c + HD], stat(f"rden{v % 2}", 2)[:, g:g + 1],
                                                     None, ALU.mult)
                        last.then_inc(drained[b], 1)
                    if u >= 3 and diff:
                        sum_square(stg, units, u - 3)
                if diff:
                    sum_square(stg, units, n - 1)

            def sum_square(stg, units, v):
                un = units[v]
                dve.wait_ge(*is_drained(stg, f"o{v}"))
                o = o_sb[:, un["tok"], un["head"] * P:(un["head"] + 1) * P]
                j = un["tok"] * 8 + un["head"]
                if v >= 2:
                    dve.wait_ge(s["oms"], at(stg, "oms", v - 1))
                dve.tensor_tensor_reduce(out=junk[:, v % 2, :], in0=o, in1=o, scale=1.0 / VD, scalar=0.0, op0=ALU.mult,
                                         op1=ALU.add, accum_out=stat("oms", 16)[:, j:j + 1]).then_inc(s["oms"], 1)

            rtmp = xq[:, 0, 0:S]
            junk = rt

            S_ = st["load"]
            chain.enter(S_, 0)
            dve.wait_ge(s["const_in"], 48)
            norm(st["norm_in1"], col("g_mix"), [(s["x_in"], 16)] * TOK)
            dve.wait_ge(s["gate_w"], 1)
            dve.tensor_tensor(gt_lo[:], gt_in[:], gt_hi[:].bitcast(F32), ALU.subtract).then_inc(s["gate_w"], 1)
            for slot in range(SLOTS):
                dve.wait_ge(hi_done[slot], 1)
                dve.tensor_tensor(w_lo[:, slot, :], w_in[:, slot, :], w_hi[:, slot, :].bitcast(F32),
                                  ALU.subtract).then_inc(lo_done[slot], 1)
            lam = row("lambda").rearrange("p (v d) -> p v d", v=4)
            for j in range(2):
                last = dve.tensor_tensor_reduce(out=rt[:, j, 0:HD], in0=lam[:, 2 * j, :], in1=lam[:, 2 * j + 1, :],
                                                scale=1.0, scalar=0.0, op0=ALU.mult, op1=ALU.add,
                                                accum_out=stat("dots", 2)[:, j:j + 1])
            last.then_inc(s["lam"], 1)
            g = col("gains")
            link(dve.tensor_scalar(gq[:], g, col("unrotated", 0), col("rotated", 0), ALU.mult, ALU.add))
            gq2 = gq[:].rearrange("p (g c) -> p g c", c=2)
            link(dve.tensor_scalar(gq2[:, :, 0:1], gq2[:, :, 0:1], -(HD ** -0.5), None, ALU.mult))
            link(dve.tensor_scalar(col("g_heads", 0, 4), col("g_heads", 0, 4), 1.0 - LAMBDA_INIT, None, ALU.mult))
            grow = row("gain_rows").rearrange("p (g h d) -> p g h d", h=2, d=ROT // 2)
            for j in range(8):
                rp = const("rope_a" if j < 6 else "rope_b", "p (c t d) -> p c t d", dict(c=2, t=TOK))
                for t in range(TOK):
                    cos, sin = rp[:, 0, t, :], rp[:, 1, t, :]
                    T = tabs[:, j, t, :, :]
                    dve.tensor_tensor(T[:, 0, 0:8], cos, grow[:, j, 0, :], ALU.mult)
                    dve.tensor_tensor(T[:, 0, 8:16], cos, grow[:, j, 1, :], ALU.mult)
                    dve.tensor_tensor(T[:, 1, 0:8], sin, grow[:, j, 0, :], ALU.mult)
                    dve.scalar_tensor_tensor(out=T[:, 1, 8:16], in0=sin, scalar=-1.0, in1=grow[:, j, 1, :],
                                             op0=ALU.mult, op1=ALU.mult)
            dve.wait_ge(s["lam"], 2)
            e = stat("elam", 2)
            link(dve.tensor_tensor(stat("dlam"), e[:, 1:2], e[:, 0:1], ALU.subtract))
            link(dve.tensor_scalar(stat("neglam"), stat("dlam"), LAMBDA_INIT, None, ALU.subtract))
            chain.leave()

            S_ = st["in1"]
            chain.enter(S_, 0)

            def rotate_full(names, t):
                dve.wait_ge(*is_full(S_, names[t]))
                b = bank(S_, names[t])
                v = rope_view(ps[:, b, :], 8, 2, 32)
                a = rope_view(xq[:, t, :], 8, 2, 32)
                w = rope_view(sqb[:, t, :], 8, 2, 32)
                rp = const("rope1", "p (c t d) -> p c t d", dict(c=2, t=TOK))
                cos, sin = (rp[:, c, t, :].unsqueeze(1) for c in range(2))
                dve.tensor_tensor(xq[:, t, :].rearrange("p (h d) -> p h d", d=32),
                                  ps[:, b, :].rearrange("p (h d) -> p h d", d=32),
                                  cos.broadcast_to([P, 16, 32]), ALU.mult)
                dve.tensor_tensor(w[:, :, 0, :], v[:, :, 1, :], sin.broadcast_to([P, 8, 32]), ALU.mult)
                dve.tensor_tensor(w[:, :, 1, :], v[:, :, 0, :], sin.broadcast_to([P, 8, 32]), ALU.mult)\
                    .then_inc(drained[b], 1)
                dve.wait_ge(drained[b], filled(S_, names[t]))
                dve.tensor_tensor(a[:, :, 0, :], a[:, :, 0, :], w[:, :, 0, :], ALU.subtract)
                dve.tensor_tensor(a[:, :, 1, :], a[:, :, 1, :], w[:, :, 1, :], ALU.add).then_inc(s["rot"], 1)

            splits(S_, range(0, 4))
            dve.wait_ge(*is_full(S_, "gate"))
            dve.tensor_copy(gtok[:], ps[:, 7, 0:16].rearrange("p (t g) -> p t g", t=2)).then_inc(drained[7], 1)
            for t in range(TOK):
                rotate_full(("dq0", "dq1"), t)
            dve.wait_ge(*is_full(S_, "gate_t"))
            link(dve.tensor_scalar(gi[:], ps[0:4, 7, 0:S], col("b_i", 0)[0:4, :], None, ALU.add))
            dve.tensor_scalar(gm[0:4, 7, :], ps[0:4, 7, S:2 * S], col("b_f", 0)[0:4, :], None, ALU.add)\
                .then_inc(drained[7], 1)
            dve.wait_ge(*is_drained(S_, "gate_t"))
            dve.tensor_scalar(gm[0:4, 0, :], gm[0:4, 7, :], 0.0, None, ALU.min).then_inc(s["gates"], 1)
            link(dve.tensor_scalar(gm[0:4, 6, :], gm[0:4, 7, :], 0.0, None, ALU.max))
            dve.tensor_tensor(gm[0:4, 1, :], gm[0:4, 0, :], gm[0:4, 6, :], ALU.subtract).then_inc(s["gates"], 1)
            splits(S_, range(4, 8))
            dve.wait_ge(s["lnf"], at(S_, "lnf", 2))
            link(dve.tensor_tensor(gm[0:4, 3, :], gm[0:4, 0, :], gm[0:4, 3, :], ALU.subtract))
            dve.tensor_tensor_scan(gm[0:4, 4, :], gm[0:4, 3, :], gm[0:4, 3, :], 0.0, ALU.add, ALU.bypass)\
                .then_inc(s["gates"], 1)
            dve.wait_ge(s["gates"], at(S_, "gates", 3))
            link(dve.tensor_tensor(gm[0:4, 5, :], gi[:], gm[0:4, 4, :], ALU.subtract))
            dve.tensor_tensor_scan(gm[0:4, 6, :], gm[0:4, 5, :], gm[0:4, 5, :], 0.0, ALU.max, ALU.bypass)\
                .then_inc(s["gates"], 1)
            dve.wait_ge(s["gates"], at(S_, "gates", 4))
            dve.tensor_tensor(gm[0:4, 7, :], gm[0:4, 4, :], gm[0:4, 6, :], ALU.add).then_inc(s["gates"], 1)
            splits(S_, range(8, 12))
            for f in range(4):
                dve.wait_ge(s["cv"], at(S_, "cv", f + 1))
                for back in (1, 2, 3):
                    ins_ = dve.scalar_tensor_tensor(out=hid[:, f, back:S], in0=ps[:, 4 + f, 0:S - back],
                                                    scalar=col("cw1", f * 4 + 3 - back), in1=hid[:, f, back:S],
                                                    op0=ALU.mult, op1=ALU.add)
                    if back < 3:
                        link(ins_)
                    else:
                        ins_.then_inc(drained[4 + f], 1)
            dve.wait_ge(drained[7], filled(S_, "mqk3"))
            splits(S_, range(12, 16))
            dve.wait_ge(*is_full(S_, "qt0"))
            dve.wait_ge(*is_full(S_, "qt1"))
            for t in range(TOK):
                rotate_full(("dk0", "dk1"), t)
            dve.wait_ge(s["ecv"], at(S_, "ecv", 1))
            link(dve.tensor_scalar(u32[:], u32[:], 1.0, None, ALU.add))
            link(dve.reciprocal(u32[:], u32[:]))
            for j, sc in enumerate((HD ** -0.5, 1.0)):
                dve.scalar_tensor_tensor(out=mqkT[:, 2 * j:2 * j + 2, :].rearrange("p a b -> p (a b)"),
                                         in0=hid[:, 2 * j:2 * j + 2, :].rearrange("p a b -> p (a b)"), scalar=sc,
                                         in1=u32[:, j * 512:(j + 1) * 512], op0=ALU.mult, op1=ALU.mult)\
                    .then_inc(s["mqk"], 1)
            splits(S_, range(16, 24))
            for t in range(TOK):
                dve.wait_ge(*is_drained(S_, f"mo{t}"))
                link(dve.tensor_scalar(sqb[:, t, :], sqb[:, t, :], 1.0, None, ALU.add))
                ins_ = dve.reciprocal(sqb[:, t, :], sqb[:, t, :])
            ins_.then_inc(s["sig"], 1)
            chain.leave()

            S_ = st["diff"]
            chain.enter(S_, 0)
            attention(S_, units_diff(), 0)
            chain.leave()

            S_ = st["mlstm"]
            chain.enter(S_, 0)
            ct = const("causal_t")

            def mlstm_head(g):
                b = bank(S_, f"o{g}")
                dve.wait_ge(*is_full(S_, f"o{g}"))
                v = ps[:, b, :].rearrange("p (t c) -> p t c", t=2)
                den = v[:, :, VD:VD + 1]
                nd, dm = (stat(n, 2).rearrange("p (t c) -> p t c", t=2) for n in ("nd", "dm"))
                em = atok[:, 1, :, g:g + 1]
                link(dve.tensor_scalar(nd, den, -1.0, None, ALU.mult))
                link(dve.tensor_tensor(nd, nd, em, ALU.max))
                link(dve.tensor_tensor(dm, den, nd, ALU.max))
                link(dve.reciprocal(dm, dm))
                for t in range(TOK):
                    last = dve.tensor_scalar(o_sb[:, t, 512 + g * P:512 + (g + 1) * P], v[:, t, 0:VD],
                                             stat("dm", 2)[:, t:t + 1], None, ALU.mult)
                last.then_inc(drained[b], 1)
                dve.wait_ge(*is_drained(S_, f"o{g}"))
                for t in range(TOK):
                    o = o_sb[:, t, 512 + g * P:512 + (g + 1) * P]
                    j = t * 8 + 4 + g
                    last = dve.tensor_tensor_reduce(out=junk[:, t, :], in0=o, in1=o, scale=1.0 / VD, scalar=0.0,
                                                    op0=ALU.mult, op1=ALU.add, accum_out=stat("oms", 16)[:, j:j + 1])
                last.then_inc(s["oms"], 1)
            for h in range(NH1):
                dve.wait_ge(*is_full(S_, f"m{h}"))
                dve.tensor_tensor(sm[:, h % 2, 0:S], ps[:, 6, 0:S], ct, ALU.add)
                dve.tensor_tensor(sm[:, h % 2, S:S + P], ps[:, 6, P:S], ct[:, 0:P], ALU.add).then_inc(drained[6], 1)
                if h >= 1:
                    mlstm_head(h - 1)
                dve.wait_ge(*is_full(S_, f"s{h}"))
                dve.wait_ge(s["wm"], at(S_, "wm", h + 1))
                dve.tensor_tensor(pts[:, h % 2, 0:S + P], ps[:, 7, 0:S + P], prob[:, h % 2, 0:S + P], ALU.mult)\
                    .then_inc(drained[7], 1)
            mlstm_head(NH1 - 1)
            dve.wait_ge(s["orstd"], at(S_, "orstd", 1))
            r = stat("orstd", 16).rearrange("p (t h) -> p t h", t=TOK)
            for t in range(TOK):
                ov = o_sb[:, t, :].rearrange("p (h c) -> p h c", c=P)
                last = dve.tensor_tensor(ov, ov, r[:, t, :].unsqueeze(2).broadcast_to([P, 8, P]), ALU.mult)
            link(last)
            for t in range(TOK):
                last = dve.tensor_tensor(o_sb[:, t, 512:1024], o_sb[:, t, 512:1024], sqb[:, t, :], ALU.mult)
            last.then_inc(s["osq"], 1)
            chain.leave()
            turned(st["turn_mix"], col("g_heads"))
            splits(st["out1"], range(8))
            post_norm("post_mix", "mix_post")
            norm(st["norm_mlp"], col("g_mlp"), after_post("post_mix"))

            def square(stg, i, n, before):
                for f in range(4):
                    dve.wait_ge(*is_drained(stg, before[f], i))
                if stg is not st["mlp_head"] or n > 1:
                    dve.wait_ge(s["uhi"], at(stg, "uhi", n - 1, i))
                    dve.wait_ge(s["ulo"], at(stg, "ulo", n - 1, i))
                dve.tensor_tensor(u32[:], hid[:].rearrange("p a b -> p (a b)"), hid[:].rearrange("p a b -> p (a b)"),
                                  ALU.mult).then_inc(s["u"], 1)

            def hidden_lo(stg, i, n, W=4 * S):
                dve.wait_ge(s["uhi"], at(stg, "uhi", n, i))
                dve.tensor_tensor(u_lo[:, 0:W], u32[:, 0:W], u_hi[:, 0:W].bitcast(F32), ALU.subtract)\
                    .then_inc(s["ulo"], 1)

            A4, B4 = [f"a{f}" for f in range(4)], [f"b{f}" for f in range(4)]
            S_ = st["mlp_head"]
            splits(S_, range(0, 4))
            square(S_, 0, 1, A4)
            hidden_lo(S_, 0, 1)
            splits(S_, range(4, 8))
            square(S_, 0, 2, B4)
            splits(S_, range(8, 12))
            hidden_lo(S_, 0, 2)
            S_ = st["mlp_loop"]
            with trips(dve, S_) as i:
                splits(S_, range(0, 4), i)
                square(S_, i, 1, A4)
                splits(S_, range(4, 8), i)
                hidden_lo(S_, i, 1)
            splits(st["mlp_tail"], range(4))
            post_norm("post_mlp", "mlp_post")

            def project_heads(S_, i, groups, layer):
                n = [0]

                def head_norms(names, which, j):
                    for t in range(TOK):
                        dve.wait_ge(s["sq"], at(S_, "sq", n[0] + 1, i))
                        dve.tensor_reduce(stat(f"ms8{t}", 8), sqb[:, t, :].rearrange("p (h d) -> p h d", d=HD),
                                          AX.X, ALU.add).then_inc(s["ms8"], 1)
                        n[0] += 1
                        dve.wait_ge(s["rs8"], at(S_, "rs8", n[0], i))
                        b = bank(S_, names[t])
                        xv = xq[:, t, :].rearrange("p (h d) -> p h d", d=HD)
                        dve.tensor_tensor(xv, ps[:, b, :].rearrange("p (h d) -> p h d", d=HD),
                                          stat(f"rs8{t}", 8).unsqueeze(2).broadcast_to([P, 8, HD]),
                                          ALU.mult).then_inc(drained[b], 1)
                        dve.wait_ge(*is_drained(S_, names[t], i))
                        T = tabs[:, j, t, :, :]
                        r1, r2 = (rt[:, c, :].rearrange("p (h d) -> p h d", d=ROT) for c in range(2))
                        dve.tensor_tensor(r1, xv[:, :, 0:ROT], T[:, 0, :].unsqueeze(1).broadcast_to([P, 8, ROT]), ALU.mult)
                        link(dve.tensor_tensor(r2, xv[:, :, 0:ROT], T[:, 1, :].unsqueeze(1).broadcast_to([P, 8, ROT]), ALU.mult))
                        dve.tensor_tensor(xv[:, :, 0:8], r1[:, :, 0:8], r2[:, :, 8:16], ALU.add)
                        dve.tensor_tensor(xv[:, :, 8:16], r1[:, :, 8:16], r2[:, :, 0:8], ALU.add)\
                            .then_inc(s["rot"], 1)
                for g in range(groups):
                    q0 = g * 12
                    splits(S_, range(q0, q0 + 4), i)
                    if g > 0:
                        for j in range(2):
                            dve.wait_ge(*is_full(S_, f"kt{g - 1}{j}", i))
                    head_norms((f"q{g}0", f"q{g}1"), 0, (layer * 3 + g) * 2)
                    splits(S_, range(q0 + 4, q0 + 8), i)
                    for j in range(2):
                        dve.wait_ge(*is_full(S_, f"qt{g}{j}", i))
                    head_norms((f"k{g}0", f"k{g}1"), 1, (layer * 3 + g) * 2 + 1)
                    splits(S_, range(q0 + 8, q0 + 12), i)

            def ffn(tag):
                W = 2 * S
                cw = col(f"cw2{tag}").rearrange("p (j c) -> p j c", c=16)

                def convolve(stg, i, names, j, n):
                    for f in range(4):
                        dve.wait_ge(s["cv"], at(stg, "cv", 4 * (n - 1) + f + 1, i))
                        for back in (1, 2):
                            sc = cw[:, bass.ds(j, 1), 4 * f + 2 - back:4 * f + 3 - back].rearrange("p a b -> p (a b)")
                            ins_ = dve.scalar_tensor_tensor(out=hid[:, f, back:S], in0=ps[:, 4 + f, 0:S - back],
                                                            scalar=sc, in1=hid[:, f, back:S], op0=ALU.mult, op1=ALU.add)
                            if back < 2:
                                link(ins_)
                            else:
                                ins_.then_inc(drained[4 + f], 1)
                    dve.wait_ge(*is_drained(stg, names[3], i))
                    dve.wait_ge(s["silu"], at(stg, "silu", n, i))
                    dve.wait_ge(s["uhi"], at(stg, "uhi", n - 1, i))
                    dve.wait_ge(s["ulo"], at(stg, "ulo", n - 1, i))
                    dve.tensor_tensor(u32[:, 0:W], u32[:, W:2 * W], hid[:, 2:4, :].rearrange("p a b -> p (a b)"),
                                      ALU.mult).then_inc(s["u"], 1)
                S_ = st[f"ffn_{tag}_head"]
                chain.enter(S_, 0)
                splits(S_, range(0, 4))
                convolve(S_, 0, A4, 0, 1)
                hidden_lo(S_, 0, 1, W)
                splits(S_, range(4, 8))
                convolve(S_, 0, B4, 1, 2)
                splits(S_, range(8, 10))
                hidden_lo(S_, 0, 2, W)
                chain.leave()
                S_ = st[f"ffn_{tag}_loop"]
                with trips(dve, S_) as i:
                    chain.enter(S_, i)
                    splits(S_, range(0, 4), i)
                    convolve(S_, i, A4, i * 2 + 2, 1)
                    splits(S_, range(4, 6), i)
                    hidden_lo(S_, i, 1, W)
                    splits(S_, range(6, 10), i)
                    convolve(S_, i, B4, i * 2 + 3, 2)
                    splits(S_, range(10, 12), i)
                    hidden_lo(S_, i, 2, W)
                    chain.leave()
                S_ = st[f"ffn_{tag}_tail"]
                chain.enter(S_, 0)
                splits(S_, range(0, 4))
                convolve(S_, 0, A4, U2 - 1, 1)
                splits(S_, range(4, 6))
                hidden_lo(S_, 0, 1, W)
                splits(S_, range(6, 8))
                chain.leave()
                add_rows(S_, [f"acc{b}" for b in range(4)])

            norm(st["norm_a"], col("g_a"), after_post("post_mlp"))
            S_ = st["half_a"]
            with trips(dve, S_) as i:
                chain.enter(S_, i)
                project_heads(S_, i, NG, 0)
                attention(S_, units_a(), i)
                chain.leave()
            turned(st["turn_a"], None)
            splits(st["out_a"], range(8))
            add_rows(st["out_a"], ("r0", "r1", "r2", "r3"))
            norm(st["norm_ffn_a"], col("g_fa"), after_sum("out_a", ("r1", "r3")))
            ffn("a")
            norm(st["norm_b"], col("g_b"), after_sum("ffn_a_tail", ("acc1", "acc3")))
            S_ = st["half_b"]
            with trips(dve, S_) as i:
                chain.enter(S_, i)
                project_heads(S_, i, 1, 1)
                attention(S_, units_b(), i)
                chain.leave()
            turned(st["turn_b"], None)
            splits(st["out_b"], range(8))
            add_rows(st["out_b"], ("r0", "r1", "r2", "r3"))
            norm(st["norm_ffn_b"], col("g_fb"), after_sum("out_b", ("r1", "r3")))
            ffn("b")


def lay_out(inputs):
    def feat(a):
        return np.asarray(a, np.float32).reshape(-1, P).T

    def twice(a):
        return np.concatenate([a, a], 0)
    unit = {n: np.asarray(v) for n, v in inputs.items()}
    gains = [unit["a_q_norm_2"][0], unit["a_k_norm_2"][0]]
    g = [gains[c][j] for j in range(NG) for c in range(2)] + [unit["b_q_norm_2"][0], unit["b_k_norm_2"][0]]
    rot = (np.arange(P) % HD < ROT).astype(np.float32)[:, None]

    def pad4(a):
        return np.concatenate([a.reshape(4, 1), np.zeros((P - 4, 1), np.float32)], 0)
    cols = {
        "g_mix": feat(unit["norm_mix_pre"]), "g_mlp": feat(unit["norm_mlp_pre"]),
        "g_a": feat(unit["attn_norm_2"][0]), "g_b": feat(unit["attn_norm_2"][1]),
        "g_fa": feat(unit["ffn_norm_2"][0]), "g_fb": feat(unit["ffn_norm_2"][1]),
        "g_heads": np.concatenate([feat(unit["diff_norm"])] * NH1 + [feat(unit["mlstm_norm"])], 1),
        "cw1": unit["conv_w"][0].reshape(CONV1, 4, P).transpose(2, 1, 0),
        "cb1": unit["conv_b"][0].reshape(4, P).T,
        "b_i": pad4(unit["b_igate"]), "b_f": pad4(unit["b_fgate"]),
        "gains": np.stack([twice(v) for v in g], 1),
        "rotated": rot, "unrotated": 1 - rot,
    }
    for layer, tag in enumerate("ab"):
        w = np.concatenate([unit["ffn_conv_w_2"][layer], unit["ffn_conv_b_2"][layer][None]], 0)
        w = w.reshape(4, 2, U2, 2, P)
        cols[f"cw2{tag}"] = w.transpose(4, 2, 1, 3, 0)
    rows = {
        "mix_post": unit["norm_mix_post"][0], "mlp_post": unit["norm_mlp_post"][0],
        "lambda": np.concatenate([unit[f"lambda_{n}"][0] for n in ("q1", "k1", "q2", "k2")]),
        "gain_rows": np.concatenate([v[:ROT] for v in g]),
    }
    packed, at_col = pack(cols)
    at_row, n = {}, 0
    for name, a in rows.items():
        at_row[name] = (n, a.size)
        n += a.size
    return packed, at_col, np.ascontiguousarray(np.concatenate(list(rows.values()))[None], dtype=np.float32), at_row


def kernel(**inputs):
    import concourse.bacc as _bacc
    from concourse.bass_utils import run_bass_kernel_spmd as _run

    nc = _bacc.Bacc("TRN2", target_bir_lowering=False, num_devices=1)
    consts, at_const = pack(constant_tables())
    cols, at_col, rows, at_row = lay_out(inputs)
    arrays = {"consts": consts, "cols": cols, "rows": rows}
    for name in ("x", "w_in", "w_out", "w_up", "w_down"):
        arrays[name] = np.ascontiguousarray(inputs[name])
    for name in ("a_w_qkv", "a_w_o", "b_w_qkv", "b_w_o", "ffn_w_up", "ffn_w_down"):
        arrays[name] = np.ascontiguousarray(inputs[name + "_2"])
    up = arrays["ffn_w_up"]
    arrays["ffn_w_up"] = np.ascontiguousarray(
        up.reshape(2, D, 2, U2, 256).transpose(0, 1, 3, 2, 4).reshape(2, D, 2 * FF2))
    args = {n: nc.dram_tensor(f"in_{n}", a.shape, mybir.dt.from_np(a.dtype), kind="ExternalInput").ap()
            for n, a in arrays.items()}
    out = nc.dram_tensor("out_0", (1, S, D), F32, kind="ExternalOutput").ap()
    blocks_kernel(nc, args, out, at_const, at_col, at_row)
    r = _run(nc, [{f"in_{n}": a for n, a in arrays.items()}], core_ids=[0])
    return r.results[0]["out_0"]
```

```python
from contextlib import ExitStack, contextmanager

import numpy as np

import concourse.bass as bass
import concourse.mybir as mybir

F32 = mybir.dt.float32
F32R = mybir.dt.float32r
ALU = mybir.AluOpType
ACT = mybir.ActivationFunctionType
AX = mybir.AxisListType

P = 128
S = 256
TOK = S // P
D = 1024
KT = D // P
HD = 64
SLOTS = 4
QW = 1024
EPS = 1e-6
BIG = 1e30
LAMBDA_INIT = 0.8 - 0.6 * 1.0

NH1 = 4
VD = 128
CONV1 = 4
FF1 = 4096
U1 = FF1 // 512
NH = 16
NG = 3
ROT = 16
FF2 = 2816
U2 = FF2 // 256
DILS = ((128, 1), (512, 4), (2048, 16))


def residue_order():
    t = np.arange(S)
    return (t % 4) * 64 + (t // 4 % 4) * 16 + t // 16


def constant_tables():
    c = {}
    c["ident"] = np.eye(P)
    pos = residue_order()
    token_at = np.argsort(pos)
    src = np.arange(P)
    perm_in = np.zeros((P, P))
    perm_in[src, (src % 4) * 32 + (src // 4 % 4) * 8 + src // 16] = 1
    perm_out = np.zeros((P, P))
    perm_out[src, (src % 16) * 8 + (src // 16 % 4) * 2 + src // 64] = 1
    c["perm_in"], c["perm_out"] = perm_in, perm_out
    mask_a = np.zeros((P, TOK, 512))
    for qt in range(TOK):
        tq = token_at[qt * P:(qt + 1) * P][:, None]
        own = token_at[qt * P:(qt + 1) * P][None, :]
        for g, ks in ((0, token_at[None, :]), (1, own), (2, own)):
            window, dil = DILS[g]
            ok = (tq >= ks) & (tq - ks <= window) & ((tq - ks) % dil == 0)
            col = (0, 256, 384)[g]
            mask_a[:, qt, col:col + ks.shape[1]] = np.where(ok, 0.0, BIG)
    c["mask_a"] = mask_a
    row, col = np.arange(P)[:, None], np.arange(P)[None, :]
    c["causal"] = np.concatenate([np.zeros((P, P)), np.where(row >= col, 0.0, BIG)], 1)
    c["causal_t"] = np.concatenate([np.where(col >= row, 0.0, BIG), np.zeros((P, P))], 1)

    def rope(theta, dim, tokens):
        inv = np.float32(theta) ** (-np.arange(0, dim, 2, dtype=np.float32) / np.float32(dim))
        ang = tokens.astype(np.float32)[:, None] * inv[None, :].astype(np.float32)
        both = np.stack([np.cos(ang), np.sin(ang)])
        return both.reshape(2, TOK, P, dim // 2).transpose(2, 0, 1, 3)
    c["rope1"] = rope(10000.0, HD, np.arange(S))
    for name, tokens in (("rope_a", token_at), ("rope_b", np.arange(S))):
        both = rope(500000.0, ROT, tokens).transpose(0, 2, 1, 3)
        cos, sin = both[:, :, 0], both[:, :, 1]
        c[name] = np.stack([cos, cos, sin, -sin], 2)
    sel = np.zeros((P, NH1, P))
    for h in range(NH1):
        sel[h, h, :] = 1
    c["sel"] = sel
    c["rotated"] = (np.arange(P) % HD < ROT).astype(np.float32)[:, None]
    return c


def pack(parts):
    where, cols, n = {}, [], 0
    for name, a in parts.items():
        flat = np.asarray(a).reshape(P, -1)
        where[name] = (n, flat.shape[1])
        cols.append(flat)
        n += flat.shape[1]
    return np.ascontiguousarray(np.concatenate(cols, 1), dtype=np.float32), where


class Stage:

    def __init__(self, name, trips=1, uses=(), quarters=(), counts=None):
        self.name, self.trips, self.uses, self.quarters = name, trips, list(uses), list(quarters)
        self.counts = dict(counts or {})
        assert trips == 1 or len(self.quarters) % SLOTS == 0


class Plan:

    def __init__(self, stages):
        self.stage, tally, self.nq = {}, {}, 0
        for s in stages:
            s.base = dict(tally)
            s.q0 = self.nq
            per = dict(s.counts)
            s.use = {}
            for name, bank in s.uses:
                s.use[name] = (bank, per.get(("bank", bank), 0))
                per[("bank", bank)] = per.get(("bank", bank), 0) + 1
            s.released = []
            for n, by in enumerate(s.quarters):
                slot = (s.q0 + n) % SLOTS
                if by is None:
                    per[("used", slot)] = per.get(("used", slot), 0) + 1
                    s.released.append((("used", slot), per[("used", slot)]))
                else:
                    s.released.append(by)
            s.per = per
            for k, v in per.items():
                tally[k] = tally.get(k, 0) + v * s.trips
            self.nq += len(s.quarters) * s.trips
            self.stage[s.name] = s
        self.total = tally

    def at(self, s, key, k, i=0):
        per = s.per.get(key, 0) if s.trips > 1 else 0
        v = s.base.get(key, 0) + k
        return v if per == 0 else i * per + v

    def filled(self, s, name, i=0):
        bank, n = s.use[name]
        return self.at(s, ("bank", bank), n + 1, i)

    def free(self, s, name, i=0):
        bank, n = s.use[name]
        return self.at(s, ("bank", bank), n, i)

    def slot(self, s, n):
        return (s.q0 + n) % SLOTS

    def turn(self, s, n, i=0, ahead=0):
        v = (s.q0 + n + ahead) // SLOTS
        return v if s.trips == 1 else i * (len(s.quarters) // SLOTS) + v


def up_names(tag):
    return [(f"{tag}{f}", 4 + f) for f in range(4)]


def norm_stage(name, first_bank=0, **more):
    return Stage(name, uses=[(f"t{k}", (first_bank + k) % 8) for k in range(8)],
                 counts={"hiT": 8, "ms": 2, "rstd": 1, "xn": 2, "act_step": 1, **more})


def turn_stage(name, **more):
    return Stage(name, uses=[(f"t{k}", k) for k in range(8)], counts={"hiT": 8, **more})


def row_out_quarters():
    return [None] * 3 + ["r2"] + [None] * 3 + ["r3"]


def row_out_uses():
    return [("r0", 0), ("r2", 2), ("r1", 1), ("r3", 3)]


def attention_uses(n):
    out = []
    for u in range(n):
        out += [(f"s{u}", u % 2), (f"p{u}", 2 + u % 2), (f"o{u}", 4 + u % 2)]
    return out


def make_plan():
    in1 = Stage(
        "in1",
        uses=[("dq0", 0), ("dq1", 1), ("gate_t", 7), ("dk0", 2), ("dk1", 3)]
        + [("mqk0", 4), ("mqk1", 5), ("mqk2", 6), ("mqk3", 7)]
        + [("dv0", 0), ("dv1", 1), ("gate_m", 4), ("qt0", 6), ("qt1", 7), ("mv0", 2), ("mv1", 3)]
        + [("kt0", 6), ("kt1", 7)],
        quarters=[None] * 3 + ["dq1"] + [None] * 3 + ["dk1"] + [None] * 3 + ["mqk3"]
        + [None] * 3 + ["dv1"] + [None] * 3 + ["mv1"],
        counts={"gates": 5, "lnf": 2, "gate_w": 2, "rot": 4, "cv": 4, "ecv": 1, "mqk": 2, "dve_step": 12, "act_step": 2})
    uses = [("mo0", 4), ("mo1", 5)]
    for u in range(2 * NH1):
        uses += [(f"s{u}", u % 2), (f"p{u}", 2), (f"o{u}", 3)]
    for h in range(NH1):
        uses += [(f"m{h}", 6), (f"ls{h}", 7)] + ([(f"lo{h - 1}", 6)] if h else [])
    mix = Stage("mix", uses=uses + [(f"lo{NH1 - 1}", 6)], quarters=[None] * 3 + ["mo1"],
                counts={"prob": 8, "pd": 8, "oms": 12, "wm": 4, "gated": 4, "orstd": 1, "osq": 3,
                        "dve_step": 24 + 16, "sig": 2, "act_step": 1 + 2})

    proj_a = []
    q_a = []
    for g in range(NG):
        proj_a += [(f"q{g}0", 0), (f"q{g}1", 1), (f"k{g}0", 2), (f"k{g}1", 3)]
        proj_a += [(f"qt{g}0", 6), (f"qt{g}1", 7), (f"v{g}0", 4), (f"v{g}1", 5), (f"kt{g}0", 6), (f"kt{g}1", 7)]
        q_a += [None] * 3 + [f"q{g}1"] + [None] * 3 + [f"k{g}1"] + [None] * 3 + [f"v{g}1"]
    half_a = Stage("half_a", trips=2, uses=proj_a + attention_uses(16), quarters=q_a,
                   counts={"sq": 12, "ms8": 12, "rs8": 12, "rot": 12, "act_step": 12, "prob": 16, "dve_step": 12 + 16})
    proj_b = [("q00", 0), ("q01", 1), ("k00", 2), ("k01", 3), ("qt00", 6), ("qt01", 7),
              ("v00", 4), ("v01", 5), ("kt00", 6), ("kt01", 7)]
    half_b = Stage("half_b", trips=2, uses=proj_b + attention_uses(8),
                   quarters=[None] * 3 + ["q01"] + [None] * 3 + ["k01"] + [None] * 3 + ["v01"],
                   counts={"sq": 4, "ms8": 4, "rs8": 4, "rot": 4, "act_step": 4, "prob": 8, "dve_step": 4 + 8})
    acc = [(f"acc{b}", b) for b in range(4)]

    def ffn(tag):
        up = {"cv": 4, "silu": 1, "u": 1, "uhi": 1, "ulo": 1, "dve_step": 4}
        return [
            Stage(f"ffn_{tag}_head", uses=up_names("a") + up_names("b"),
                  quarters=[None] * 3 + ["a3"] + [None] * 3 + ["b3"] + [None] * 2,
                  counts={k: 2 * v for k, v in up.items()}),
            Stage(f"ffn_{tag}_loop", trips=(U2 - 3) // 2, uses=up_names("a") + up_names("b"),
                  quarters=[None] * 3 + ["a3"] + [None] * 5 + ["b3"] + [None] * 2,
                  counts={k: 2 * v for k, v in up.items()}),
            Stage(f"ffn_{tag}_tail", uses=up_names("a") + acc,
                  quarters=[None] * 3 + ["a3"] + [None] * 3 + ["acc3"], counts=up),
        ]
    mlp_up = {"u": 1, "uhi": 1, "ulo": 1}
    stages = [
        Stage("load", counts={"dve_step": 5}),
        norm_stage("norm_in1"), in1, mix,
        turn_stage("turn_mix"),
        Stage("out1", uses=row_out_uses(), quarters=row_out_quarters()),
        Stage("post_mix", counts={"msq": 4, "pms": 1, "rstd": 1, "act_step": 1, "x_new": 2}),
        norm_stage("norm_mlp", 4),
        Stage("mlp_head", uses=up_names("a") + up_names("b"),
              quarters=[None] * 3 + ["a3"] + [None] * 3 + ["b3"] + [None] * 4, counts={k: 2 * v for k, v in mlp_up.items()}),
        Stage("mlp_loop", trips=U1 - 2, uses=up_names("a"), quarters=[None] * 3 + ["a3"] + [None] * 4, counts=mlp_up),
        Stage("mlp_tail", uses=acc, quarters=[None] * 3 + ["acc3"]),
        Stage("post_mlp", counts={"msq": 4, "pms": 1, "rstd": 1, "act_step": 1, "x_new": 2}),
        norm_stage("norm_a"), half_a,
        turn_stage("turn_a"),
        Stage("out_a", uses=row_out_uses(), quarters=row_out_quarters()),
        norm_stage("norm_ffn_a", 4), *ffn("a"),
        norm_stage("norm_b"), half_b,
        turn_stage("turn_b"),
        Stage("out_b", uses=row_out_uses(), quarters=row_out_quarters()),
        norm_stage("norm_ffn_b", 4), *ffn("b"),
    ]
    return Plan(stages)


def rope_view(ap, heads, halves, dim):
    return ap.rearrange("p (h s d) -> p h s d", h=heads, s=halves, d=dim)


def blocks_kernel(nc, ins, out, at_const, at_col, at_row):
    plan = make_plan()
    st = plan.stage
    at, filled, free = plan.at, plan.filled, plan.free
    with ExitStack() as ctx:
        def sb(name, shape, dt=F32):
            return ctx.enter_context(nc.sbuf_tensor(name, shape, dt))

        def sem(name):
            return ctx.enter_context(nc.semaphore(name))

        ps = ctx.enter_context(nc.psum_tensor("ps", [P, 8, 512], F32))
        w_in = sb("w_stage", [P, SLOTS, QW])
        w_hi = sb("w_hi", [P, SLOTS, QW], F32R)
        w_lo = sb("w_lo", [P, SLOTS, QW], F32R)
        x = sb("x", [P, TOK, D])
        xn = sb("xn", [P, TOK, D])
        o_sb = sb("o_sb", [P, TOK, D])
        aT_hi = sb("aT_hi", [P, KT, S], F32R)
        aT_lo = sb("aT_lo", [P, KT, S], F32R)
        u32 = sb("u32", [P, 4 * S])
        u_hi = sb("u_hi", [P, 4 * S], F32R)
        u_lo = sb("u_lo", [P, 4 * S], F32R)
        hid = sb("hid", [P, 4, S])
        qz = sb("qz", [P, 12, 2, S])
        kT = sb("kT", [P, 12, S])
        vv = sb("vv", [P, TOK, 1536])
        sm = sb("sm", [P, 2, 512])
        prob = sb("prob", [P, 2, 512])
        pdf = sb("pdf", [P, 2, S])
        pts = sb("pts", [P, 2, 512])
        xq = sb("xq", [P, TOK, 512])
        sqb = sb("sqb", [P, TOK, 512])
        rt = sb("rt", [P, 2, P])
        consts = sb("consts", [P, sum(n for _, n in at_const.values())])
        cols = sb("cols", [P, sum(n for _, n in at_col.values())])
        rows = sb("rows", [P, sum(n for _, n in at_row.values())])
        small = sb("small", [P, 256])
        gt_in = sb("gt_in", [P, KT * 8])
        gt_hi = sb("gt_hi", [P, KT * 8], F32R)
        gt_lo = sb("gt_lo", [P, KT * 8], F32R)
        gi = sb("gi", [4, S])
        atok = sb("atok", [P, 2, TOK, 4])
        tabs = sb("tabs", [P, 8, TOK, 2, ROT])
        gq = sb("gq", [P, 8])

        def const(name, *shape):
            a, n = at_const[name]
            v = consts[:, a:a + n]
            return v.rearrange(*shape[:1], **shape[1]) if shape else v

        def col(name, j=None, n=1):
            a, w = at_col[name]
            return cols[:, a:a + w] if j is None else cols[:, a + j:a + j + n]

        def row(name):
            a, n = at_row[name]
            return rows[:, a:a + n]
        ident = const("ident")
        gm = xn[0:4, :, :].rearrange("p t (r s) -> p (t r) s", s=S)
        cell = {}

        def stat(name, n=1):
            if name not in cell:
                cell[name] = (sum(m for _, m in cell.values()), n)
            a, m = cell[name]
            return small[:, a:a + m]

        mqkT = kT[:, 4:8, :]

        turned_keys = prob
        lsm = hid[:].rearrange("p (a b) s -> p a (b s)", a=2)
        wmat = u32[:].rearrange("p (a s) -> p a s", a=2)

        def vm(tok):
            return vv[:, tok, 512:512 + 4 * 132].rearrange("p (h c) -> p h c", c=132)

        full = [sem(f"full{b}") for b in range(8)]
        drained = [sem(f"drained{b}") for b in range(8)]
        loaded = [sem(f"loaded{q}") for q in range(SLOTS)]
        hi_done = [sem(f"hi_done{q}") for q in range(SLOTS)]
        lo_done = [sem(f"lo_done{q}") for q in range(SLOTS)]
        used = [sem(f"used{q}") for q in range(SLOTS)]
        s = {n: sem(n) for n in (
            "x_in0", "x_in1", "ident_in", "cols_in", "const_in", "gate_in", "stored", "hiT", "ms", "rstd", "xn", "act_step", "dve_step",
            "gates", "lnf", "rot", "cv", "ecv", "mqk", "sig", "gated", "prob", "pd", "oms", "wm",
            "orstd", "osq", "sq", "ms8", "rs8", "silu", "u", "uhi", "ulo", "msq", "pms", "x_new", 
            "lam", "const_ready", "gate_w", "unit")}

        def is_full(stg, name, i=0):
            return full[stg.use[name][0]], filled(stg, name, i)

        def is_drained(stg, name, i=0):
            return drained[stg.use[name][0]], filled(stg, name, i)

        def is_free(stg, name, i=0):
            return drained[stg.use[name][0]], free(stg, name, i)

        def bank(stg, name):
            return stg.use[name][0]

        def was_read(stg, n, i):
            by = stg.released[n]
            if isinstance(by, str):
                return is_full(stg, by, i)
            return used[by[0][1]], at(stg, by[0], by[1], i)

        def after_post(name):
            return [(s["x_new"], at(st[name], "x_new", t + 1)) for t in range(TOK)]

        def after_sum(name, last):
            return [is_drained(st[name], last[t]) for t in range(TOK)]

        @contextmanager
        def trips(eng, stg):
            if stg.trips == 1:
                yield 0
            else:
                with eng.Fori(0, stg.trips) as i:
                    yield i

        class Chain:

            def __init__(self, eng, key):
                self.eng, self.key, self.n = eng, key, 0

            def enter(self, stg, i):
                self.stg, self.i, self.n = stg, i, 0

            def link(self, ins):
                self.n += 1
                ins.then_inc(s[self.key], 1)
                self.eng.wait_ge(s[self.key], at(self.stg, self.key, self.n, self.i))

            def leave(self):
                want = self.stg.per.get(self.key, 0)
                assert self.n == want, f"{self.stg.name} {self.key}: {self.n} increments, {want} in the plan"

        block = ctx.enter_context(nc.Block())

        @block.sync
        def _(sp):
            for t in range(TOK):
                sp.dma_start(x[:, t, :], ins["x"][0, t * P:(t + 1) * P, :]).then_inc(s[f"x_in{t}"], 16)
            sp.dma_start(consts[:, 0:P], ins["consts"][:, 0:P]).then_inc(s["ident_in"], 16)
            sp.dma_start(cols[:], ins["cols"]).then_inc(s["cols_in"], 16)

            def k_rows(w):
                return w.rearrange("(k p) n -> p k n", p=P)

            def load_cols(stg, i, n0, w, c0):
                for q in range(4):
                    sl = slice(c0, c0 + 512) if isinstance(c0, int) else bass.ds(c0, 512)
                    slot = plan.slot(stg, n0 + q)
                    if stg.q0 + n0 + q >= SLOTS:
                        sp.wait_ge(lo_done[slot], plan.turn(stg, n0 + q, i))
                    sp.dma_start(w_in[:, slot, :].rearrange("p (k n) -> p k n", k=2),
                                 k_rows(w)[:, 2 * q:2 * q + 2, sl]).then_inc(loaded[slot], 16)

            def load_pair(stg, i, n0, w, j):
                load_cols(stg, i, n0, w, j * 512)

            def load_rows(stg, i, n0, nq, w, t0):
                for q in range(nq):
                    slot = plan.slot(stg, n0 + q)
                    if stg.q0 + n0 + q >= SLOTS:
                        sp.wait_ge(lo_done[slot], plan.turn(stg, n0 + q, i))
                    r0 = (t0 + q) * P
                    sl = slice(r0, r0 + P) if isinstance(r0, int) else bass.ds(r0, P)
                    sp.dma_start(w_in[:, slot, :], w[sl, :]).then_inc(loaded[slot], 16)

            S_ = st["in1"]
            w = ins["w_in"][0]
            for n, c0 in enumerate((0, 512, 1536, 1024, 2048)):
                load_cols(S_, 0, 4 * n, w, c0)
                if n == 0:
                    sp.dma_start(gt_in[:].rearrange("p (k n) -> p k n", k=KT),
                                 k_rows(w)[:, :, 3072:3080]).then_inc(s["gate_in"], 16)
                    sp.dma_start(consts[:, P:], ins["consts"][:, P:]).then_inc(s["const_in"], 16)
                    sp.dma_start(rows[:], ins["rows"].partition_broadcast(P)).then_inc(s["const_in"], 16)
            load_cols(st["mix"], 0, 0, w, 2560)
            for n in range(2):
                load_cols(st["out1"], 0, 4 * n, ins["w_out"][0], 512 * n)
            up, down = ins["w_up"][0], ins["w_down"][0]
            S_ = st["mlp_head"]
            load_cols(S_, 0, 0, up, 0)
            load_cols(S_, 0, 4, up, 512)
            load_rows(S_, 0, 8, 4, down, 0)
            S_ = st["mlp_loop"]
            with trips(sp, S_) as i:
                load_cols(S_, i, 0, up, i * 512 + 1024)
                load_rows(S_, i, 4, 4, down, i * 4 + 4)
            load_rows(st["mlp_tail"], 0, 0, 4, down, 4 * (U1 - 1))

            def attention_weights(S_, w, groups):
                with trips(sp, S_) as i:
                    for g in range(groups):
                        for kind in range(3):
                            load_cols(S_, i, (g * 3 + kind) * 4, w, i * 512 + (kind * groups + g) * D)

            def ffn_weights(tag, layer):
                up, down = ins["ffn_w_up"][layer], ins["ffn_w_down"][layer]
                S_ = st[f"ffn_{tag}_head"]
                load_pair(S_, 0, 0, up, 0)
                load_pair(S_, 0, 4, up, 1)
                load_rows(S_, 0, 8, 2, down, 0)
                S_ = st[f"ffn_{tag}_loop"]
                with trips(sp, S_) as i:
                    load_pair(S_, i, 0, up, i * 2 + 2)
                    load_rows(S_, i, 4, 2, down, i * 4 + 2)
                    load_pair(S_, i, 6, up, i * 2 + 3)
                    load_rows(S_, i, 10, 2, down, i * 4 + 4)
                S_ = st[f"ffn_{tag}_tail"]
                load_pair(S_, 0, 0, up, U2 - 1)
                load_rows(S_, 0, 4, 4, down, 2 * (U2 - 2))

            attention_weights(st["half_a"], ins["a_w_qkv"][0], NG)
            for n in range(2):
                load_cols(st["out_a"], 0, 4 * n, ins["a_w_o"][0], 512 * n)
            ffn_weights("a", 0)
            attention_weights(st["half_b"], ins["b_w_qkv"][0], 1)
            for n in range(2):
                load_cols(st["out_b"], 0, 4 * n, ins["b_w_o"][0], 512 * n)
            ffn_weights("b", 1)
            for b, (t, h) in enumerate(((0, 0), (0, 1), (1, 0), (1, 1))):
                sp.wait_ge(*is_drained(st["ffn_b_tail"], f"acc{2 * t + h}"))
                sp.dma_start(out[0, t * P:(t + 1) * P, h * 512:(h + 1) * 512],
                             x[:, t, h * 512:(h + 1) * 512]).then_inc(s["stored"], 16)
            sp.wait_ge(s["stored"], 64)

        def units_a():
            mask = const("mask_a", "p (t c) -> p t c", dict(t=TOK))
            for pr in range(4):
                for h in range(2):
                    for qt in range(TOK):
                        q = [qz[:, g * 4 + pr, h, qt * P:(qt + 1) * P] for g in range(NG)]
                        own = slice(qt * P, (qt + 1) * P)
                        yield dict(
                            tok=qt,
                            scores=[(0, 256, q[0], kT[:, pr, :]), (256, 128, q[1], kT[:, 4 + pr, own]),
                                    (384, 128, q[2], kT[:, 8 + pr, own])],
                            segments=[(0, 512, mask[:, qt, :])],
                            tiles=4,
                            values=[(0, [(0, vv[:, 0, pr * P:(pr + 1) * P]), (1, vv[:, 1, pr * P:(pr + 1) * P]),
                                         (2, vv[:, qt, 512 + pr * P:512 + (pr + 1) * P]),
                                         (3, vv[:, qt, 1024 + pr * P:1024 + (pr + 1) * P])])],
                            outs=[(0, h * HD, pr * P + h * HD)])

        def units_pair(heads, kof, vof):
            mask = const("causal")
            for pr in range(heads):
                for qt in range(TOK):
                    W = (qt + 1) * P
                    yield dict(
                        tok=qt, head=pr,
                        scores=[(c * W, W, qz[:, pr, c, qt * P:(qt + 1) * P], kof(pr)[:, 0:W]) for c in range(2)],
                        segments=[(c * W, W, mask[:, 2 * P - W:2 * P]) for c in range(2)],
                        tiles=2 * (qt + 1),
                        values=[(c * P, [(c * (qt + 1) + t, vof(t, pr)) for t in range(qt + 1)]) for c in range(2)],
                        outs=[(c, c * P + c * HD, pr * P + c * HD) for c in range(2)])

        def units_diff():
            for u in units_pair(NH1, lambda h: kT[:, h, :], lambda t, h: vv[:, t, h * P:(h + 1) * P]):
                u["tiles"] = u["tok"] + 1
                u["values"] = u["values"][:1]
                yield u

        def units_b():
            return units_pair(4, lambda p_: kT[:, p_, :], lambda t, p_: vv[:, t, p_ * P:(p_ + 1) * P])

        MO_TILES = ((0, 1, 2), (3,), (4,), (5,), (6,), (7,))
        MO_STEPS = tuple(u for q in range(4) for u, tiles in enumerate(MO_TILES) if 2 * q + 1 in tiles)

        def oms_at_head(g):
            return 3 * g + 2

        @block.tensor
        def _(pe):
            def await_weights(stg, n, i):
                slot = plan.slot(stg, n)
                pe.wait_ge(lo_done[slot], plan.turn(stg, n, i) + 1)
                return slot

            def signal(stg, n, ins_):
                by = stg.released[n]
                if not isinstance(by, str):
                    ins_.then_inc(used[by[0][1]], 1)

            def dense_rows(stg, i, n0, names, turned=None, tiles=range(KT)):
                for k in tiles:
                    q, kk = divmod(k, 2)
                    slot = await_weights(stg, n0 + q, i)
                    if turned:
                        pe.wait_ge(*is_drained(st[turned], f"t{k}"))
                    wh, wl = (w[:, slot, kk * 512:(kk + 1) * 512] for w in (w_hi, w_lo))
                    for t in range(TOK):
                        o = ps[:, bank(stg, names[t]), :]
                        if k == 0:
                            pe.wait_ge(*is_free(stg, names[t], i))
                        ah, al = (a[:, k, t * P:(t + 1) * P] for a in (aT_hi, aT_lo))
                        pe.matmul(o, ah, wh, start=(k == 0), stop=False)
                        pe.matmul(o, ah, wl, start=False, stop=False)
                        last = pe.matmul(o, al, wh, start=False, stop=(k == KT - 1))
                        if k == KT - 1:
                            last.then_inc(full[bank(stg, names[t])], 1)
                    if kk == 1 and q < 3:
                        signal(stg, n0 + q, last)

            def dense_cols(stg, i, n0, names, turned=None):
                for q in range(4):
                    slot = await_weights(stg, n0 + q, i)
                    for kk in range(2):
                        k = 2 * q + kk
                        if turned:
                            pe.wait_ge(*is_drained(st[turned], f"t{k}"))
                        for f in range(4):
                            c0 = kk * 512 + f * P
                            wh, wl = (w[:, slot, c0:c0 + P] for w in (w_hi, w_lo))
                            o = ps[:, bank(stg, names[f]), 0:S]
                            if k == 0:
                                pe.wait_ge(*is_free(stg, names[f], i))
                            pe.matmul(o, wh, aT_hi[:, k, :], start=(k == 0), stop=False)
                            pe.matmul(o, wh, aT_lo[:, k, :], start=False, stop=False)
                            last = pe.matmul(o, wl, aT_hi[:, k, :], start=False, stop=(k == KT - 1))
                            if k == KT - 1:
                                last.then_inc(full[bank(stg, names[f])], 1)
                    if q < 3:
                        signal(stg, n0 + q, last)

            def down(stg, i, n0, tiles, first=False, final=False):
                for f in tiles:
                    slot = await_weights(stg, n0 + f, i)
                    for t in range(TOK):
                        ah, al = (u[:, f * S + t * P:f * S + (t + 1) * P] for u in (u_hi, u_lo))
                        for h in range(2):
                            wh, wl = (w[:, slot, h * 512:(h + 1) * 512] for w in (w_hi, w_lo))
                            o = ps[:, 2 * t + h, :]
                            b0 = first and f == tiles[0]
                            e0 = final and f == tiles[-1]
                            pe.matmul(o, ah, wh, start=b0, stop=False)
                            pe.matmul(o, ah, wl, start=False, stop=False)
                            last = pe.matmul(o, al, wh, start=False, stop=e0)
                            if e0:
                                last.then_inc(full[2 * t + h], 1)
                    if not e0:
                        signal(stg, n0 + f, last)

            def turn(stg, src, order):
                for k in range(KT):
                    if stg is not st["norm_in1"]:
                        pe.wait_ge(*is_free(stg, f"t{k}"))
                    b = bank(stg, f"t{k}")
                    for t in range(TOK):
                        o = ps[:, b, 0:S]
                        if order is None:
                            m, o = ident, o[:, t * P:(t + 1) * P]
                        elif order == "in":
                            m = const("perm_in")
                            o = o.rearrange("p (r t c) -> p r t c", t=TOK, c=8)[:, :, t, :]
                        else:
                            m = const("perm_out")
                            o = o.rearrange("p (r t c) -> p r t c", t=TOK, c=2)[:, :, t, :]
                        last = pe.transpose(o, src[:, t, k * P:(k + 1) * P], m)
                    last.then_inc(full[b], 1)

            def norm(stg, order=None):
                pe.wait_ge(s["xn"], at(stg, "xn", 2))
                turn(stg, xn, order)

            def attention(stg, units, i, probs, ready=None, prefix=""):
                units = list(units)
                n = len(units)
                for u in range(n + 2):
                    if u < n:
                        un = units[u]
                        b = bank(stg, f"s{u}")
                        pe.wait_ge(*is_free(stg, f"s{u}", i))
                        for c, W, q, k in un["scores"]:
                            last = pe.matmul(ps[:, b, c:c + W], q, k, start=True, stop=True)
                        last.then_inc(full[b], 1)
                    if 1 <= u <= n:
                        v = u - 1
                        b = bank(stg, f"p{v}")
                        pe.wait_ge(*is_free(stg, f"p{v}", i))
                        pe.wait_ge(s[ready], at(stg, ready, v + 1, i))
                        for t in range(units[v]["tiles"]):
                            last = pe.transpose(ps[:, b, t * P:(t + 1) * P], probs[:, v % 2, t * P:(t + 1) * P], ident)
                        last.then_inc(full[b], 1)
                    if u >= 2:
                        v = u - 2
                        b = bank(stg, f"o{v}")
                        pe.wait_ge(*is_free(stg, f"o{v}", i))
                        pe.wait_ge(*is_drained(stg, f"p{v}", i))
                        for c, pairs in units[v]["values"]:
                            for j, (t, val) in enumerate(pairs):
                                last = pe.matmul(ps[:, b, c:c + P], pts[:, v % 2, t * P:(t + 1) * P], val,
                                                 start=(j == 0), stop=(j == len(pairs) - 1))
                        last.then_inc(full[b], 1)

            def turn_heads(stg, names, i, n_rot, src=xq):
                pe.wait_ge(s["rot"], at(stg, "rot", n_rot, i))
                for h in range(2):
                    b = bank(stg, names[h])
                    pe.wait_ge(*is_free(stg, names[h], i))
                    for j in range(2):
                        for t in range(TOK):
                            last = pe.transpose(ps[:, b, j * S + t * P:j * S + (t + 1) * P],
                                                src[:, t, (2 * h + j) * P:(2 * h + j + 1) * P], ident)
                    last.then_inc(full[b], 1)

            pe.wait_ge(s["ident_in"], 16)
            norm(st["norm_in1"])
            S_ = st["in1"]
            dense_rows(S_, 0, 0, ("dq0", "dq1"), "norm_in1")
            pe.wait_ge(s["gate_w"], at(S_, "gate_w", 2))
            pe.wait_ge(*is_free(S_, "gate_t"))
            for gi in range(2):
                o = ps[0:4, 7, gi * S:(gi + 1) * S]
                for k in range(KT):
                    gh, gl = (g_[:, k * 8 + 4 * gi:k * 8 + 4 * gi + 4] for g_ in (gt_hi, gt_lo))
                    pe.matmul(o, gh, aT_hi[:, k, :], start=(k == 0), stop=False)
                    pe.matmul(o, gh, aT_lo[:, k, :], start=False, stop=False)
                    last = pe.matmul(o, gl, aT_hi[:, k, :], start=False, stop=(k == KT - 1))
            last.then_inc(full[7], 1)
            dense_rows(S_, 0, 4, ("dk0", "dk1"))
            dense_cols(S_, 0, 8, ("mqk0", "mqk1", "mqk2", "mqk3"))
            dense_rows(S_, 0, 12, ("dv0", "dv1"))
            pe.wait_ge(s["gates"], at(S_, "gates", 5))
            pe.wait_ge(*is_free(S_, "gate_m"))
            for j, r in enumerate((5, 7)):
                for t in range(TOK):
                    last = pe.transpose(ps[:, 4, (j * 2 + t) * 4:(j * 2 + t) * 4 + 4],
                                        gm[0:4, r, t * P:(t + 1) * P], ident[0:4, 0:4])
            last.then_inc(full[4], 1)
            turn_heads(S_, ("qt0", "qt1"), 0, 2)
            dense_rows(S_, 0, 16, ("mv0", "mv1"))
            turn_heads(S_, ("kt0", "kt1"), 0, 4, turned_keys)

            S_ = st["mix"]
            units = list(units_diff())
            n = len(units)
            sel = const("sel", "p (h c) -> p h c", dict(h=NH1))
            for u in range(n + 2):
                if u == 0:
                    dense_rows(S_, 0, 0, ("mo0", "mo1"), tiles=MO_TILES[0])
                    for nm in ("qt0", "qt1", "kt0", "kt1", "dv0", "dv1"):
                        pe.wait_ge(*is_drained(st["in1"], nm))
                if u < n:
                    b = bank(S_, f"s{u}")
                    pe.wait_ge(*is_free(S_, f"s{u}"))
                    for c, W, q, k in units[u]["scores"]:
                        last = pe.matmul(ps[:, b, c:c + W], q, k, start=True, stop=True)
                    last.then_inc(full[b], 1)
                if u == 0:
                    pe.wait_ge(s["const_ready"], 2)
                    pe.wait_ge(s["mqk"], at(st["in1"], "mqk", 2))
                    for nm in ("mv0", "mv1"):
                        pe.wait_ge(*is_drained(st["in1"], nm))
                h, odd = divmod(u, 2)
                if h < NH1 and not odd:
                    pe.wait_ge(*is_free(S_, f"m{h}"))
                    pe.matmul(ps[:, 6, 0:S], sel[0:4, h, :], gm[0:4, 6, :], start=True, stop=True).then_inc(full[6], 1)
                    r0 = (h % 2) * HD
                    pe.wait_ge(*is_free(S_, f"ls{h}"))
                    kk, qq = mqkT[r0:r0 + HD, 2 + h // 2, :], mqkT[r0:r0 + HD, h // 2, :]
                    pe.matmul(ps[:, 7, 0:S], kk[:, 0:P], qq, start=True, stop=True)
                    pe.matmul(ps[:, 7, S:S + P], kk[:, P:S], qq[:, P:S], start=True, stop=True).then_inc(full[7], 1)
                if 1 <= u < len(MO_TILES):
                    dense_rows(S_, 0, 0, ("mo0", "mo1"), tiles=MO_TILES[u])
                if 1 <= u <= n:
                    v = u - 1
                    pe.wait_ge(*is_free(S_, f"p{v}"))
                    pe.wait_ge(s["pd"], at(S_, "pd", v + 1))
                    for t in range(units[v]["tiles"]):
                        last = pe.transpose(ps[:, 2, t * P:(t + 1) * P], pdf[:, v % 2, t * P:(t + 1) * P], ident)
                    last.then_inc(full[2], 1)
                if u >= 2:
                    v = u - 2
                    pe.wait_ge(*is_free(S_, f"o{v}"))
                    pe.wait_ge(*is_drained(S_, f"p{v}"))
                    for c, pairs in units[v]["values"]:
                        for j, (t, val) in enumerate(pairs):
                            last = pe.matmul(ps[:, 3, c:c + P], pts[:, v % 2, t * P:(t + 1) * P], val,
                                             start=(j == 0), stop=(j == len(pairs) - 1))
                    last.then_inc(full[3], 1)
                if h >= 1 and not odd and h <= NH1:
                    g = h - 1
                    pe.wait_ge(*is_free(S_, f"lo{g}"))
                    pe.wait_ge(*is_drained(S_, f"ls{g}"))
                    w = lsm[:, g % 2, :]
                    pe.matmul(ps[:, 6, 0:129], w[:, 0:P], vm(0)[:, g, 0:129], start=True, stop=True)
                    pe.matmul(ps[:, 6, 256:385], w[:, P:2 * P], vm(0)[:, g, 0:129], start=True, stop=False)
                    pe.matmul(ps[:, 6, 256:385], w[:, 2 * P:3 * P], vm(1)[:, g, 0:129],
                              start=False, stop=True).then_inc(full[6], 1)

            pe.wait_ge(s["osq"], at(S_, "osq", 3))
            turn(st["turn_mix"], o_sb, None)

            def project_out(name, turned):
                stg = st[name]
                dense_rows(stg, 0, 0, ("r0", "r2"), turned)
                dense_rows(stg, 0, 4, ("r1", "r3"))
            project_out("out1", "turn_mix")

            norm(st["norm_mlp"])
            def await_hidden(stg, n, i):
                pe.wait_ge(s["ulo"], at(stg, "ulo", n, i))

            A4, B4 = [f"a{f}" for f in range(4)], [f"b{f}" for f in range(4)]
            S_ = st["mlp_head"]
            dense_cols(S_, 0, 0, A4, "norm_mlp")
            dense_cols(S_, 0, 4, B4)
            await_hidden(S_, 1, 0)
            down(S_, 0, 8, range(4), first=True)
            S_ = st["mlp_loop"]
            with trips(pe, S_) as i:
                dense_cols(S_, i, 0, A4)
                await_hidden(S_, 0, i)
                down(S_, i, 4, range(4))
            S_ = st["mlp_tail"]
            await_hidden(S_, 0, 0)
            down(S_, 0, 0, range(4), final=True)

            def project_heads(S_, i, groups, turned):
                for g in range(groups):
                    n = g * 12
                    dense_rows(S_, i, n, (f"q{g}0", f"q{g}1"), turned if g == 0 else None)
                    dense_rows(S_, i, n + 4, (f"k{g}0", f"k{g}1"))
                    turn_heads(S_, (f"qt{g}0", f"qt{g}1"), i, 4 * g + 2)
                    dense_rows(S_, i, n + 8, (f"v{g}0", f"v{g}1"))
                    turn_heads(S_, (f"kt{g}0", f"kt{g}1"), i, 4 * g + 4)
                g = groups - 1
                for nm in (f"v{g}0", f"v{g}1", f"kt{g}0", f"kt{g}1"):
                    pe.wait_ge(*is_drained(S_, nm, i))

            def ffn(tag):
                norm(st[f"norm_ffn_{tag}"])
                S_ = st[f"ffn_{tag}_head"]
                dense_cols(S_, 0, 0, A4, f"norm_ffn_{tag}")
                dense_cols(S_, 0, 4, B4)
                await_hidden(S_, 1, 0)
                down(S_, 0, 8, range(2), first=True)
                S_ = st[f"ffn_{tag}_loop"]
                with trips(pe, S_) as i:
                    dense_cols(S_, i, 0, A4)
                    await_hidden(S_, 0, i)
                    down(S_, i, 4, range(2))
                    dense_cols(S_, i, 6, B4)
                    await_hidden(S_, 1, i)
                    down(S_, i, 10, range(2))
                S_ = st[f"ffn_{tag}_tail"]
                dense_cols(S_, 0, 0, A4)
                await_hidden(S_, 0, 0)
                down(S_, 0, 4, range(2))
                await_hidden(S_, 1, 0)
                down(S_, 0, 6, range(2), final=True)

            norm(st["norm_a"], "in")
            S_ = st["half_a"]
            with trips(pe, S_) as i:
                project_heads(S_, i, NG, "norm_a")
                attention(S_, units_a(), i, prob, "prob")
            for b in (4, 5):
                pe.wait_ge(drained[b], at(st["turn_a"], ("bank", b), 0))
            turn(st["turn_a"], o_sb, "out")
            project_out("out_a", "turn_a")
            ffn("a")
            norm(st["norm_b"])
            S_ = st["half_b"]
            with trips(pe, S_) as i:
                project_heads(S_, i, 1, "norm_b")
                attention(S_, units_b(), i, prob, "prob")
            for b in (4, 5):
                pe.wait_ge(drained[b], at(st["turn_b"], ("bank", b), 0))
            turn(st["turn_b"], o_sb, None)
            project_out("out_b", "turn_b")
            ffn("b")

        @block.scalar
        def _(act):
            chain = Chain(act, "act_step")
            LN_EXP = "natural_log_exp_and_others"

            def split(stg, n, i=0):
                if stg.q0 + n + SLOTS >= plan.nq:
                    return
                slot = plan.slot(stg, n)
                act.wait_ge(*was_read(stg, n, i))
                act.wait_ge(loaded[slot], (plan.turn(stg, n, i, SLOTS) + 1) * 16)
                act.activation(w_hi[:, slot, :], w_in[:, slot, :], ACT.Copy).then_inc(hi_done[slot], 1)

            def splits(stg, ns, i=0):
                for n in ns:
                    split(stg, n, i)

            def rsqrt(dst, src, tmp, key):
                chain.link(act.activation(tmp, src, ACT.Ln, bias=EPS))
                act.activation(dst, tmp, ACT.Exp, scale=-0.5).then_inc(s[key], 1)

            def turned(stg, gain):
                for k in range(KT):
                    act.wait_ge(*is_full(stg, f"t{k}"))
                    g = 1.0 if gain is None else gain[:, k:k + 1]
                    act.activation(aT_hi[:, k, :], ps[:, bank(stg, f"t{k}"), 0:S], ACT.Copy, scale=g).then_inc(s["hiT"], 1)

            def norm(stg, gain, x_ready):
                chain.enter(stg, 0)
                act.wait_ge(*x_ready[0])
                act.activation(hid[:].rearrange("p a b -> p (a b)"), x[:, 0, :], ACT.Square, scale=D ** -0.5,
                               accum_out=stat("ms", 2)[:, 0:1]).then_inc(s["ms"], 1)
                act.wait_ge(s["ms"], at(stg, "ms", 2))
                rsqrt(stat("rstd", 2), stat("ms", 2), stat("lnms", 2), "rstd")
                act.wait_ge(*x_ready[1])
                act.wait_ge(s["rstd"], at(stg, "rstd", 1))
                act.activation(xn[:, 1, :], x[:, 1, :], ACT.Copy, scale=stat("rstd", 2)[:, 1:2]).then_inc(s["xn"], 1)
                chain.leave()
                if stg is st["norm_in1"]:
                    first_split(0)
                turned(stg, gain)

            def first_split(slot):
                act.wait_ge(loaded[slot], 16)
                act.activation(w_hi[:, slot, :], w_in[:, slot, :], ACT.Copy).then_inc(hi_done[slot], 1)

            def post_norm(name, out_stage, names):
                stg = st[name]
                chain.enter(stg, 0)
                for n, nm in enumerate(names):
                    act.wait_ge(*is_full(out_stage, nm))
                    act.activation(hid[:].rearrange("p a b -> p (a b)")[:, (n % 2) * 512:(n % 2 + 1) * 512],
                                   ps[:, n, :], ACT.Square, scale=D ** -0.5,
                                   accum_out=stat("msq", 4)[:, n:n + 1]).then_inc(s["msq"], 1)
                    act.wait_ge(s["msq"], at(stg, "msq", n + 1))
                act.wait_ge(s["pms"], at(stg, "pms", 1))
                rsqrt(stat("prstd", 2), stat("pms", 2), stat("lnms", 2), "rstd")
                chain.leave()

            def attention(stg, units, i):
                units = list(units)
                n = len(units)
                for u in range(n + 1):
                    if u < n:
                        un = units[u]
                        act.wait_ge(*is_drained(stg, f"s{u}", i))
                        if u >= 2:
                            act.wait_ge(*is_full(stg, f"p{u - 2}", i))
                        nseg = len(un["segments"])
                        for g, (c, W, _) in enumerate(un["segments"]):
                            last = act.activation(prob[:, u % 2, c:c + W], sm[:, u % 2, c:c + W], ACT.Exp, scale=-1.0,
                                                  bias=stat(f"nmax{u % 2}", 2)[:, g:g + 1],
                                                  accum_out=stat(f"den{u % 2}", 2)[:, g:g + 1])
                        last.then_inc(s["prob"], 1)
                    if 1 <= u <= n:
                        v = u - 1
                        act.wait_ge(*is_full(stg, f"p{v}", i))
                        if v >= 2:
                            act.wait_ge(*is_full(stg, f"o{v - 2}", i))
                        W = units[v]["tiles"] * P
                        b = bank(stg, f"p{v}")
                        act.activation(pts[:, v % 2, 0:W], ps[:, b, 0:W], ACT.Copy).then_inc(drained[b], 1)

            def evac_v(stg, name, i, dst, src=None):
                act.wait_ge(*is_full(stg, name, i))
                b = bank(stg, name)
                src = ps[:, b, :] if src is None else src
                act.activation(dst, src, ACT.Copy).then_inc(drained[b], 1)

            def evac_q(stg, name, i, j0, scale):
                act.wait_ge(*is_full(stg, name, i))
                b = bank(stg, name)
                v = ps[:, b, :].rearrange("p (j s) -> p j s", j=2)
                for h in range(2):
                    r = slice(h * HD, (h + 1) * HD)
                    sc = scale if isinstance(scale, float) else scale[r, :]
                    last = act.activation(qz[r, j0:j0 + 2, h, :], v[r, :, :], ACT.Copy, scale=sc)
                last.then_inc(drained[b], 1)

            def evac_k(stg, name, i, j0, scale):
                act.wait_ge(*is_full(stg, name, i))
                b = bank(stg, name)
                act.activation(kT[:, j0:j0 + 2, :], ps[:, b, :].rearrange("p (j s) -> p j s", j=2), ACT.Copy,
                               scale=scale).then_inc(drained[b], 1)

            act.preload_act_table_set(LN_EXP)
            S_ = st["norm_in1"]
            act.wait_ge(s["cols_in"], 16)
            norm(S_, col("g_mix"), [(s[f"x_in{t}"], 16) for t in range(TOK)])
            for slot in range(1, SLOTS):
                first_split(slot)
            act.wait_ge(s["gate_in"], 16)
            act.activation(gt_hi[:], gt_in[:], ACT.Copy).then_inc(s["gate_w"], 1)
            act.wait_ge(s["lam"], 1)
            act.activation(stat("elam", 2), stat("dots", 2), ACT.Exp).then_inc(s["lam"], 1)

            S_ = st["in1"]
            chain.enter(S_, 0)
            splits(S_, range(0, 4))
            splits(S_, range(4, 8))
            act.wait_ge(s["gates"], at(S_, "gates", 2))
            act.activation(gm[0:4, 2, :], gm[0:4, 1, :], ACT.Exp).then_inc(s["lnf"], 1)
            act.wait_ge(s["lnf"], at(S_, "lnf", 1))
            act.activation(gm[0:4, 3, :], gm[0:4, 2, :], ACT.Ln, bias=1.0).then_inc(s["lnf"], 1)
            splits(S_, range(8, 12))
            for f in range(4):
                act.wait_ge(*is_full(S_, f"mqk{f}"))
                act.activation(hid[:, f, :], ps[:, 4 + f, 0:S], ACT.Identity, scale=col("cw1", f * 4 + 3),
                               bias=col("cb1", f)).then_inc(s["cv"], 1)
            splits(S_, range(12, 16))
            for t in range(TOK):
                evac_v(S_, f"dv{t}", 0, vv[:, t, 0:512])
            act.wait_ge(*is_full(S_, "gate_m"))
            act.activation(atok[:, 0, :, :], ps[:, 4, 0:8].rearrange("p (t h) -> p t h", t=2), ACT.Copy)
            act.activation(atok[:, 1, :, :], ps[:, 4, 8:16].rearrange("p (t h) -> p t h", t=2), ACT.Exp,
                           scale=-1.0).then_inc(drained[4], 1)
            for f in range(4):
                act.wait_ge(*is_drained(S_, f"mqk{f}"))
            chain.link(act.activation(u32[:], hid[:].rearrange("p a b -> p (a b)"), ACT.Exp, scale=-1.0))
            chain.link(act.activation(u32[:], u32[:], ACT.Ln, bias=1.0))
            act.activation(u32[:], u32[:], ACT.Exp, scale=-1.0).then_inc(s["ecv"], 1)
            act.wait_ge(s["const_ready"], 2)
            for j in range(2):
                evac_q(S_, f"qt{j}", 0, 2 * j, -(HD ** -0.5))
            splits(S_, range(16, 20))
            for t in range(TOK):
                evac_v(S_, f"mv{t}", 0, vm(t)[:, :, 0:VD], ps[:, 2 + t, :].rearrange("p (h c) -> p h c", h=NH1))
            for j in range(2):
                evac_k(S_, f"kt{j}", 0, 2 * j, 1.0)
            chain.leave()

            S_ = st["mix"]
            chain.enter(S_, 0)
            units = list(units_diff())
            n = len(units)
            for u in range(n + 2):
                if u < n:
                    act.wait_ge(*is_drained(S_, f"s{u}"))
                    if u >= 2:
                        act.wait_ge(s["pd"], at(S_, "pd", u - 1))
                    for g, (c, W, _) in enumerate(units[u]["segments"]):
                        last = act.activation(prob[:, u % 2, c:c + W], sm[:, u % 2, c:c + W], ACT.Exp, scale=-1.0,
                                              bias=stat(f"nmax{u % 2}", 2)[:, g:g + 1],
                                              accum_out=stat(f"den{u % 2}", 2)[:, g:g + 1])
                    last.then_inc(s["prob"], 1)
                h, odd = divmod(u, 2)
                if h < NH1 and not odd:
                    if h == 0:
                        act.wait_ge(*is_drained(st["in1"], "gate_m"))
                    act.wait_ge(*is_drained(S_, f"m{h}"))
                    if h >= 2:
                        act.wait_ge(*is_drained(S_, f"ls{h - 2}"))
                    for c, W, t in ((0, S, 0), (S, P, 1)):
                        last = act.activation(wmat[:, h % 2, c:c + W], lsm[:, h % 2, c:c + W], ACT.Exp, scale=-1.0,
                                              bias=atok[:, 0, t, h:h + 1])
                    last.then_inc(s["wm"], 1)
                if 1 <= u <= n:
                    v = u - 1
                    act.wait_ge(*is_full(S_, f"p{v}"))
                    if v >= 2:
                        act.wait_ge(*is_full(S_, f"o{v - 2}"))
                    W = units[v]["tiles"] * P
                    act.activation(pts[:, v % 2, 0:W], ps[:, 2, 0:W], ACT.Copy).then_inc(drained[2], 1)
                if u >= 2:
                    v = u - 2
                    un = units[v]
                    act.wait_ge(*is_full(S_, f"o{v}"))
                    act.activation(o_sb[:, un["tok"], un["head"] * P:(un["head"] + 1) * P], ps[:, 3, 0:P],
                                   ACT.Copy).then_inc(drained[3], 1)
                if u in MO_STEPS:
                    split(S_, MO_STEPS.index(u))
                if u in (MO_STEPS[-1] + 1, MO_STEPS[-1] + 2):
                    t = u - MO_STEPS[-1] - 1
                    act.wait_ge(*is_full(S_, f"mo{t}"))
                    act.activation(sqb[:, t, :], ps[:, 4 + t, :], ACT.Exp, scale=-1.0).then_inc(drained[4 + t], 1)
                    act.wait_ge(*is_drained(S_, f"mo{t}"))
                    chain.link(act.activation(sqb[:, t, :], sqb[:, t, :], ACT.Ln, bias=1.0))
                    act.activation(sqb[:, t, :], sqb[:, t, :], ACT.Exp, scale=-1.0).then_inc(s["sig"], 1)
            act.wait_ge(s["oms"], at(S_, "oms", 12))
            rsqrt(stat("orstd", 16), stat("oms", 16), stat("lno", 16), "orstd")
            act.wait_ge(s["orstd"], at(S_, "orstd", 1))
            for h in range(4):
                last = act.activation(o_sb[:, 1, h * P:(h + 1) * P], o_sb[:, 1, h * P:(h + 1) * P], ACT.Copy,
                                      scale=stat("orstd", 16)[:, 8 + h:9 + h])
            last.then_inc(s["osq"], 1)
            chain.leave()
            turned(st["turn_mix"], col("g_heads"))
            splits(st["out1"], range(8))
            post_norm("post_mix", st["out1"], ("r0", "r1", "r2", "r3"))
            norm(st["norm_mlp"], col("g_mlp"), after_post("post_mix"))

            def relu_rows(stg, i, names, first):
                for f in range(4):
                    act.wait_ge(*is_full(stg, names[f], i))
                    act.activation(hid[:, f, :], ps[:, 4 + f, 0:S], ACT.Relu).then_inc(drained[4 + f], 1)

            def hidden_hi(stg, i, n, W=4 * S):
                act.wait_ge(s["u"], at(stg, "u", n, i))
                act.activation(u_hi[:, 0:W], u32[:, 0:W], ACT.Copy).then_inc(s["uhi"], 1)

            A4, B4 = [f"a{f}" for f in range(4)], [f"b{f}" for f in range(4)]
            S_ = st["mlp_head"]
            splits(S_, range(0, 4))
            relu_rows(S_, 0, A4, True)
            hidden_hi(S_, 0, 1)
            splits(S_, range(4, 8))
            relu_rows(S_, 0, B4, False)
            splits(S_, range(8, 12))
            hidden_hi(S_, 0, 2)
            S_ = st["mlp_loop"]
            with trips(act, S_) as i:
                splits(S_, range(0, 4), i)
                relu_rows(S_, i, A4, False)
                splits(S_, range(4, 8), i)
                hidden_hi(S_, i, 1)
            splits(st["mlp_tail"], range(4))
            post_norm("post_mlp", st["mlp_tail"], [f"acc{b}" for b in range(4)])

            def project_heads(S_, i, groups, layer):
                n = [0]

                def head_norms(names):
                    for t in range(TOK):
                        act.wait_ge(*is_full(S_, names[t], i))
                        if n[0] >= 2:
                            act.wait_ge(s["ms8"], at(S_, "ms8", n[0] - 1, i))
                        act.activation(sqb[:, t, :], ps[:, bank(S_, names[t]), :], ACT.Square,
                                       scale=HD ** -0.5).then_inc(s["sq"], 1)
                        n[0] += 1
                        act.wait_ge(s["ms8"], at(S_, "ms8", n[0], i))
                        rsqrt(stat(f"rs8{t}", 8), stat(f"ms8{t}", 8), stat(f"ln8{t}", 8), "rs8")
                for g in range(groups):
                    q0 = g * 12
                    splits(S_, range(q0, q0 + 4), i)
                    head_norms((f"q{g}0", f"q{g}1"))
                    splits(S_, range(q0 + 4, q0 + 8), i)
                    for j in range(2):
                        evac_q(S_, f"qt{g}{j}", i, g * 4 + 2 * j, gq[:, 2 * (layer * 3 + g):2 * (layer * 3 + g) + 1])
                    head_norms((f"k{g}0", f"k{g}1"))
                    splits(S_, range(q0 + 8, q0 + 12), i)
                    for t in range(TOK):
                        evac_v(S_, f"v{g}{t}", i, vv[:, t, g * 512:(g + 1) * 512])
                    for j in range(2):
                        evac_k(S_, f"kt{g}{j}", i, g * 4 + 2 * j, gq[:, 2 * (layer * 3 + g) + 1:2 * (layer * 3 + g) + 2])

            def ffn(tag, layer):
                W = 2 * S
                cw = col(f"cw2{tag}").rearrange("p (j c) -> p j c", c=16)

                def convolve(stg, i, names, j, n):
                    for f in range(4):
                        act.wait_ge(*is_full(stg, names[f], i))
                        sc = cw[:, bass.ds(j, 1), 4 * f + 2:4 * f + 3].rearrange("p a b -> p (a b)")
                        bi = cw[:, bass.ds(j, 1), 4 * f + 3:4 * f + 4].rearrange("p a b -> p (a b)")
                        act.activation(hid[:, f, :], ps[:, 4 + f, 0:S], ACT.Identity, scale=sc, bias=bi).then_inc(s["cv"], 1)
                    for f in range(2):
                        act.wait_ge(*is_drained(stg, names[f], i))
                    act.activation(u32[:, W:2 * W], hid[:, 0:2, :].rearrange("p a b -> p (a b)"), ACT.Silu)\
                        .then_inc(s["silu"], 1)
                act.preload_act_table(ACT.Silu)
                S_ = st[f"ffn_{tag}_head"]
                splits(S_, range(0, 4))
                convolve(S_, 0, A4, 0, 1)
                hidden_hi(S_, 0, 1, W)
                splits(S_, range(4, 8))
                convolve(S_, 0, B4, 1, 2)
                splits(S_, range(8, 10))
                hidden_hi(S_, 0, 2, W)
                S_ = st[f"ffn_{tag}_loop"]
                with trips(act, S_) as i:
                    splits(S_, range(0, 4), i)
                    convolve(S_, i, A4, i * 2 + 2, 1)
                    splits(S_, range(4, 6), i)
                    hidden_hi(S_, i, 1, W)
                    splits(S_, range(6, 10), i)
                    convolve(S_, i, B4, i * 2 + 3, 2)
                    splits(S_, range(10, 12), i)
                    hidden_hi(S_, i, 2, W)
                S_ = st[f"ffn_{tag}_tail"]
                splits(S_, range(0, 4))
                convolve(S_, 0, A4, U2 - 1, 1)
                splits(S_, range(4, 6))
                act.wait_ge(*was_read(S_, 5, 0))
                hidden_hi(S_, 0, 1, W)
                splits(S_, range(6, 8))
                act.preload_act_table_set(LN_EXP)

            norm(st["norm_a"], col("g_a"), after_post("post_mlp"))
            S_ = st["half_a"]
            with trips(act, S_) as i:
                chain.enter(S_, i)
                project_heads(S_, i, NG, 0)
                attention(S_, units_a(), i)
                chain.leave()
            turned(st["turn_a"], None)
            splits(st["out_a"], range(8))
            norm(st["norm_ffn_a"], col("g_fa"), after_sum("out_a", ("r1", "r3")))
            ffn("a", 0)
            norm(st["norm_b"], col("g_b"), after_sum("ffn_a_tail", ("acc1", "acc3")))
            S_ = st["half_b"]
            with trips(act, S_) as i:
                chain.enter(S_, i)
                project_heads(S_, i, 1, 1)
                attention(S_, units_b(), i)
                chain.leave()
            turned(st["turn_b"], None)
            splits(st["out_b"], range(8))
            norm(st["norm_ffn_b"], col("g_fb"), after_sum("out_b", ("r1", "r3")))
            ffn("b", 1)

        @block.gpsimd
        def _(pool):
            pool.memset(qz[:], 0.0).then_inc(s["const_ready"], 1)
            for t in range(TOK):
                last = pool.memset(vm(t)[:, :, VD:VD + 1], 1.0)
            last.then_inc(s["const_ready"], 1)
            S_ = st["mix"]
            for t in range(TOK):
                pool.wait_ge(s["sig"], at(S_, "sig", t + 1))
            for g in range(NH1):
                pool.wait_ge(s["oms"], at(S_, "oms", oms_at_head(g)))
                o = o_sb[:, :, 512 + g * P:512 + (g + 1) * P]
                pool.tensor_tensor(o, o, sqb[:, :, g * P:(g + 1) * P], ALU.mult).then_inc(s["gated"], 1)

        @block.vector
        def _(dve):
            chain = Chain(dve, "dve_step")
            link = chain.link

            def split(stg, n, i=0):
                if stg.q0 + n + SLOTS >= plan.nq:
                    return
                slot = plan.slot(stg, n)
                dve.wait_ge(hi_done[slot], plan.turn(stg, n, i, SLOTS) + 1)
                dve.tensor_tensor(w_lo[:, slot, :], w_in[:, slot, :], w_hi[:, slot, :].bitcast(F32),
                                  ALU.subtract).then_inc(lo_done[slot], 1)

            def splits(stg, ns, i=0):
                for n in ns:
                    split(stg, n, i)

            def turned(stg, gain):
                for k in range(KT):
                    dve.wait_ge(s["hiT"], at(stg, "hiT", k + 1))
                    g = 1.0 if gain is None else gain[:, k:k + 1]
                    b = bank(stg, f"t{k}")
                    dve.scalar_tensor_tensor(out=aT_lo[:, k, :], in0=ps[:, b, 0:S], scalar=g,
                                             in1=aT_hi[:, k, :].bitcast(F32), op0=ALU.mult,
                                             op1=ALU.subtract).then_inc(drained[b], 1)

            def norm(stg, gain, x_ready):
                dve.wait_ge(*x_ready[1])
                dve.tensor_tensor_reduce(out=u32[:], in0=x[:, 1, :], in1=x[:, 1, :], scale=1.0 / D, scalar=0.0,
                                         op0=ALU.mult, op1=ALU.add,
                                         accum_out=stat("ms", 2)[:, 1:2]).then_inc(s["ms"], 1)
                dve.wait_ge(*x_ready[0])
                dve.wait_ge(s["rstd"], at(stg, "rstd", 1))
                dve.tensor_scalar(xn[:, 0, :], x[:, 0, :], stat("rstd", 2)[:, 0:1], None, ALU.mult).then_inc(s["xn"], 1)
                if stg is st["norm_in1"]:
                    first_split(0)
                turned(stg, gain)

            def first_split(slot):
                dve.wait_ge(hi_done[slot], 1)
                dve.tensor_tensor(w_lo[:, slot, :], w_in[:, slot, :], w_hi[:, slot, :].bitcast(F32),
                                  ALU.subtract).then_inc(lo_done[slot], 1)

            def post_norm(name, gain):
                stg = st[name]
                dve.wait_ge(s["msq"], at(stg, "msq", 4))
                m = stat("msq", 4).rearrange("p (t h) -> p t h", h=2)
                dve.tensor_tensor(stat("pms", 2).rearrange("p (t h) -> p t h", h=1), m[:, :, 0:1], m[:, :, 1:2],
                                  ALU.add).then_inc(s["pms"], 1)
                dve.wait_ge(s["rstd"], at(stg, "rstd", 1))
                for b in range(4):
                    t, h = divmod(b, 2)
                    sl = slice(h * 512, (h + 1) * 512)
                    dve.scalar_tensor_tensor(out=xn[:, t, sl], in0=ps[:, b, :], scalar=stat("prstd", 2)[:, t:t + 1],
                                             in1=row(gain)[:, sl], op0=ALU.mult, op1=ALU.mult).then_inc(drained[b], 1)
                for t in range(TOK):
                    for h in range(2):
                        b = 2 * t + h
                        sl = slice(h * 512, (h + 1) * 512)
                        if h == 0:
                            dve.wait_ge(drained[b + 1], at(stg, ("bank", b + 1), 0))
                            last = dve.tensor_tensor(x[:, t, sl], x[:, t, sl], xn[:, t, sl], ALU.add)
                        else:
                            dve.tensor_tensor(x[:, t, sl], x[:, t, sl], xn[:, t, sl], ALU.add).then_inc(s["x_new"], 1)

            def add_rows(stg, names):
                for b in range(4):
                    t, h = divmod(b, 2)
                    dve.wait_ge(*is_full(stg, names[b]))
                    sl = slice(h * 512, (h + 1) * 512)
                    dve.tensor_tensor(x[:, t, sl], ps[:, b, :], x[:, t, sl], ALU.add).then_inc(drained[b], 1)

            def attention(stg, units, i, lag_out=2):
                units = list(units)
                n = len(units)
                for u in range(n + 2):
                    if u < n:
                        un = units[u]
                        dve.wait_ge(*is_full(stg, f"s{u}", i))
                        if u >= 2:
                            dve.wait_ge(s["prob"], at(stg, "prob", u - 1, i))
                        b = bank(stg, f"s{u}")
                        dve.sem_inc(s["unit"], 1)
                        for g, (c, W, mask) in enumerate(un["segments"]):
                            last = dve.tensor_tensor_reduce(
                                out=sm[:, u % 2, c:c + W], in0=ps[:, b, c:c + W], in1=mask, scale=1.0, scalar=BIG,
                                op0=ALU.add, op1=ALU.min, accum_out=stat(f"nmax{u % 2}", 2)[:, g:g + 1])
                        last.then_inc(drained[b], 1)
                    if 1 <= u <= n:
                        v = u - 1
                        nseg = len(units[v]["segments"])
                        dve.wait_ge(s["prob"], at(stg, "prob", v + 1, i))
                        if v >= 2:
                            dve.wait_ge(*is_drained(stg, f"o{v - 2}", i))
                        link(dve.reciprocal(stat(f"rden{v % 2}", 2)[:, 0:nseg], stat(f"den{v % 2}", 2)[:, 0:nseg]))
                    if u >= 2:
                        v = u - 2
                        un = units[v]
                        dve.wait_ge(*is_full(stg, f"o{v}", i))
                        b = bank(stg, f"o{v}")
                        for g, c, oc in un["outs"]:
                            if stg.trips > 1:
                                dst = o_sb[:, un["tok"], bass.ds(i * 512 + oc, HD)]
                            last = dve.tensor_scalar(dst, ps[:, b, c:c + HD], stat(f"rden{v % 2}", 2)[:, g:g + 1],
                                                     None, ALU.mult)
                        last.then_inc(drained[b], 1)

            def sum_square(un, v, counted):
                dve.wait_ge(*is_drained(st["mix"], f"o{v}"))
                o = o_sb[:, un["tok"], un["head"] * P:(un["head"] + 1) * P]
                j = un["tok"] * 8 + un["head"]
                if v >= 2:
                    dve.wait_ge(s["oms"], at(st["mix"], "oms", counted[v - 2]))
                dve.tensor_tensor_reduce(out=rt[:, v % 2, :], in0=o, in1=o, scale=1.0 / VD, scalar=0.0, op0=ALU.mult,
                                         op1=ALU.add, accum_out=stat("oms", 16)[:, j:j + 1]).then_inc(s["oms"], 1)

            rtmp = xq[:, 0, 0:S]

            S_ = st["load"]
            chain.enter(S_, 0)
            dve.wait_ge(s["cols_in"], 16)
            norm(st["norm_in1"], col("g_mix"), [(s[f"x_in{t}"], 16) for t in range(TOK)])
            for slot in range(1, SLOTS):
                first_split(slot)
            dve.wait_ge(s["gate_w"], 1)
            dve.tensor_tensor(gt_lo[:], gt_in[:], gt_hi[:].bitcast(F32), ALU.subtract).then_inc(s["gate_w"], 1)
            dve.wait_ge(s["const_in"], 32)
            lam = row("lambda").rearrange("p (v d) -> p v d", v=4)
            for j in range(2):
                last = dve.tensor_tensor_reduce(out=rt[:, j, 0:HD], in0=lam[:, 2 * j, :], in1=lam[:, 2 * j + 1, :],
                                                scale=1.0, scalar=0.0, op0=ALU.mult, op1=ALU.add,
                                                accum_out=stat("dots", 2)[:, j:j + 1])
            last.then_inc(s["lam"], 1)
            g = col("gains")
            link(dve.tensor_scalar(gq[:], g, col("unrotated", 0), col("rotated", 0), ALU.mult, ALU.add))
            gq2 = gq[:].rearrange("p (g c) -> p g c", c=2)
            link(dve.tensor_scalar(gq2[:, :, 0:1], gq2[:, :, 0:1], -(HD ** -0.5), None, ALU.mult))
            link(dve.tensor_scalar(col("g_heads", 0, 4), col("g_heads", 0, 4), 1.0 - LAMBDA_INIT, None, ALU.mult))
            grow = row("gain_rows").rearrange("p (g d) -> p g d", d=ROT)
            for j in range(8):
                dve.tensor_tensor(tabs[:, j, :, :, :].rearrange("p t c d -> p (t c) d"),
                                  const("rope_a" if j < 6 else "rope_b", "p (c d) -> p c d", dict(d=ROT)),
                                  grow[:, j:j + 1, :].broadcast_to([P, 2 * TOK, ROT]), ALU.mult)
            dve.wait_ge(s["lam"], 2)
            e = stat("elam", 2)
            link(dve.tensor_tensor(stat("dlam"), e[:, 1:2], e[:, 0:1], ALU.subtract))
            link(dve.tensor_scalar(stat("neglam"), stat("dlam"), LAMBDA_INIT, None, ALU.subtract))
            chain.leave()

            S_ = st["in1"]
            chain.enter(S_, 0)

            def rotate_full(names, t, dst):
                dve.wait_ge(*is_full(S_, names[t]))
                b = bank(S_, names[t])
                v = rope_view(ps[:, b, :], 8, 2, 32)
                a = rope_view(dst[:, t, :], 8, 2, 32)
                w = rope_view(sqb[:, t, :], 8, 2, 32)
                rp = const("rope1", "p (c t d) -> p c t d", dict(c=2, t=TOK))
                cos, sin = (rp[:, c, t, :].unsqueeze(1) for c in range(2))
                dve.tensor_tensor(dst[:, t, :].rearrange("p (h d) -> p h d", d=32),
                                  ps[:, b, :].rearrange("p (h d) -> p h d", d=32),
                                  cos.broadcast_to([P, 16, 32]), ALU.mult)
                dve.tensor_tensor(w[:, :, 0, :], v[:, :, 1, :], sin.broadcast_to([P, 8, 32]), ALU.mult)
                dve.tensor_tensor(w[:, :, 1, :], v[:, :, 0, :], sin.broadcast_to([P, 8, 32]), ALU.mult)\
                    .then_inc(drained[b], 1)
                dve.wait_ge(drained[b], filled(S_, names[t]))
                dve.tensor_tensor(a[:, :, 0, :], a[:, :, 0, :], w[:, :, 0, :], ALU.subtract)
                dve.tensor_tensor(a[:, :, 1, :], a[:, :, 1, :], w[:, :, 1, :], ALU.add).then_inc(s["rot"], 1)

            splits(S_, range(0, 4))
            for t in range(TOK):
                rotate_full(("dq0", "dq1"), t, xq)
            splits(S_, range(4, 8))
            dve.wait_ge(*is_full(S_, "gate_t"))
            link(dve.tensor_scalar(gi[:], ps[0:4, 7, 0:S], col("b_i", 0)[0:4, :], None, ALU.add))
            dve.tensor_scalar(gm[0:4, 7, :], ps[0:4, 7, S:2 * S], col("b_f", 0)[0:4, :], None, ALU.add)\
                .then_inc(drained[7], 1)
            dve.wait_ge(*is_drained(S_, "gate_t"))
            dve.tensor_scalar(gm[0:4, 0, :], gm[0:4, 7, :], 0.0, None, ALU.min).then_inc(s["gates"], 1)
            link(dve.tensor_scalar(gm[0:4, 6, :], gm[0:4, 7, :], 0.0, None, ALU.max))
            dve.tensor_tensor(gm[0:4, 1, :], gm[0:4, 0, :], gm[0:4, 6, :], ALU.subtract).then_inc(s["gates"], 1)
            for t in range(TOK):
                rotate_full(("dk0", "dk1"), t, turned_keys)
            splits(S_, range(8, 12))
            dve.wait_ge(s["lnf"], at(S_, "lnf", 2))
            link(dve.tensor_tensor(gm[0:4, 3, :], gm[0:4, 0, :], gm[0:4, 3, :], ALU.subtract))
            dve.tensor_tensor_scan(gm[0:4, 4, :], gm[0:4, 3, :], gm[0:4, 3, :], 0.0, ALU.add, ALU.bypass)\
                .then_inc(s["gates"], 1)
            dve.wait_ge(s["gates"], at(S_, "gates", 3))
            link(dve.tensor_tensor(gm[0:4, 5, :], gi[:], gm[0:4, 4, :], ALU.subtract))
            dve.tensor_tensor_scan(gm[0:4, 6, :], gm[0:4, 5, :], gm[0:4, 5, :], 0.0, ALU.max, ALU.bypass)\
                .then_inc(s["gates"], 1)
            dve.wait_ge(s["gates"], at(S_, "gates", 4))
            dve.tensor_tensor(gm[0:4, 7, :], gm[0:4, 4, :], gm[0:4, 6, :], ALU.add).then_inc(s["gates"], 1)
            for f in range(4):
                dve.wait_ge(s["cv"], at(S_, "cv", f + 1))
                for back in (1, 2, 3):
                    ins_ = dve.scalar_tensor_tensor(out=hid[:, f, back:S], in0=ps[:, 4 + f, 0:S - back],
                                                    scalar=col("cw1", f * 4 + 3 - back), in1=hid[:, f, back:S],
                                                    op0=ALU.mult, op1=ALU.add)
                    if back < 3:
                        link(ins_)
                    else:
                        ins_.then_inc(drained[4 + f], 1)
            dve.wait_ge(drained[7], filled(S_, "mqk3"))
            splits(S_, range(12, 16))
            dve.wait_ge(s["ecv"], at(S_, "ecv", 1))
            for j, sc in enumerate((HD ** -0.5, 1.0)):
                dve.scalar_tensor_tensor(out=mqkT[:, 2 * j:2 * j + 2, :].rearrange("p a b -> p (a b)"),
                                         in0=hid[:, 2 * j:2 * j + 2, :].rearrange("p a b -> p (a b)"), scalar=sc,
                                         in1=u32[:, j * 512:(j + 1) * 512], op0=ALU.mult, op1=ALU.mult)\
                    .then_inc(s["mqk"], 1)
            splits(S_, range(16, 20))
            chain.leave()

            S_ = st["mix"]
            chain.enter(S_, 0)
            ct = const("causal_t")

            def mlstm_head(g):
                dve.wait_ge(*is_full(S_, f"lo{g}"))
                v = ps[:, 6, :].rearrange("p (t c) -> p t c", t=2)
                den = v[:, :, VD:VD + 1]
                nd, dm = (stat(n, 2).rearrange("p (t c) -> p t c", t=2) for n in ("nd", "dm"))
                em = atok[:, 1, :, g:g + 1]
                link(dve.tensor_scalar(nd, den, -1.0, None, ALU.mult))
                link(dve.tensor_tensor(nd, nd, em, ALU.max))
                link(dve.tensor_tensor(dm, den, nd, ALU.max))
                link(dve.reciprocal(dm, dm))
                for t in range(TOK):
                    last = dve.tensor_scalar(o_sb[:, t, 512 + g * P:512 + (g + 1) * P], v[:, t, 0:VD],
                                             stat("dm", 2)[:, t:t + 1], None, ALU.mult)
                last.then_inc(drained[6], 1)
                dve.wait_ge(*is_drained(S_, f"lo{g}"))
                for t in range(TOK):
                    o = o_sb[:, t, 512 + g * P:512 + (g + 1) * P]
                    j = t * 8 + 4 + g
                    last = dve.tensor_tensor_reduce(out=xq[:, 1, t * P:(t + 1) * P], in0=o, in1=o, scale=1.0 / VD,
                                                    scalar=0.0, op0=ALU.mult, op1=ALU.add,
                                                    accum_out=stat("oms", 16)[:, j:j + 1])
                last.then_inc(s["oms"], 1)

            units = list(units_diff())
            n = len(units)
            n_oms, counted = 0, []
            for u in range(n + 3):
                if u < n:
                    dve.wait_ge(*is_full(S_, f"s{u}"))
                    if u >= 2:
                        dve.wait_ge(s["prob"], at(S_, "prob", u - 1))
                    b = bank(S_, f"s{u}")
                    dve.sem_inc(s["unit"], 1)
                    for g, (c, W, mask) in enumerate(units[u]["segments"]):
                        last = dve.tensor_tensor_reduce(
                            out=sm[:, u % 2, c:c + W], in0=ps[:, b, c:c + W], in1=mask, scale=1.0, scalar=BIG,
                            op0=ALU.add, op1=ALU.min, accum_out=stat(f"nmax{u % 2}", 2)[:, g:g + 1])
                    last.then_inc(drained[b], 1)
                h, odd = divmod(u, 2)
                if h < NH1 and not odd:
                    dve.wait_ge(*is_full(S_, f"m{h}"))
                    if h >= 2:
                        dve.wait_ge(*is_full(S_, f"lo{h - 2}"))
                    dve.tensor_tensor(lsm[:, h % 2, 0:S], ps[:, 6, 0:S], ct, ALU.add)
                    dve.tensor_tensor(lsm[:, h % 2, S:S + P], ps[:, 6, P:S], ct[:, 0:P], ALU.add)\
                        .then_inc(drained[6], 1)
                if 1 <= u <= n:
                    v = u - 1
                    r = stat(f"rden{v % 2}", 2)
                    W = units[v]["segments"][0][1]
                    dve.wait_ge(s["prob"], at(S_, "prob", v + 1))
                    link(dve.reciprocal(r, stat(f"den{v % 2}", 2)))
                    link(dve.tensor_scalar(stat("rlam"), r[:, 1:2], stat("neglam"), None, ALU.mult))
                    if v >= 2:
                        dve.wait_ge(*is_full(S_, f"p{v - 2}"))
                    link(dve.tensor_scalar(rtmp[:, 0:W], prob[:, v % 2, W:2 * W], stat("rlam"), None, ALU.mult))
                    dve.scalar_tensor_tensor(out=pdf[:, v % 2, 0:W], in0=prob[:, v % 2, 0:W], scalar=r[:, 0:1],
                                             in1=rtmp[:, 0:W], op0=ALU.mult, op1=ALU.add).then_inc(s["pd"], 1)
                if h < NH1 and odd:
                    dve.wait_ge(*is_full(S_, f"ls{h}"))
                    dve.wait_ge(s["wm"], at(S_, "wm", h + 1))
                    dve.tensor_tensor(lsm[:, h % 2, 0:S + P], ps[:, 7, 0:S + P], wmat[:, h % 2, 0:S + P], ALU.mult)\
                        .then_inc(drained[7], 1)
                if u >= 3:
                    sum_square(units[u - 3], u - 3, counted)
                    n_oms += 1
                    counted.append(n_oms)
                if odd and 1 <= h <= NH1:
                    mlstm_head(h - 1)
                    n_oms += 1
                    assert n_oms == oms_at_head(h - 1)
                if u in MO_STEPS:
                    split(S_, MO_STEPS.index(u))
            dve.wait_ge(s["orstd"], at(S_, "orstd", 1))
            dve.wait_ge(s["gated"], at(S_, "gated", 4))
            for t, h0 in ((0, 0), (1, 4)):
                ov = o_sb[:, t, h0 * P:].rearrange("p (h c) -> p h c", c=P)
                r = stat("orstd", 16)[:, t * 8 + h0:t * 8 + 8]
                dve.tensor_tensor(ov, ov, r.unsqueeze(2).broadcast_to([P, 8 - h0, P]), ALU.mult).then_inc(s["osq"], 1)
            chain.leave()
            turned(st["turn_mix"], col("g_heads"))
            splits(st["out1"], range(8))
            post_norm("post_mix", "mix_post")
            norm(st["norm_mlp"], col("g_mlp"), after_post("post_mix"))

            def square(stg, i, n, before):
                for f in range(4):
                    dve.wait_ge(*is_drained(stg, before[f], i))
                if stg is not st["mlp_head"] or n > 1:
                    dve.wait_ge(s["uhi"], at(stg, "uhi", n - 1, i))
                    dve.wait_ge(s["ulo"], at(stg, "ulo", n - 1, i))
                dve.tensor_tensor(u32[:], hid[:].rearrange("p a b -> p (a b)"), hid[:].rearrange("p a b -> p (a b)"),
                                  ALU.mult).then_inc(s["u"], 1)

            def hidden_lo(stg, i, n, W=4 * S):
                dve.wait_ge(s["uhi"], at(stg, "uhi", n, i))
                dve.tensor_tensor(u_lo[:, 0:W], u32[:, 0:W], u_hi[:, 0:W].bitcast(F32), ALU.subtract)\
                    .then_inc(s["ulo"], 1)

            A4, B4 = [f"a{f}" for f in range(4)], [f"b{f}" for f in range(4)]
            S_ = st["mlp_head"]
            splits(S_, range(0, 4))
            square(S_, 0, 1, A4)
            hidden_lo(S_, 0, 1)
            splits(S_, range(4, 8))
            square(S_, 0, 2, B4)
            splits(S_, range(8, 12))
            hidden_lo(S_, 0, 2)
            S_ = st["mlp_loop"]
            with trips(dve, S_) as i:
                splits(S_, range(0, 4), i)
                square(S_, i, 1, A4)
                splits(S_, range(4, 8), i)
                hidden_lo(S_, i, 1)
            splits(st["mlp_tail"], range(4))
            post_norm("post_mlp", "mlp_post")

            def project_heads(S_, i, groups, layer):
                n = [0]

                def head_norms(names, which, j):
                    for t in range(TOK):
                        dve.wait_ge(s["sq"], at(S_, "sq", n[0] + 1, i))
                        dve.tensor_reduce(stat(f"ms8{t}", 8), sqb[:, t, :].rearrange("p (h d) -> p h d", d=HD),
                                          AX.X, ALU.add).then_inc(s["ms8"], 1)
                        n[0] += 1
                        dve.wait_ge(s["rs8"], at(S_, "rs8", n[0], i))
                        b = bank(S_, names[t])
                        xv = xq[:, t, :].rearrange("p (h d) -> p h d", d=HD)
                        dve.tensor_tensor(xv, ps[:, b, :].rearrange("p (h d) -> p h d", d=HD),
                                          stat(f"rs8{t}", 8).unsqueeze(2).broadcast_to([P, 8, HD]),
                                          ALU.mult).then_inc(drained[b], 1)
                        dve.wait_ge(*is_drained(S_, names[t], i))
                        T = tabs[:, j, t, :, :]
                        r1, r2 = (rt[:, c, :].rearrange("p (h d) -> p h d", d=ROT) for c in range(2))
                        dve.tensor_tensor(r1, xv[:, :, 0:ROT], T[:, 0, :].unsqueeze(1).broadcast_to([P, 8, ROT]), ALU.mult)
                        link(dve.tensor_tensor(r2, xv[:, :, 0:ROT], T[:, 1, :].unsqueeze(1).broadcast_to([P, 8, ROT]), ALU.mult))
                        dve.tensor_tensor(xv[:, :, 0:8], r1[:, :, 0:8], r2[:, :, 8:16], ALU.add)
                        dve.tensor_tensor(xv[:, :, 8:16], r1[:, :, 8:16], r2[:, :, 0:8], ALU.add)\
                            .then_inc(s["rot"], 1)
                for g in range(groups):
                    q0 = g * 12
                    splits(S_, range(q0, q0 + 4), i)
                    if g > 0:
                        for j in range(2):
                            dve.wait_ge(*is_full(S_, f"kt{g - 1}{j}", i))
                    head_norms((f"q{g}0", f"q{g}1"), 0, (layer * 3 + g) * 2)
                    splits(S_, range(q0 + 4, q0 + 8), i)
                    for j in range(2):
                        dve.wait_ge(*is_full(S_, f"qt{g}{j}", i))
                    head_norms((f"k{g}0", f"k{g}1"), 1, (layer * 3 + g) * 2 + 1)
                    splits(S_, range(q0 + 8, q0 + 12), i)

            def ffn(tag):
                W = 2 * S
                cw = col(f"cw2{tag}").rearrange("p (j c) -> p j c", c=16)

                def convolve(stg, i, names, j, n):
                    for f in range(4):
                        dve.wait_ge(s["cv"], at(stg, "cv", 4 * (n - 1) + f + 1, i))
                        for back in (1, 2):
                            sc = cw[:, bass.ds(j, 1), 4 * f + 2 - back:4 * f + 3 - back].rearrange("p a b -> p (a b)")
                            ins_ = dve.scalar_tensor_tensor(out=hid[:, f, back:S], in0=ps[:, 4 + f, 0:S - back],
                                                            scalar=sc, in1=hid[:, f, back:S], op0=ALU.mult, op1=ALU.add)
                            if back < 2:
                                link(ins_)
                            else:
                                ins_.then_inc(drained[4 + f], 1)
                    dve.wait_ge(*is_drained(stg, names[3], i))
                    dve.wait_ge(s["silu"], at(stg, "silu", n, i))
                    dve.wait_ge(s["uhi"], at(stg, "uhi", n - 1, i))
                    dve.wait_ge(s["ulo"], at(stg, "ulo", n - 1, i))
                    dve.tensor_tensor(u32[:, 0:W], u32[:, W:2 * W], hid[:, 2:4, :].rearrange("p a b -> p (a b)"),
                                      ALU.mult).then_inc(s["u"], 1)
                S_ = st[f"ffn_{tag}_head"]
                chain.enter(S_, 0)
                splits(S_, range(0, 4))
                convolve(S_, 0, A4, 0, 1)
                hidden_lo(S_, 0, 1, W)
                splits(S_, range(4, 8))
                convolve(S_, 0, B4, 1, 2)
                splits(S_, range(8, 10))
                hidden_lo(S_, 0, 2, W)
                chain.leave()
                S_ = st[f"ffn_{tag}_loop"]
                with trips(dve, S_) as i:
                    chain.enter(S_, i)
                    splits(S_, range(0, 4), i)
                    convolve(S_, i, A4, i * 2 + 2, 1)
                    splits(S_, range(4, 6), i)
                    hidden_lo(S_, i, 1, W)
                    splits(S_, range(6, 10), i)
                    convolve(S_, i, B4, i * 2 + 3, 2)
                    splits(S_, range(10, 12), i)
                    hidden_lo(S_, i, 2, W)
                    chain.leave()
                S_ = st[f"ffn_{tag}_tail"]
                chain.enter(S_, 0)
                splits(S_, range(0, 4))
                convolve(S_, 0, A4, U2 - 1, 1)
                splits(S_, range(4, 6))
                hidden_lo(S_, 0, 1, W)
                splits(S_, range(6, 8))
                chain.leave()
                add_rows(S_, [f"acc{b}" for b in range(4)])

            norm(st["norm_a"], col("g_a"), after_post("post_mlp"))
            S_ = st["half_a"]
            with trips(dve, S_) as i:
                chain.enter(S_, i)
                project_heads(S_, i, NG, 0)
                attention(S_, units_a(), i)
                chain.leave()
            turned(st["turn_a"], None)
            splits(st["out_a"], range(8))
            add_rows(st["out_a"], ("r0", "r1", "r2", "r3"))
            norm(st["norm_ffn_a"], col("g_fa"), after_sum("out_a", ("r1", "r3")))
            ffn("a")
            norm(st["norm_b"], col("g_b"), after_sum("ffn_a_tail", ("acc1", "acc3")))
            S_ = st["half_b"]
            with trips(dve, S_) as i:
                chain.enter(S_, i)
                project_heads(S_, i, 1, 1)
                attention(S_, units_b(), i)
                chain.leave()
            turned(st["turn_b"], None)
            splits(st["out_b"], range(8))
            add_rows(st["out_b"], ("r0", "r1", "r2", "r3"))
            norm(st["norm_ffn_b"], col("g_fb"), after_sum("out_b", ("r1", "r3")))
            ffn("b")


def lay_out(inputs):
    def feat(a):
        return np.asarray(a, np.float32).reshape(-1, P).T

    def twice(a):
        return np.concatenate([a, a], 0)
    unit = {n: np.asarray(v) for n, v in inputs.items()}
    gains = [unit["a_q_norm_2"][0], unit["a_k_norm_2"][0]]
    g = [gains[c][j] for j in range(NG) for c in range(2)] + [unit["b_q_norm_2"][0], unit["b_k_norm_2"][0]]
    rot = (np.arange(P) % HD < ROT).astype(np.float32)[:, None]

    def pad4(a):
        return np.concatenate([a.reshape(4, 1), np.zeros((P - 4, 1), np.float32)], 0)
    cols = {
        "g_mix": feat(unit["norm_mix_pre"]), "g_mlp": feat(unit["norm_mlp_pre"]),
        "g_a": feat(unit["attn_norm_2"][0]), "g_b": feat(unit["attn_norm_2"][1]),
        "g_fa": feat(unit["ffn_norm_2"][0]), "g_fb": feat(unit["ffn_norm_2"][1]),
        "g_heads": np.concatenate([feat(unit["diff_norm"])] * NH1 + [feat(unit["mlstm_norm"])], 1),
        "cw1": unit["conv_w"][0].reshape(CONV1, 4, P).transpose(2, 1, 0),
        "cb1": unit["conv_b"][0].reshape(4, P).T,
        "b_i": pad4(unit["b_igate"]), "b_f": pad4(unit["b_fgate"]),
        "gains": np.stack([twice(v) for v in g], 1),
        "rotated": rot, "unrotated": 1 - rot,
    }
    for layer, tag in enumerate("ab"):
        w = np.concatenate([unit["ffn_conv_w_2"][layer], unit["ffn_conv_b_2"][layer][None]], 0)
        w = w.reshape(4, 2, U2, 2, P)
        cols[f"cw2{tag}"] = w.transpose(4, 2, 1, 3, 0)
    rows = {
        "mix_post": unit["norm_mix_post"][0], "mlp_post": unit["norm_mlp_post"][0],
        "lambda": np.concatenate([unit[f"lambda_{n}"][0] for n in ("q1", "k1", "q2", "k2")]),
        "gain_rows": np.concatenate([v[:ROT] for v in g]),
    }
    packed, at_col = pack(cols)
    at_row, n = {}, 0
    for name, a in rows.items():
        at_row[name] = (n, a.size)
        n += a.size
    return packed, at_col, np.ascontiguousarray(np.concatenate(list(rows.values()))[None], dtype=np.float32), at_row


def kernel(**inputs):
    import concourse.bacc as _bacc
    from concourse.bass_utils import run_bass_kernel_spmd as _run

    nc = _bacc.Bacc("TRN2", target_bir_lowering=False, num_devices=1)
    consts, at_const = pack(constant_tables())
    cols, at_col, rows, at_row = lay_out(inputs)
    arrays = {"consts": consts, "cols": cols, "rows": rows}
    for name in ("x", "w_in", "w_out", "w_up", "w_down"):
        arrays[name] = np.ascontiguousarray(inputs[name])
    for name in ("a_w_qkv", "a_w_o", "b_w_qkv", "b_w_o", "ffn_w_up", "ffn_w_down"):
        arrays[name] = np.ascontiguousarray(inputs[name + "_2"])
    up = arrays["ffn_w_up"]
    arrays["ffn_w_up"] = np.ascontiguousarray(
        up.reshape(2, D, 2, U2, 256).transpose(0, 1, 3, 2, 4).reshape(2, D, 2 * FF2))
    args = {n: nc.dram_tensor(f"in_{n}", a.shape, mybir.dt.from_np(a.dtype), kind="ExternalInput").ap()
            for n, a in arrays.items()}
    out = nc.dram_tensor("out_0", (1, S, D), F32, kind="ExternalOutput").ap()
    blocks_kernel(nc, args, out, at_const, at_col, at_row)
    r = _run(nc, [{f"in_{n}": a for n, a in arrays.items()}], core_ids=[0])
    return r.results[0]["out_0"]
```

```python
from contextlib import ExitStack, contextmanager

import numpy as np

import concourse.bass as bass
import concourse.mybir as mybir

F32 = mybir.dt.float32
F32R = mybir.dt.float32r
ALU = mybir.AluOpType
ACT = mybir.ActivationFunctionType
AX = mybir.AxisListType

P = 128
S = 256
TOK = S // P
D = 1024
KT = D // P
HD = 64
SLOTS = 4
QW = 1024
EPS = 1e-6
BIG = 1e30
LAMBDA_INIT = 0.8 - 0.6 * 1.0

NH1 = 4
VD = 128
CONV1 = 4
FF1 = 4096
U1 = FF1 // 512
NH = 16
NG = 3
ROT = 16
FF2 = 2816
U2 = FF2 // 256
DILS = ((128, 1), (512, 4), (2048, 16))


def residue_order():
    t = np.arange(S)
    return (t % 4) * 64 + (t // 4 % 4) * 16 + t // 16


def constant_tables():
    c = {}
    c["ident"] = np.eye(P)
    pos = residue_order()
    token_at = np.argsort(pos)
    src = np.arange(P)
    perm_in = np.zeros((P, P))
    perm_in[src, (src % 4) * 32 + (src // 4 % 4) * 8 + src // 16] = 1
    perm_out = np.zeros((P, P))
    perm_out[src, (src % 16) * 8 + (src // 16 % 4) * 2 + src // 64] = 1
    c["perm_in"], c["perm_out"] = perm_in, perm_out
    mask_a = np.zeros((P, TOK, 512))
    for qt in range(TOK):
        tq = token_at[qt * P:(qt + 1) * P][:, None]
        own = token_at[qt * P:(qt + 1) * P][None, :]
        for g, ks in ((0, token_at[None, :]), (1, own), (2, own)):
            window, dil = DILS[g]
            ok = (tq >= ks) & (tq - ks <= window) & ((tq - ks) % dil == 0)
            col = (0, 256, 384)[g]
            mask_a[:, qt, col:col + ks.shape[1]] = np.where(ok, 0.0, BIG)
    c["mask_a"] = mask_a
    row, col = np.arange(P)[:, None], np.arange(P)[None, :]
    c["causal"] = np.concatenate([np.zeros((P, P)), np.where(row >= col, 0.0, BIG)], 1)
    c["causal_t"] = np.concatenate([np.where(col >= row, 0.0, BIG), np.zeros((P, P))], 1)

    def rope(theta, dim, tokens):
        inv = np.float32(theta) ** (-np.arange(0, dim, 2, dtype=np.float32) / np.float32(dim))
        ang = tokens.astype(np.float32)[:, None] * inv[None, :].astype(np.float32)
        both = np.stack([np.cos(ang), np.sin(ang)])
        return both.reshape(2, TOK, P, dim // 2).transpose(2, 0, 1, 3)
    c["rope1"] = rope(10000.0, HD, np.arange(S))
    for name, tokens in (("rope_a", token_at), ("rope_b", np.arange(S))):
        both = rope(500000.0, ROT, tokens).transpose(0, 2, 1, 3)
        cos, sin = both[:, :, 0], both[:, :, 1]
        c[name] = np.stack([cos, cos, sin, -sin], 2)
    sel = np.zeros((P, NH1, P))
    for h in range(NH1):
        sel[h, h, :] = 1
    c["sel"] = sel
    c["rotated"] = (np.arange(P) % HD < ROT).astype(np.float32)[:, None]
    return c


def pack(parts):
    where, cols, n = {}, [], 0
    for name, a in parts.items():
        flat = np.asarray(a).reshape(P, -1)
        where[name] = (n, flat.shape[1])
        cols.append(flat)
        n += flat.shape[1]
    return np.ascontiguousarray(np.concatenate(cols, 1), dtype=np.float32), where


class Stage:

    def __init__(self, name, trips=1, uses=(), quarters=(), counts=None):
        self.name, self.trips, self.uses, self.quarters = name, trips, list(uses), list(quarters)
        self.counts = dict(counts or {})
        assert trips == 1 or len(self.quarters) % SLOTS == 0


class Plan:

    def __init__(self, stages):
        self.stage, tally, self.nq = {}, {}, 0
        for s in stages:
            s.base = dict(tally)
            s.q0 = self.nq
            per = dict(s.counts)
            s.use = {}
            for name, bank in s.uses:
                s.use[name] = (bank, per.get(("bank", bank), 0))
                per[("bank", bank)] = per.get(("bank", bank), 0) + 1
            s.released = []
            for n, by in enumerate(s.quarters):
                slot = (s.q0 + n) % SLOTS
                if by is None:
                    per[("used", slot)] = per.get(("used", slot), 0) + 1
                    s.released.append((("used", slot), per[("used", slot)]))
                else:
                    s.released.append(by)
            s.per = per
            for k, v in per.items():
                tally[k] = tally.get(k, 0) + v * s.trips
            self.nq += len(s.quarters) * s.trips
            self.stage[s.name] = s
        self.total = tally

    def at(self, s, key, k, i=0):
        per = s.per.get(key, 0) if s.trips > 1 else 0
        v = s.base.get(key, 0) + k
        return v if per == 0 else i * per + v

    def filled(self, s, name, i=0):
        bank, n = s.use[name]
        return self.at(s, ("bank", bank), n + 1, i)

    def free(self, s, name, i=0):
        bank, n = s.use[name]
        return self.at(s, ("bank", bank), n, i)

    def slot(self, s, n):
        return (s.q0 + n) % SLOTS

    def turn(self, s, n, i=0, ahead=0):
        v = (s.q0 + n + ahead) // SLOTS
        return v if s.trips == 1 else i * (len(s.quarters) // SLOTS) + v


def up_names(tag):
    return [(f"{tag}{f}", 4 + f) for f in range(4)]


def norm_stage(name, first_bank=0, **more):
    return Stage(name, uses=[(f"t{k}", (first_bank + k) % 8) for k in range(8)],
                 counts={"hiT": 8, "mh": 4, "ms": 2, "rstd": 2, "xn": 4, "ln_norm": 2, **more})


def turn_stage(name, **more):
    return Stage(name, uses=[(f"t{k}", k) for k in range(8)], counts={"hiT": 8, **more})


def row_out_quarters():
    return [None] * 3 + ["r2"] + [None] * 3 + ["r3"]


def row_out_uses():
    return [("r0", 0), ("r2", 2), ("r1", 1), ("r3", 3)]


def attention_uses(n):
    out = []
    for u in range(n):
        out += [(f"s{u}", u % 2), (f"p{u}", 2 + u % 2), (f"o{u}", 4 + u % 2)]
    return out


def make_plan():
    in1 = Stage(
        "in1",
        uses=[("dq0", 0), ("dq1", 1), ("gate_t", 7), ("dk0", 2), ("dk1", 3)]
        + [("mqk0", 4), ("mqk1", 5), ("mqk2", 6), ("mqk3", 7)]
        + [("dv0", 0), ("dv1", 1), ("gate_m", 4), ("qt0", 6), ("qt1", 7), ("mv0", 2), ("mv1", 3)]
        + [("kt0", 6), ("kt1", 7)],
        quarters=[None] * 3 + ["dq1"] + [None] * 3 + ["dk1"] + [None] * 3 + ["mqk3"]
        + [None] * 3 + ["dv1"] + [None] * 3 + ["mv1"],
        counts={"gates": 5, "lnf": 2, "gate_w": 2, "rot": 4, "cv": 4, "ecv": 1, "mqk": 2, "dve_step": 12, "act_step": 2})
    uses = [("mo0", 4), ("mo1", 5)]
    for u in range(2 * NH1):
        uses += [(f"s{u}", u % 2), (f"p{u}", 2), (f"o{u}", 3)]
    for h in range(NH1):
        uses += [(f"m{h}", 6), (f"ls{h}", 7)] + ([(f"lo{h - 1}", 6)] if h else [])
    mix = Stage("mix", uses=uses + [(f"lo{NH1 - 1}", 6)], quarters=[None] * 3 + ["mo1"],
                counts={"prob": 8, "pd": 8, "oms": 12, "wm": 4, "gated": 4, "orstd": 1, "osq": 3,
                        "dve_step": 24 + 16, "sig": 2, "act_step": 1 + 2})

    proj_a = []
    q_a = []
    for g in range(NG):
        proj_a += [(f"q{g}0", 0), (f"q{g}1", 1), (f"k{g}0", 2), (f"k{g}1", 3)]
        proj_a += [(f"qt{g}0", 6), (f"qt{g}1", 7), (f"v{g}0", 4), (f"v{g}1", 5), (f"kt{g}0", 6), (f"kt{g}1", 7)]
        q_a += [None] * 3 + [f"q{g}1"] + [None] * 3 + [f"k{g}1"] + [None] * 3 + [f"v{g}1"]
    half_a = Stage("half_a", trips=2, uses=proj_a + attention_uses(16), quarters=q_a,
                   counts={"sq": 12, "ms8": 12, "rs8": 12, "rot": 12, "act_step": 12, "prob": 16, "dve_step": 12 + 16})
    proj_b = [("q00", 0), ("q01", 1), ("k00", 2), ("k01", 3), ("qt00", 6), ("qt01", 7),
              ("v00", 4), ("v01", 5), ("kt00", 6), ("kt01", 7)]
    half_b = Stage("half_b", trips=2, uses=proj_b + attention_uses(8),
                   quarters=[None] * 3 + ["q01"] + [None] * 3 + ["k01"] + [None] * 3 + ["v01"],
                   counts={"sq": 4, "ms8": 4, "rs8": 4, "rot": 4, "act_step": 4, "prob": 8, "dve_step": 4 + 8})
    acc = [(f"acc{b}", b) for b in range(4)]

    def ffn(tag):
        up = {"cv": 4, "silu": 1, "u": 1, "uhi": 1, "ulo": 1, "dve_step": 4}
        return [
            Stage(f"ffn_{tag}_head", uses=up_names("a") + up_names("b"),
                  quarters=[None] * 3 + ["a3"] + [None] * 3 + ["b3"] + [None] * 2,
                  counts={k: 2 * v for k, v in up.items()}),
            Stage(f"ffn_{tag}_loop", trips=(U2 - 3) // 2, uses=up_names("a") + up_names("b"),
                  quarters=[None] * 3 + ["a3"] + [None] * 5 + ["b3"] + [None] * 2,
                  counts={k: 2 * v for k, v in up.items()}),
            Stage(f"ffn_{tag}_tail", uses=up_names("a") + acc,
                  quarters=[None] * 3 + ["a3"] + [None] * 3 + ["acc3"], counts=up),
        ]
    mlp_up = {"u": 1, "uhi": 1, "ulo": 1}
    stages = [
        Stage("load", counts={"dve_step": 5}),
        norm_stage("norm_in1"), in1, mix,
        turn_stage("turn_mix"),
        Stage("out1", uses=row_out_uses(), quarters=row_out_quarters()),
        Stage("post_mix", counts={"msq": 4, "pms": 2, "prstd": 2, "ln_post": 2, "x_new": 4}),
        norm_stage("norm_mlp", 4),
        Stage("mlp_head", uses=up_names("a") + up_names("b"),
              quarters=[None] * 3 + ["a3"] + [None] * 3 + ["b3"] + [None] * 4, counts={k: 2 * v for k, v in mlp_up.items()}),
        Stage("mlp_loop", trips=U1 - 2, uses=up_names("a"), quarters=[None] * 3 + ["a3"] + [None] * 4, counts=mlp_up),
        Stage("mlp_tail", uses=acc, quarters=[None] * 3 + ["acc3"]),
        Stage("post_mlp", counts={"msq": 4, "pms": 2, "prstd": 2, "ln_post": 2, "x_new": 4}),
        norm_stage("norm_a"), half_a,
        turn_stage("turn_a"),
        Stage("out_a", uses=row_out_uses(), quarters=row_out_quarters()),
        norm_stage("norm_ffn_a", 4), *ffn("a"),
        norm_stage("norm_b"), half_b,
        turn_stage("turn_b"),
        Stage("out_b", uses=row_out_uses(), quarters=row_out_quarters()),
        norm_stage("norm_ffn_b", 4), *ffn("b"),
    ]
    return Plan(stages)


def rope_view(ap, heads, halves, dim):
    return ap.rearrange("p (h s d) -> p h s d", h=heads, s=halves, d=dim)


def blocks_kernel(nc, ins, out, at_const, at_col, at_row):
    plan = make_plan()
    st = plan.stage
    at, filled, free = plan.at, plan.filled, plan.free
    with ExitStack() as ctx:
        def sb(name, shape, dt=F32):
            return ctx.enter_context(nc.sbuf_tensor(name, shape, dt))

        def sem(name):
            return ctx.enter_context(nc.semaphore(name))

        ps = ctx.enter_context(nc.psum_tensor("ps", [P, 8, 512], F32))
        w_in = sb("w_stage", [P, SLOTS, QW])
        w_hi = sb("w_hi", [P, SLOTS, QW], F32R)
        w_lo = sb("w_lo", [P, SLOTS, QW], F32R)
        x = sb("x", [P, TOK, D])
        xn = sb("xn", [P, TOK, D])
        o_sb = sb("o_sb", [P, TOK, D])
        aT_hi = sb("aT_hi", [P, KT, S], F32R)
        aT_lo = sb("aT_lo", [P, KT, S], F32R)
        u32 = sb("u32", [P, 4 * S])
        u_hi = sb("u_hi", [P, 4 * S], F32R)
        u_lo = sb("u_lo", [P, 4 * S], F32R)
        hid = sb("hid", [P, 4, S])
        qz = sb("qz", [P, 12, 2, S])
        kT = sb("kT", [P, 12, S])
        vv = sb("vv", [P, TOK, 1536])
        sm = sb("sm", [P, 2, 512])
        prob = sb("prob", [P, 3, 512])
        pdf = sb("pdf", [P, 3, S])
        pts = sb("pts", [P, 2, 512])
        xq = sb("xq", [P, TOK, 512])
        sqb = sb("sqb", [P, TOK, 512])
        rt = sb("rt", [P, 2, P])
        consts = sb("consts", [P, sum(n for _, n in at_const.values())])
        cols = sb("cols", [P, sum(n for _, n in at_col.values())])
        rows = sb("rows", [P, sum(n for _, n in at_row.values())])
        small = sb("small", [P, 256])
        gt_in = sb("gt_in", [P, KT * 8])
        gt_hi = sb("gt_hi", [P, KT * 8], F32R)
        gt_lo = sb("gt_lo", [P, KT * 8], F32R)
        gi = sb("gi", [4, S])
        atok = sb("atok", [P, 2, TOK, 4])
        tabs = sb("tabs", [P, 8, TOK, 2, ROT])
        gq = sb("gq", [P, 8])

        def const(name, *shape):
            a, n = at_const[name]
            v = consts[:, a:a + n]
            return v.rearrange(*shape[:1], **shape[1]) if shape else v

        def col(name, j=None, n=1):
            a, w = at_col[name]
            return cols[:, a:a + w] if j is None else cols[:, a + j:a + j + n]

        def row(name):
            a, n = at_row[name]
            return rows[:, a:a + n]
        ident = const("ident")
        gm = xn[0:4, :, :].rearrange("p t (r s) -> p (t r) s", s=S)
        cell = {}

        def stat(name, n=1):
            if name not in cell:
                cell[name] = (sum(m for _, m in cell.values()), n)
            a, m = cell[name]
            return small[:, a:a + m]

        mqkT = kT[:, 4:8, :]

        turned_keys = prob
        lsm = hid[:].rearrange("p (a b) s -> p a (b s)", a=2)
        wmat = u32[:].rearrange("p (a s) -> p a s", a=2)

        def vm(tok):
            return vv[:, tok, 512:512 + 4 * 132].rearrange("p (h c) -> p h c", c=132)

        full = [sem(f"full{b}") for b in range(8)]
        drained = [sem(f"drained{b}") for b in range(8)]
        loaded = [sem(f"loaded{q}") for q in range(SLOTS)]
        hi_done = [sem(f"hi_done{q}") for q in range(SLOTS)]
        lo_done = [sem(f"lo_done{q}") for q in range(SLOTS)]
        used = [sem(f"used{q}") for q in range(SLOTS)]
        s = {n: sem(n) for n in (
            "x_in0", "x_in1", "ident_in", "cols_in", "const_in", "gate_in", "stored", "ln_norm", "ln_post", "hiT", "mh", "ms", "rstd", "xn", "act_step", "dve_step",
            "gates", "lnf", "rot", "cv", "ecv", "mqk", "sig", "gated", "prob", "pd", "oms", "wm",
            "orstd", "osq", "sq", "ms8", "rs8", "silu", "u", "uhi", "ulo", "msq", "pms", "prstd", "x_new",
            "lam", "const_ready", "gate_w", "unit")}

        def is_full(stg, name, i=0):
            return full[stg.use[name][0]], filled(stg, name, i)

        def is_drained(stg, name, i=0):
            return drained[stg.use[name][0]], filled(stg, name, i)

        def is_free(stg, name, i=0):
            return drained[stg.use[name][0]], free(stg, name, i)

        def bank(stg, name):
            return stg.use[name][0]

        def was_read(stg, n, i):
            by = stg.released[n]
            if isinstance(by, str):
                return is_full(stg, by, i)
            return used[by[0][1]], at(stg, by[0], by[1], i)

        def after_post(name):
            return [[(s["x_new"], at(st[name], "x_new", 2 * t + h + 1)) for h in range(2)] for t in range(TOK)]

        def after_sum(name, rows_):
            return [[is_drained(st[name], f"{rows_}{2 * t + h}") for h in range(2)] for t in range(TOK)]

        OUT_SPLITS = ((4,), (), (5,), (), (6, 7))
        MLP_SPLITS = ((), (), (0,), (1,), (2, 3))
        FFN_SPLITS = ((), (), (), (), (6, 7))

        @contextmanager
        def trips(eng, stg):
            if stg.trips == 1:
                yield 0
            else:
                with eng.Fori(0, stg.trips) as i:
                    yield i

        class Chain:

            def __init__(self, eng, key):
                self.eng, self.key, self.n = eng, key, 0

            def enter(self, stg, i, done=0):
                self.stg, self.i, self.n = stg, i, done

            def link(self, ins):
                self.n += 1
                ins.then_inc(s[self.key], 1)
                self.eng.wait_ge(s[self.key], at(self.stg, self.key, self.n, self.i))

            def leave(self):
                want = self.stg.per.get(self.key, 0)
                assert self.n == want, f"{self.stg.name} {self.key}: {self.n} increments, {want} in the plan"

        block = ctx.enter_context(nc.Block())

        @block.sync
        def _(sp):
            for t in range(TOK):
                sp.dma_start(x[:, t, :], ins["x"][0, t * P:(t + 1) * P, :]).then_inc(s[f"x_in{t}"], 16)
            sp.dma_start(consts[:, 0:P], ins["consts"][:, 0:P]).then_inc(s["ident_in"], 16)
            sp.dma_start(cols[:], ins["cols"]).then_inc(s["cols_in"], 16)

            def k_rows(w):
                return w.rearrange("(k p) n -> p k n", p=P)

            def load_cols(stg, i, n0, w, c0):
                for q in range(4):
                    sl = slice(c0, c0 + 512) if isinstance(c0, int) else bass.ds(c0, 512)
                    slot = plan.slot(stg, n0 + q)
                    if stg.q0 + n0 + q >= SLOTS:
                        sp.wait_ge(lo_done[slot], plan.turn(stg, n0 + q, i))
                    sp.dma_start(w_in[:, slot, :].rearrange("p (k n) -> p k n", k=2),
                                 k_rows(w)[:, 2 * q:2 * q + 2, sl]).then_inc(loaded[slot], 16)

            def load_pair(stg, i, n0, w, j):
                load_cols(stg, i, n0, w, j * 512)

            def load_rows(stg, i, n0, nq, w, t0):
                for q in range(nq):
                    slot = plan.slot(stg, n0 + q)
                    if stg.q0 + n0 + q >= SLOTS:
                        sp.wait_ge(lo_done[slot], plan.turn(stg, n0 + q, i))
                    r0 = (t0 + q) * P
                    sl = slice(r0, r0 + P) if isinstance(r0, int) else bass.ds(r0, P)
                    sp.dma_start(w_in[:, slot, :], w[sl, :]).then_inc(loaded[slot], 16)

            S_ = st["in1"]
            w = ins["w_in"][0]
            for n, c0 in enumerate((0, 512, 1536, 1024, 2048)):
                load_cols(S_, 0, 4 * n, w, c0)
                if n == 0:
                    sp.dma_start(gt_in[:].rearrange("p (k n) -> p k n", k=KT),
                                 k_rows(w)[:, :, 3072:3080]).then_inc(s["gate_in"], 16)
                    sp.dma_start(consts[:, P:], ins["consts"][:, P:]).then_inc(s["const_in"], 16)
                    sp.dma_start(rows[:], ins["rows"].partition_broadcast(P)).then_inc(s["const_in"], 16)
            load_cols(st["mix"], 0, 0, w, 2560)
            for n in range(2):
                load_cols(st["out1"], 0, 4 * n, ins["w_out"][0], 512 * n)
            up, down = ins["w_up"][0], ins["w_down"][0]
            S_ = st["mlp_head"]
            load_cols(S_, 0, 0, up, 0)
            load_cols(S_, 0, 4, up, 512)
            load_rows(S_, 0, 8, 4, down, 0)
            S_ = st["mlp_loop"]
            with trips(sp, S_) as i:
                load_cols(S_, i, 0, up, i * 512 + 1024)
                load_rows(S_, i, 4, 4, down, i * 4 + 4)
            load_rows(st["mlp_tail"], 0, 0, 4, down, 4 * (U1 - 1))

            def attention_weights(S_, w, groups):
                with trips(sp, S_) as i:
                    for g in range(groups):
                        for kind in range(3):
                            load_cols(S_, i, (g * 3 + kind) * 4, w, i * 512 + (kind * groups + g) * D)

            def ffn_weights(tag, layer):
                up, down = ins["ffn_w_up"][layer], ins["ffn_w_down"][layer]
                S_ = st[f"ffn_{tag}_head"]
                load_pair(S_, 0, 0, up, 0)
                load_pair(S_, 0, 4, up, 1)
                load_rows(S_, 0, 8, 2, down, 0)
                S_ = st[f"ffn_{tag}_loop"]
                with trips(sp, S_) as i:
                    load_pair(S_, i, 0, up, i * 2 + 2)
                    load_rows(S_, i, 4, 2, down, i * 4 + 2)
                    load_pair(S_, i, 6, up, i * 2 + 3)
                    load_rows(S_, i, 10, 2, down, i * 4 + 4)
                S_ = st[f"ffn_{tag}_tail"]
                load_pair(S_, 0, 0, up, U2 - 1)
                load_rows(S_, 0, 4, 4, down, 2 * (U2 - 2))

            attention_weights(st["half_a"], ins["a_w_qkv"][0], NG)
            for n in range(2):
                load_cols(st["out_a"], 0, 4 * n, ins["a_w_o"][0], 512 * n)
            ffn_weights("a", 0)
            attention_weights(st["half_b"], ins["b_w_qkv"][0], 1)
            for n in range(2):
                load_cols(st["out_b"], 0, 4 * n, ins["b_w_o"][0], 512 * n)
            ffn_weights("b", 1)
            for b, (t, h) in enumerate(((0, 0), (0, 1), (1, 0), (1, 1))):
                sp.wait_ge(*is_drained(st["ffn_b_tail"], f"acc{2 * t + h}"))
                sp.dma_start(out[0, t * P:(t + 1) * P, h * 512:(h + 1) * 512],
                             x[:, t, h * 512:(h + 1) * 512]).then_inc(s["stored"], 16)
            sp.wait_ge(s["stored"], 64)

        def units_a():
            mask = const("mask_a", "p (t c) -> p t c", dict(t=TOK))
            for pr in range(4):
                for h in range(2):
                    for qt in range(TOK):
                        q = [qz[:, g * 4 + pr, h, qt * P:(qt + 1) * P] for g in range(NG)]
                        own = slice(qt * P, (qt + 1) * P)
                        yield dict(
                            tok=qt,
                            scores=[(0, 256, q[0], kT[:, pr, :]), (256, 128, q[1], kT[:, 4 + pr, own]),
                                    (384, 128, q[2], kT[:, 8 + pr, own])],
                            segments=[(0, 512, mask[:, qt, :])],
                            tiles=4,
                            values=[(0, [(0, vv[:, 0, pr * P:(pr + 1) * P]), (1, vv[:, 1, pr * P:(pr + 1) * P]),
                                         (2, vv[:, qt, 512 + pr * P:512 + (pr + 1) * P]),
                                         (3, vv[:, qt, 1024 + pr * P:1024 + (pr + 1) * P])])],
                            outs=[(0, h * HD, pr * P + h * HD)])

        def units_pair(heads, kof, vof):
            mask = const("causal")
            for pr in range(heads):
                for qt in range(TOK):
                    W = (qt + 1) * P
                    yield dict(
                        tok=qt, head=pr,
                        scores=[(c * W, W, qz[:, pr, c, qt * P:(qt + 1) * P], kof(pr)[:, 0:W]) for c in range(2)],
                        segments=[(c * W, W, mask[:, 2 * P - W:2 * P]) for c in range(2)],
                        tiles=2 * (qt + 1),
                        values=[(c * P, [(c * (qt + 1) + t, vof(t, pr)) for t in range(qt + 1)]) for c in range(2)],
                        outs=[(c, c * P + c * HD, pr * P + c * HD) for c in range(2)])

        def units_diff():
            for u in units_pair(NH1, lambda h: kT[:, h, :], lambda t, h: vv[:, t, h * P:(h + 1) * P]):
                u["tiles"] = u["tok"] + 1
                u["values"] = u["values"][:1]
                yield u

        def units_b():
            return units_pair(4, lambda p_: kT[:, p_, :], lambda t, p_: vv[:, t, p_ * P:(p_ + 1) * P])

        MO_TILES = ((0, 1, 2), (3,), (4,), (5,), (6,), (7,))
        MO_STEPS = tuple(u for q in range(4) for u, tiles in enumerate(MO_TILES) if 2 * q + 1 in tiles)

        def oms_at_head(g):
            return 3 * g + 1

        @block.tensor
        def _(pe):
            def await_weights(stg, n, i):
                slot = plan.slot(stg, n)
                pe.wait_ge(lo_done[slot], plan.turn(stg, n, i) + 1)
                return slot

            def signal(stg, n, ins_):
                by = stg.released[n]
                if not isinstance(by, str):
                    ins_.then_inc(used[by[0][1]], 1)

            def dense_rows(stg, i, n0, names, turned=None, tiles=range(KT)):
                for k in tiles:
                    q, kk = divmod(k, 2)
                    slot = await_weights(stg, n0 + q, i)
                    if turned:
                        pe.wait_ge(*is_drained(st[turned], f"t{k}"))
                    wh, wl = (w[:, slot, kk * 512:(kk + 1) * 512] for w in (w_hi, w_lo))
                    for t in range(TOK):
                        o = ps[:, bank(stg, names[t]), :]
                        if k == 0:
                            pe.wait_ge(*is_free(stg, names[t], i))
                        ah, al = (a[:, k, t * P:(t + 1) * P] for a in (aT_hi, aT_lo))
                        pe.matmul(o, ah, wh, start=(k == 0), stop=False)
                        pe.matmul(o, ah, wl, start=False, stop=False)
                        last = pe.matmul(o, al, wh, start=False, stop=(k == KT - 1))
                        if k == KT - 1:
                            last.then_inc(full[bank(stg, names[t])], 1)
                    if kk == 1 and q < 3:
                        signal(stg, n0 + q, last)

            def dense_cols(stg, i, n0, names, turned=None):
                for q in range(4):
                    slot = await_weights(stg, n0 + q, i)
                    for kk in range(2):
                        k = 2 * q + kk
                        if turned:
                            pe.wait_ge(*is_drained(st[turned], f"t{k}"))
                        for f in range(4):
                            c0 = kk * 512 + f * P
                            wh, wl = (w[:, slot, c0:c0 + P] for w in (w_hi, w_lo))
                            o = ps[:, bank(stg, names[f]), 0:S]
                            if k == 0:
                                pe.wait_ge(*is_free(stg, names[f], i))
                            pe.matmul(o, wh, aT_hi[:, k, :], start=(k == 0), stop=False)
                            pe.matmul(o, wh, aT_lo[:, k, :], start=False, stop=False)
                            last = pe.matmul(o, wl, aT_hi[:, k, :], start=False, stop=(k == KT - 1))
                            if k == KT - 1:
                                last.then_inc(full[bank(stg, names[f])], 1)
                    if q < 3:
                        signal(stg, n0 + q, last)

            def last_rows(stg, n0, names):
                for t in range(TOK):
                    b = bank(stg, names[t])
                    o = ps[:, b, :]
                    for k in range(KT):
                        q, kk = divmod(k, 2)
                        slot = await_weights(stg, n0 + q, 0)
                        if k == 0:
                            pe.wait_ge(*is_free(stg, names[t]))
                        wh, wl = (w[:, slot, kk * 512:(kk + 1) * 512] for w in (w_hi, w_lo))
                        ah, al = (a[:, k, t * P:(t + 1) * P] for a in (aT_hi, aT_lo))
                        pe.matmul(o, ah, wh, start=(k == 0), stop=False)
                        pe.matmul(o, ah, wl, start=False, stop=False)
                        last = pe.matmul(o, al, wh, start=False, stop=(k == KT - 1))
                        if k == KT - 1:
                            last.then_inc(full[b], 1)
                        elif t == TOK - 1 and kk == 1:
                            signal(stg, n0 + q, last)

            def last_down(stg, n0, tiles):
                for t in range(TOK):
                    for h in range(2):
                        for f in tiles:
                            slot = await_weights(stg, n0 + f, 0)
                            ah, al = (u[:, f * S + t * P:f * S + (t + 1) * P] for u in (u_hi, u_lo))
                            wh, wl = (w[:, slot, h * 512:(h + 1) * 512] for w in (w_hi, w_lo))
                            o = ps[:, 2 * t + h, :]
                            end = f == tiles[-1]
                            pe.matmul(o, ah, wh, start=False, stop=False)
                            pe.matmul(o, ah, wl, start=False, stop=False)
                            last = pe.matmul(o, al, wh, start=False, stop=end)
                            if end:
                                last.then_inc(full[2 * t + h], 1)
                            elif t == TOK - 1 and h == 1:
                                signal(stg, n0 + f, last)

            def down(stg, i, n0, tiles, first=False):
                for f in tiles:
                    slot = await_weights(stg, n0 + f, i)
                    for t in range(TOK):
                        ah, al = (u[:, f * S + t * P:f * S + (t + 1) * P] for u in (u_hi, u_lo))
                        for h in range(2):
                            wh, wl = (w[:, slot, h * 512:(h + 1) * 512] for w in (w_hi, w_lo))
                            o = ps[:, 2 * t + h, :]
                            pe.matmul(o, ah, wh, start=(first and f == tiles[0]), stop=False)
                            pe.matmul(o, ah, wl, start=False, stop=False)
                            last = pe.matmul(o, al, wh, start=False, stop=False)
                    signal(stg, n0 + f, last)

            def turn(stg, src, order, ready=None):
                for t in range(TOK):
                    if ready:
                        pe.wait_ge(*ready[t])
                    for k in range(KT):
                        if t == 0 and stg is not st["norm_in1"]:
                            pe.wait_ge(*is_free(stg, f"t{k}"))
                        b = bank(stg, f"t{k}")
                        o = ps[:, b, 0:S]
                        if order is None:
                            m, o = ident, o[:, t * P:(t + 1) * P]
                        elif order == "in":
                            m = const("perm_in")
                            o = o.rearrange("p (r t c) -> p r t c", t=TOK, c=8)[:, :, t, :]
                        else:
                            m = const("perm_out")
                            o = o.rearrange("p (r t c) -> p r t c", t=TOK, c=2)[:, :, t, :]
                        last = pe.transpose(o, src[:, t, k * P:(k + 1) * P], m)
                        if t == TOK - 1:
                            last.then_inc(full[b], 1)

            def norm(stg, order=None):
                turn(stg, xn, order, [(s["xn"], at(stg, "xn", 2 * t + 2)) for t in range(TOK)])

            def attention(stg, units, i, probs, ready, last_values):
                units = list(units)
                n = len(units)
                for u in range(n + 2):
                    if u < n:
                        un = units[u]
                        b = bank(stg, f"s{u}")
                        pe.wait_ge(*is_free(stg, f"s{u}", i))
                        for c, W, q, k in un["scores"]:
                            last = pe.matmul(ps[:, b, c:c + W], q, k, start=True, stop=True)
                        last.then_inc(full[b], 1)
                    if 1 <= u <= n:
                        v = u - 1
                        b = bank(stg, f"p{v}")
                        pe.wait_ge(*is_free(stg, f"p{v}", i))
                        pe.wait_ge(s[ready], at(stg, ready, v + 1, i))
                        for t in range(units[v]["tiles"]):
                            last = pe.transpose(ps[:, b, t * P:(t + 1) * P], probs[:, v % 2, t * P:(t + 1) * P], ident)
                        last.then_inc(full[b], 1)
                    if u >= 2:
                        v = u - 2
                        b = bank(stg, f"o{v}")
                        pe.wait_ge(*is_free(stg, f"o{v}", i))
                        pe.wait_ge(*is_drained(stg, f"p{v}", i))
                        if v == 0:
                            for nm in last_values:
                                pe.wait_ge(*is_drained(stg, nm, i))
                        for c, pairs in units[v]["values"]:
                            for j, (t, val) in enumerate(pairs):
                                last = pe.matmul(ps[:, b, c:c + P], pts[:, v % 2, t * P:(t + 1) * P], val,
                                                 start=(j == 0), stop=(j == len(pairs) - 1))
                        last.then_inc(full[b], 1)

            def turn_heads(stg, names, i, n_rot, src=xq):
                pe.wait_ge(s["rot"], at(stg, "rot", n_rot, i))
                for h in range(2):
                    b = bank(stg, names[h])
                    pe.wait_ge(*is_free(stg, names[h], i))
                    for j in range(2):
                        for t in range(TOK):
                            last = pe.transpose(ps[:, b, j * S + t * P:j * S + (t + 1) * P],
                                                src[:, t, (2 * h + j) * P:(2 * h + j + 1) * P], ident)
                    last.then_inc(full[b], 1)

            pe.wait_ge(s["ident_in"], 16)
            norm(st["norm_in1"])
            S_ = st["in1"]
            dense_rows(S_, 0, 0, ("dq0", "dq1"), "norm_in1")
            pe.wait_ge(s["gate_w"], at(S_, "gate_w", 2))
            pe.wait_ge(*is_free(S_, "gate_t"))
            for gi in range(2):
                o = ps[0:4, 7, gi * S:(gi + 1) * S]
                for k in range(KT):
                    gh, gl = (g_[:, k * 8 + 4 * gi:k * 8 + 4 * gi + 4] for g_ in (gt_hi, gt_lo))
                    pe.matmul(o, gh, aT_hi[:, k, :], start=(k == 0), stop=False)
                    pe.matmul(o, gh, aT_lo[:, k, :], start=False, stop=False)
                    last = pe.matmul(o, gl, aT_hi[:, k, :], start=False, stop=(k == KT - 1))
            last.then_inc(full[7], 1)
            dense_rows(S_, 0, 4, ("dk0", "dk1"))
            dense_cols(S_, 0, 8, ("mqk0", "mqk1", "mqk2", "mqk3"))
            dense_rows(S_, 0, 12, ("dv0", "dv1"))
            pe.wait_ge(s["gates"], at(S_, "gates", 5))
            pe.wait_ge(*is_free(S_, "gate_m"))
            for j, r in enumerate((5, 7)):
                for t in range(TOK):
                    last = pe.transpose(ps[:, 4, (j * 2 + t) * 4:(j * 2 + t) * 4 + 4],
                                        gm[0:4, r, t * P:(t + 1) * P], ident[0:4, 0:4])
            last.then_inc(full[4], 1)
            turn_heads(S_, ("qt0", "qt1"), 0, 2)
            dense_rows(S_, 0, 16, ("mv0", "mv1"))
            turn_heads(S_, ("kt0", "kt1"), 0, 4, turned_keys)

            S_ = st["mix"]
            units = list(units_diff())
            n = len(units)
            sel = const("sel", "p (h c) -> p h c", dict(h=NH1))
            for u in range(n + 3):
                if u == 0:
                    dense_rows(S_, 0, 0, ("mo0", "mo1"), tiles=MO_TILES[0])
                    for nm in ("qt0", "qt1", "kt0", "kt1", "dv0", "dv1"):
                        pe.wait_ge(*is_drained(st["in1"], nm))
                if u < n:
                    b = bank(S_, f"s{u}")
                    pe.wait_ge(*is_free(S_, f"s{u}"))
                    for c, W, q, k in units[u]["scores"]:
                        last = pe.matmul(ps[:, b, c:c + W], q, k, start=True, stop=True)
                    last.then_inc(full[b], 1)
                if u == 0:
                    pe.wait_ge(s["const_ready"], 2)
                    pe.wait_ge(s["mqk"], at(st["in1"], "mqk", 2))
                    for nm in ("mv0", "mv1"):
                        pe.wait_ge(*is_drained(st["in1"], nm))
                h, odd = divmod(u, 2)
                if h < NH1 and not odd:
                    pe.wait_ge(*is_free(S_, f"m{h}"))
                    pe.matmul(ps[:, 6, 0:S], sel[0:4, h, :], gm[0:4, 6, :], start=True, stop=True).then_inc(full[6], 1)
                    r0 = (h % 2) * HD
                    pe.wait_ge(*is_free(S_, f"ls{h}"))
                    kk, qq = mqkT[r0:r0 + HD, 2 + h // 2, :], mqkT[r0:r0 + HD, h // 2, :]
                    pe.matmul(ps[:, 7, 0:S], kk[:, 0:P], qq, start=True, stop=True)
                    pe.matmul(ps[:, 7, S:S + P], kk[:, P:S], qq[:, P:S], start=True, stop=True).then_inc(full[7], 1)
                if 1 <= u < len(MO_TILES):
                    dense_rows(S_, 0, 0, ("mo0", "mo1"), tiles=MO_TILES[u])
                if 2 <= u < n + 2:
                    v = u - 2
                    pe.wait_ge(*is_free(S_, f"p{v}"))
                    pe.wait_ge(s["pd"], at(S_, "pd", v + 1))
                    for t in range(units[v]["tiles"]):
                        last = pe.transpose(ps[:, 2, t * P:(t + 1) * P], pdf[:, v % 3, t * P:(t + 1) * P], ident)
                    last.then_inc(full[2], 1)
                if u >= 3:
                    v = u - 3
                    pe.wait_ge(*is_free(S_, f"o{v}"))
                    pe.wait_ge(*is_drained(S_, f"p{v}"))
                    for c, pairs in units[v]["values"]:
                        for j, (t, val) in enumerate(pairs):
                            last = pe.matmul(ps[:, 3, c:c + P], pts[:, v % 2, t * P:(t + 1) * P], val,
                                             start=(j == 0), stop=(j == len(pairs) - 1))
                    last.then_inc(full[3], 1)
                if h >= 1 and not odd and h <= NH1:
                    g = h - 1
                    pe.wait_ge(*is_free(S_, f"lo{g}"))
                    pe.wait_ge(*is_drained(S_, f"ls{g}"))
                    w = lsm[:, g % 2, :]
                    pe.matmul(ps[:, 6, 0:129], w[:, 0:P], vm(0)[:, g, 0:129], start=True, stop=True)
                    pe.matmul(ps[:, 6, 256:385], w[:, P:2 * P], vm(0)[:, g, 0:129], start=True, stop=False)
                    pe.matmul(ps[:, 6, 256:385], w[:, 2 * P:3 * P], vm(1)[:, g, 0:129],
                              start=False, stop=True).then_inc(full[6], 1)

            pe.wait_ge(s["osq"], at(S_, "osq", 3))
            turn(st["turn_mix"], o_sb, None)

            def project_out(name, turned):
                stg = st[name]
                dense_rows(stg, 0, 0, ("r0", "r2"), turned)
                last_rows(stg, 4, ("r1", "r3"))
            project_out("out1", "turn_mix")

            norm(st["norm_mlp"])
            def await_hidden(stg, n, i):
                pe.wait_ge(s["ulo"], at(stg, "ulo", n, i))

            A4, B4 = [f"a{f}" for f in range(4)], [f"b{f}" for f in range(4)]
            S_ = st["mlp_head"]
            dense_cols(S_, 0, 0, A4, "norm_mlp")
            dense_cols(S_, 0, 4, B4)
            await_hidden(S_, 1, 0)
            down(S_, 0, 8, range(4), first=True)
            S_ = st["mlp_loop"]
            with trips(pe, S_) as i:
                dense_cols(S_, i, 0, A4)
                await_hidden(S_, 0, i)
                down(S_, i, 4, range(4))
            S_ = st["mlp_tail"]
            await_hidden(S_, 0, 0)
            last_down(S_, 0, range(4))

            def project_heads(S_, i, groups, turned):
                for g in range(groups):
                    n = g * 12
                    dense_rows(S_, i, n, (f"q{g}0", f"q{g}1"), turned if g == 0 else None)
                    dense_rows(S_, i, n + 4, (f"k{g}0", f"k{g}1"))
                    turn_heads(S_, (f"qt{g}0", f"qt{g}1"), i, 4 * g + 2)
                    dense_rows(S_, i, n + 8, (f"v{g}0", f"v{g}1"), tiles=range(KT - 1))
                    turn_heads(S_, (f"kt{g}0", f"kt{g}1"), i, 4 * g + 4)
                    dense_rows(S_, i, n + 8, (f"v{g}0", f"v{g}1"), tiles=[KT - 1])
                for nm in (f"kt{g}0", f"kt{g}1"):
                    pe.wait_ge(*is_drained(S_, nm, i))

            def ffn(tag):
                norm(st[f"norm_ffn_{tag}"])
                S_ = st[f"ffn_{tag}_head"]
                dense_cols(S_, 0, 0, A4, f"norm_ffn_{tag}")
                dense_cols(S_, 0, 4, B4)
                await_hidden(S_, 1, 0)
                down(S_, 0, 8, range(2), first=True)
                S_ = st[f"ffn_{tag}_loop"]
                with trips(pe, S_) as i:
                    dense_cols(S_, i, 0, A4)
                    await_hidden(S_, 0, i)
                    down(S_, i, 4, range(2))
                    dense_cols(S_, i, 6, B4)
                    await_hidden(S_, 1, i)
                    down(S_, i, 10, range(2))
                S_ = st[f"ffn_{tag}_tail"]
                dense_cols(S_, 0, 0, A4)
                await_hidden(S_, 0, 0)
                down(S_, 0, 4, range(2))
                await_hidden(S_, 1, 0)
                last_down(S_, 6, range(2))

            norm(st["norm_a"], "in")
            S_ = st["half_a"]
            with trips(pe, S_) as i:
                project_heads(S_, i, NG, "norm_a")
                attention(S_, units_a(), i, prob, "prob", (f"v{NG - 1}0", f"v{NG - 1}1"))
            for b in (4, 5):
                pe.wait_ge(drained[b], at(st["turn_a"], ("bank", b), 0))
            turn(st["turn_a"], o_sb, "out")
            project_out("out_a", "turn_a")
            ffn("a")
            norm(st["norm_b"])
            S_ = st["half_b"]
            with trips(pe, S_) as i:
                project_heads(S_, i, 1, "norm_b")
                attention(S_, units_b(), i, prob, "prob", ("v00", "v01"))
            for b in (4, 5):
                pe.wait_ge(drained[b], at(st["turn_b"], ("bank", b), 0))
            turn(st["turn_b"], o_sb, None)
            project_out("out_b", "turn_b")
            ffn("b")

        @block.scalar
        def _(act):
            chain = Chain(act, "act_step")
            norm_chain, post_chain = Chain(act, "ln_norm"), Chain(act, "ln_post")
            LN_EXP = "natural_log_exp_and_others"

            def split(stg, n, i=0):
                if stg.q0 + n + SLOTS >= plan.nq:
                    return
                slot = plan.slot(stg, n)
                act.wait_ge(*was_read(stg, n, i))
                act.wait_ge(loaded[slot], (plan.turn(stg, n, i, SLOTS) + 1) * 16)
                act.activation(w_hi[:, slot, :], w_in[:, slot, :], ACT.Copy).then_inc(hi_done[slot], 1)

            def splits(stg, ns, i=0):
                for n in ns:
                    split(stg, n, i)

            def rsqrt(dst, src, tmp, key, chain=chain):
                chain.link(act.activation(tmp, src, ACT.Ln, bias=EPS))
                act.activation(dst, tmp, ACT.Exp, scale=-0.5).then_inc(s[key], 1)

            def turned(stg, gain, out_stage=None, halfway=()):
                for k in range(KT):
                    act.wait_ge(*is_full(stg, f"t{k}"))
                    g = 1.0 if gain is None else gain[:, k:k + 1]
                    act.activation(aT_hi[:, k, :], ps[:, bank(stg, f"t{k}"), 0:S], ACT.Copy, scale=g).then_inc(s["hiT"], 1)
                    if k == KT // 2 - 1:
                        splits(out_stage, halfway)

            def norm_squares(stg, x_ready, t):
                for h in range(2):
                    act.wait_ge(*x_ready[t][h])
                    act.activation(u32[:, h * 512:(h + 1) * 512], x[:, t, h * 512:(h + 1) * 512], ACT.Square,
                                   scale=D ** -0.5, accum_out=stat("mh", 4)[:, 2 * t + h:2 * t + h + 1])\
                        .then_inc(s["mh"], 1)

            def norm_scale(stg, t):
                act.wait_ge(s["ms"], at(stg, "ms", t + 1))
                rsqrt(stat("rstd", 2)[:, t:t + 1], stat("ms", 2)[:, t:t + 1], stat("lnms", 2)[:, t:t + 1], "rstd",
                      norm_chain)
                act.wait_ge(s["rstd"], at(stg, "rstd", t + 1))
                act.activation(xn[:, t, 512:], x[:, t, 512:], ACT.Copy, scale=stat("rstd", 2)[:, t:t + 1])\
                    .then_inc(s["xn"], 1)

            def post_tile(stg, out_stage, rows_, t):
                for h in range(2):
                    n = 2 * t + h
                    act.wait_ge(*is_full(out_stage, f"{rows_}{n}"))
                    act.activation(hid[:].rearrange("p a b -> p (a b)")[:, h * 512:(h + 1) * 512],
                                   ps[:, n, :], ACT.Square, scale=D ** -0.5,
                                   accum_out=stat("msq", 4)[:, n:n + 1]).then_inc(s["msq"], 1)
                act.wait_ge(s["pms"], at(stg, "pms", t + 1))
                rsqrt(stat("prstd", 2)[:, t:t + 1], stat("pms", 2)[:, t:t + 1], stat("lnp", 2)[:, t:t + 1], "prstd",
                      post_chain)

            def sum_and_norm(out_stage, rows_, stg, gain, where, post=None):
                x_ready = after_post(post.name) if post else after_sum(out_stage.name, rows_)
                for t in range(TOK):
                    if post:
                        post_chain.enter(post, 0, t)
                        post_tile(post, out_stage, rows_, t)
                    norm_squares(stg, x_ready, t)
                    if t == 0:
                        splits(out_stage, where[0])
                    norm_chain.enter(stg, 0, t)
                    norm_scale(stg, t)
                    splits(out_stage, where[1 + t])
                turned(stg, gain, out_stage, where[3])
                splits(out_stage, where[4])

            def first_split(slot):
                act.wait_ge(loaded[slot], 16)
                act.activation(w_hi[:, slot, :], w_in[:, slot, :], ACT.Copy).then_inc(hi_done[slot], 1)

            def attention(stg, units, i):
                units = list(units)
                n = len(units)
                for u in range(n + 1):
                    if u < n:
                        un = units[u]
                        act.wait_ge(*is_drained(stg, f"s{u}", i))
                        if u >= 2:
                            act.wait_ge(*is_full(stg, f"p{u - 2}", i))
                        nseg = len(un["segments"])
                        for g, (c, W, _) in enumerate(un["segments"]):
                            last = act.activation(prob[:, u % 2, c:c + W], sm[:, u % 2, c:c + W], ACT.Exp, scale=-1.0,
                                                  bias=stat(f"nmax{u % 2}", 2)[:, g:g + 1],
                                                  accum_out=stat(f"den{u % 2}", 2)[:, g:g + 1])
                        last.then_inc(s["prob"], 1)
                    if 1 <= u <= n:
                        v = u - 1
                        act.wait_ge(*is_full(stg, f"p{v}", i))
                        if v >= 2:
                            act.wait_ge(*is_full(stg, f"o{v - 2}", i))
                        W = units[v]["tiles"] * P
                        b = bank(stg, f"p{v}")
                        act.activation(pts[:, v % 2, 0:W], ps[:, b, 0:W], ACT.Copy).then_inc(drained[b], 1)

            def evac_v(stg, name, i, dst, src=None):
                act.wait_ge(*is_full(stg, name, i))
                b = bank(stg, name)
                src = ps[:, b, :] if src is None else src
                act.activation(dst, src, ACT.Copy).then_inc(drained[b], 1)

            def evac_q(stg, name, i, j0, scale):
                act.wait_ge(*is_full(stg, name, i))
                b = bank(stg, name)
                v = ps[:, b, :].rearrange("p (j s) -> p j s", j=2)
                for h in range(2):
                    r = slice(h * HD, (h + 1) * HD)
                    sc = scale if isinstance(scale, float) else scale[r, :]
                    last = act.activation(qz[r, j0:j0 + 2, h, :], v[r, :, :], ACT.Copy, scale=sc)
                last.then_inc(drained[b], 1)

            def evac_k(stg, name, i, j0, scale):
                act.wait_ge(*is_full(stg, name, i))
                b = bank(stg, name)
                act.activation(kT[:, j0:j0 + 2, :], ps[:, b, :].rearrange("p (j s) -> p j s", j=2), ACT.Copy,
                               scale=scale).then_inc(drained[b], 1)

            act.preload_act_table_set(LN_EXP)
            S_ = st["norm_in1"]
            act.wait_ge(s["cols_in"], 16)
            for t in range(TOK):
                norm_squares(S_, [[(s[f"x_in{t}"], 16)] * 2 for t in range(TOK)], t)
                norm_chain.enter(S_, 0, t)
                norm_scale(S_, t)
            first_split(0)
            turned(S_, col("g_mix"))
            for slot in range(1, SLOTS):
                first_split(slot)
            act.wait_ge(s["gate_in"], 16)
            act.activation(gt_hi[:], gt_in[:], ACT.Copy).then_inc(s["gate_w"], 1)
            act.wait_ge(s["lam"], 1)
            act.activation(stat("elam", 2), stat("dots", 2), ACT.Exp).then_inc(s["lam"], 1)

            S_ = st["in1"]
            chain.enter(S_, 0)
            splits(S_, range(0, 4))
            splits(S_, range(4, 8))
            act.wait_ge(s["gates"], at(S_, "gates", 2))
            act.activation(gm[0:4, 2, :], gm[0:4, 1, :], ACT.Exp).then_inc(s["lnf"], 1)
            act.wait_ge(s["lnf"], at(S_, "lnf", 1))
            act.activation(gm[0:4, 3, :], gm[0:4, 2, :], ACT.Ln, bias=1.0).then_inc(s["lnf"], 1)
            splits(S_, range(8, 12))
            for f in range(4):
                act.wait_ge(*is_full(S_, f"mqk{f}"))
                act.activation(hid[:, f, :], ps[:, 4 + f, 0:S], ACT.Identity, scale=col("cw1", f * 4 + 3),
                               bias=col("cb1", f)).then_inc(s["cv"], 1)
            splits(S_, range(12, 16))
            for t in range(TOK):
                evac_v(S_, f"dv{t}", 0, vv[:, t, 0:512])
            act.wait_ge(*is_full(S_, "gate_m"))
            act.activation(atok[:, 0, :, :], ps[:, 4, 0:8].rearrange("p (t h) -> p t h", t=2), ACT.Copy)
            act.activation(atok[:, 1, :, :], ps[:, 4, 8:16].rearrange("p (t h) -> p t h", t=2), ACT.Exp,
                           scale=-1.0).then_inc(drained[4], 1)
            for f in range(4):
                act.wait_ge(*is_drained(S_, f"mqk{f}"))
            chain.link(act.activation(u32[:], hid[:].rearrange("p a b -> p (a b)"), ACT.Exp, scale=-1.0))
            chain.link(act.activation(u32[:], u32[:], ACT.Ln, bias=1.0))
            act.activation(u32[:], u32[:], ACT.Exp, scale=-1.0).then_inc(s["ecv"], 1)
            act.wait_ge(s["const_ready"], 2)
            for j in range(2):
                evac_q(S_, f"qt{j}", 0, 2 * j, -(HD ** -0.5))
            splits(S_, range(16, 20))
            for t in range(TOK):
                evac_v(S_, f"mv{t}", 0, vm(t)[:, :, 0:VD], ps[:, 2 + t, :].rearrange("p (h c) -> p h c", h=NH1))
            for j in range(2):
                evac_k(S_, f"kt{j}", 0, 2 * j, 1.0)
            chain.leave()

            S_ = st["mix"]
            chain.enter(S_, 0)
            units = list(units_diff())
            n = len(units)
            for u in range(n + 3):
                if u < n:
                    act.wait_ge(*is_drained(S_, f"s{u}"))
                    if u >= 3:
                        act.wait_ge(s["pd"], at(S_, "pd", u - 2))
                    for g, (c, W, _) in enumerate(units[u]["segments"]):
                        last = act.activation(prob[:, u % 3, c:c + W], sm[:, u % 2, c:c + W], ACT.Exp, scale=-1.0,
                                              bias=stat(f"nmax{u % 2}", 2)[:, g:g + 1],
                                              accum_out=stat(f"den{u % 3}", 2)[:, g:g + 1])
                    last.then_inc(s["prob"], 1)
                h, odd = divmod(u, 2)
                if h < NH1 and not odd:
                    if h == 0:
                        act.wait_ge(*is_drained(st["in1"], "gate_m"))
                    act.wait_ge(*is_drained(S_, f"m{h}"))
                    if h >= 2:
                        act.wait_ge(*is_drained(S_, f"ls{h - 2}"))
                    for c, W, t in ((0, S, 0), (S, P, 1)):
                        last = act.activation(wmat[:, h % 2, c:c + W], lsm[:, h % 2, c:c + W], ACT.Exp, scale=-1.0,
                                              bias=atok[:, 0, t, h:h + 1])
                    last.then_inc(s["wm"], 1)
                if 2 <= u < n + 2:
                    v = u - 2
                    act.wait_ge(*is_full(S_, f"p{v}"))
                    if v >= 2:
                        act.wait_ge(*is_full(S_, f"o{v - 2}"))
                    W = units[v]["tiles"] * P
                    act.activation(pts[:, v % 2, 0:W], ps[:, 2, 0:W], ACT.Copy).then_inc(drained[2], 1)
                if u >= 3:
                    v = u - 3
                    un = units[v]
                    act.wait_ge(*is_full(S_, f"o{v}"))
                    act.activation(o_sb[:, un["tok"], un["head"] * P:(un["head"] + 1) * P], ps[:, 3, 0:P],
                                   ACT.Copy).then_inc(drained[3], 1)
                if u in MO_STEPS:
                    split(S_, MO_STEPS.index(u))
                if u in (MO_STEPS[-1] + 1, MO_STEPS[-1] + 2):
                    t = u - MO_STEPS[-1] - 1
                    act.wait_ge(*is_full(S_, f"mo{t}"))
                    act.activation(sqb[:, t, :], ps[:, 4 + t, :], ACT.Exp, scale=-1.0).then_inc(drained[4 + t], 1)
                    act.wait_ge(*is_drained(S_, f"mo{t}"))
                    chain.link(act.activation(sqb[:, t, :], sqb[:, t, :], ACT.Ln, bias=1.0))
                    act.activation(sqb[:, t, :], sqb[:, t, :], ACT.Exp, scale=-1.0).then_inc(s["sig"], 1)
            act.wait_ge(s["oms"], at(S_, "oms", 12))
            rsqrt(stat("orstd", 16), stat("oms", 16), stat("lno", 16), "orstd")
            act.wait_ge(s["orstd"], at(S_, "orstd", 1))
            for h in range(4):
                last = act.activation(o_sb[:, 1, h * P:(h + 1) * P], o_sb[:, 1, h * P:(h + 1) * P], ACT.Copy,
                                      scale=stat("orstd", 16)[:, 8 + h:9 + h])
            last.then_inc(s["osq"], 1)
            chain.leave()
            turned(st["turn_mix"], col("g_heads"))
            splits(st["out1"], range(4))
            sum_and_norm(st["out1"], "r", st["norm_mlp"], col("g_mlp"), OUT_SPLITS, st["post_mix"])

            def relu_rows(stg, i, names, first):
                for f in range(4):
                    act.wait_ge(*is_full(stg, names[f], i))
                    act.activation(hid[:, f, :], ps[:, 4 + f, 0:S], ACT.Relu).then_inc(drained[4 + f], 1)

            def hidden_hi(stg, i, n, W=4 * S):
                act.wait_ge(s["u"], at(stg, "u", n, i))
                act.activation(u_hi[:, 0:W], u32[:, 0:W], ACT.Copy).then_inc(s["uhi"], 1)

            A4, B4 = [f"a{f}" for f in range(4)], [f"b{f}" for f in range(4)]
            S_ = st["mlp_head"]
            splits(S_, range(0, 4))
            relu_rows(S_, 0, A4, True)
            hidden_hi(S_, 0, 1)
            splits(S_, range(4, 8))
            relu_rows(S_, 0, B4, False)
            splits(S_, range(8, 12))
            hidden_hi(S_, 0, 2)
            S_ = st["mlp_loop"]
            with trips(act, S_) as i:
                splits(S_, range(0, 4), i)
                relu_rows(S_, i, A4, False)
                splits(S_, range(4, 7), i)
                act.wait_ge(*was_read(S_, 7, i))
                hidden_hi(S_, i, 1)
                splits(S_, range(7, 8), i)

            def project_heads(S_, i, groups, layer):
                n = [0]

                def head_norms(names):
                    for t in range(TOK):
                        act.wait_ge(*is_full(S_, names[t], i))
                        if n[0] >= 2:
                            act.wait_ge(s["ms8"], at(S_, "ms8", n[0] - 1, i))
                        act.activation(sqb[:, t, :], ps[:, bank(S_, names[t]), :], ACT.Square,
                                       scale=HD ** -0.5).then_inc(s["sq"], 1)
                        n[0] += 1
                        act.wait_ge(s["ms8"], at(S_, "ms8", n[0], i))
                        rsqrt(stat(f"rs8{t}", 8), stat(f"ms8{t}", 8), stat(f"ln8{t}", 8), "rs8")
                for g in range(groups):
                    q0 = g * 12
                    splits(S_, range(q0, q0 + 4), i)
                    head_norms((f"q{g}0", f"q{g}1"))
                    splits(S_, range(q0 + 4, q0 + 8), i)
                    for j in range(2):
                        evac_q(S_, f"qt{g}{j}", i, g * 4 + 2 * j, gq[:, 2 * (layer * 3 + g):2 * (layer * 3 + g) + 1])
                    head_norms((f"k{g}0", f"k{g}1"))
                    splits(S_, range(q0 + 8, q0 + 11), i)
                    for j in range(2):
                        evac_k(S_, f"kt{g}{j}", i, g * 4 + 2 * j, gq[:, 2 * (layer * 3 + g) + 1:2 * (layer * 3 + g) + 2])
                    splits(S_, range(q0 + 11, q0 + 12), i)
                    for t in range(TOK):
                        evac_v(S_, f"v{g}{t}", i, vv[:, t, g * 512:(g + 1) * 512])

            def ffn(tag, layer):
                W = 2 * S
                cw = col(f"cw2{tag}").rearrange("p (j c) -> p j c", c=16)

                def convolve(stg, i, names, j, n):
                    for f in range(4):
                        act.wait_ge(*is_full(stg, names[f], i))
                        sc = cw[:, bass.ds(j, 1), 4 * f + 2:4 * f + 3].rearrange("p a b -> p (a b)")
                        bi = cw[:, bass.ds(j, 1), 4 * f + 3:4 * f + 4].rearrange("p a b -> p (a b)")
                        act.activation(hid[:, f, :], ps[:, 4 + f, 0:S], ACT.Identity, scale=sc, bias=bi).then_inc(s["cv"], 1)
                    for f in range(2):
                        act.wait_ge(*is_drained(stg, names[f], i))
                    act.activation(u32[:, W:2 * W], hid[:, 0:2, :].rearrange("p a b -> p (a b)"), ACT.Silu)\
                        .then_inc(s["silu"], 1)
                act.preload_act_table(ACT.Silu)
                S_ = st[f"ffn_{tag}_head"]
                splits(S_, range(0, 3))
                convolve(S_, 0, A4, 0, 1)
                splits(S_, range(3, 4))
                hidden_hi(S_, 0, 1, W)
                splits(S_, range(4, 7))
                convolve(S_, 0, B4, 1, 2)
                splits(S_, range(7, 10))
                hidden_hi(S_, 0, 2, W)
                S_ = st[f"ffn_{tag}_loop"]
                with trips(act, S_) as i:
                    splits(S_, range(0, 3), i)
                    convolve(S_, i, A4, i * 2 + 2, 1)
                    splits(S_, range(3, 6), i)
                    hidden_hi(S_, i, 1, W)
                    splits(S_, range(6, 9), i)
                    convolve(S_, i, B4, i * 2 + 3, 2)
                    splits(S_, range(9, 12), i)
                    hidden_hi(S_, i, 2, W)
                S_ = st[f"ffn_{tag}_tail"]
                splits(S_, range(0, 3))
                convolve(S_, 0, A4, U2 - 1, 1)
                splits(S_, range(3, 4))
                act.wait_ge(*was_read(S_, 5, 0))
                hidden_hi(S_, 0, 1, W)
                splits(S_, range(4, 6))
                act.preload_act_table_set(LN_EXP)

            sum_and_norm(st["mlp_tail"], "acc", st["norm_a"], col("g_a"), MLP_SPLITS, st["post_mlp"])
            S_ = st["half_a"]
            with trips(act, S_) as i:
                chain.enter(S_, i)
                project_heads(S_, i, NG, 0)
                attention(S_, units_a(), i)
                chain.leave()
            turned(st["turn_a"], None)
            splits(st["out_a"], range(4))
            sum_and_norm(st["out_a"], "r", st["norm_ffn_a"], col("g_fa"), OUT_SPLITS)
            ffn("a", 0)
            sum_and_norm(st["ffn_a_tail"], "acc", st["norm_b"], col("g_b"), FFN_SPLITS)
            S_ = st["half_b"]
            with trips(act, S_) as i:
                chain.enter(S_, i)
                project_heads(S_, i, 1, 1)
                attention(S_, units_b(), i)
                chain.leave()
            turned(st["turn_b"], None)
            splits(st["out_b"], range(4))
            sum_and_norm(st["out_b"], "r", st["norm_ffn_b"], col("g_fb"), OUT_SPLITS)
            ffn("b", 1)

        @block.gpsimd
        def _(pool):
            pool.memset(qz[:], 0.0).then_inc(s["const_ready"], 1)
            for t in range(TOK):
                last = pool.memset(vm(t)[:, :, VD:VD + 1], 1.0)
            last.then_inc(s["const_ready"], 1)
            S_ = st["mix"]
            for t in range(TOK):
                pool.wait_ge(s["sig"], at(S_, "sig", t + 1))
            for g in range(NH1):
                pool.wait_ge(s["oms"], at(S_, "oms", oms_at_head(g)))
                o = o_sb[:, :, 512 + g * P:512 + (g + 1) * P]
                pool.tensor_tensor(o, o, sqb[:, :, g * P:(g + 1) * P], ALU.mult).then_inc(s["gated"], 1)

        @block.vector
        def _(dve):
            chain = Chain(dve, "dve_step")
            link = chain.link

            def split(stg, n, i=0):
                if stg.q0 + n + SLOTS >= plan.nq:
                    return
                slot = plan.slot(stg, n)
                dve.wait_ge(hi_done[slot], plan.turn(stg, n, i, SLOTS) + 1)
                dve.tensor_tensor(w_lo[:, slot, :], w_in[:, slot, :], w_hi[:, slot, :].bitcast(F32),
                                  ALU.subtract).then_inc(lo_done[slot], 1)

            def splits(stg, ns, i=0):
                for n in ns:
                    split(stg, n, i)

            def turned(stg, gain, out_stage=None, halfway=()):
                for k in range(KT):
                    dve.wait_ge(s["hiT"], at(stg, "hiT", k + 1))
                    g = 1.0 if gain is None else gain[:, k:k + 1]
                    b = bank(stg, f"t{k}")
                    dve.scalar_tensor_tensor(out=aT_lo[:, k, :], in0=ps[:, b, 0:S], scalar=g,
                                             in1=aT_hi[:, k, :].bitcast(F32), op0=ALU.mult,
                                             op1=ALU.subtract).then_inc(drained[b], 1)
                    if k == KT // 2 - 1:
                        splits(out_stage, halfway)

            def norm_mean(stg, t):
                dve.wait_ge(s["mh"], at(stg, "mh", 2 * t + 2))
                m = stat("mh", 4)
                dve.tensor_tensor(stat("ms", 2)[:, t:t + 1], m[:, 2 * t:2 * t + 1], m[:, 2 * t + 1:2 * t + 2],
                                  ALU.add).then_inc(s["ms"], 1)

            def norm_scale(stg, x_ready, t):
                dve.wait_ge(*x_ready[t][0])
                dve.wait_ge(s["rstd"], at(stg, "rstd", t + 1))
                dve.tensor_scalar(xn[:, t, 0:512], x[:, t, 0:512], stat("rstd", 2)[:, t:t + 1], None, ALU.mult)\
                    .then_inc(s["xn"], 1)

            def post_tile(stg, out_stage, rows_, gain, t):
                m = stat("msq", 4)
                for h in range(2):
                    b = 2 * t + h
                    sl = slice(h * 512, (h + 1) * 512)
                    dve.wait_ge(s["msq"], at(stg, "msq", b + 1))
                    if h == 1:
                        dve.tensor_tensor(stat("pms", 2)[:, t:t + 1], m[:, 2 * t:2 * t + 1], m[:, 2 * t + 1:2 * t + 2],
                                          ALU.add).then_inc(s["pms"], 1)
                    dve.tensor_tensor(xn[:, t, sl], ps[:, b, :], gain[:, sl], ALU.mult).then_inc(drained[b], 1)
                dve.wait_ge(s["prstd"], at(stg, "prstd", t + 1))
                for h in range(2):
                    sl = slice(h * 512, (h + 1) * 512)
                    dve.wait_ge(*is_drained(out_stage, f"{rows_}{2 * t + h}"))
                    dve.scalar_tensor_tensor(out=x[:, t, sl], in0=xn[:, t, sl], scalar=stat("prstd", 2)[:, t:t + 1],
                                             in1=x[:, t, sl], op0=ALU.mult, op1=ALU.add).then_inc(s["x_new"], 1)

            def sum_tile(out_stage, rows_, t):
                for h in range(2):
                    b = 2 * t + h
                    sl = slice(h * 512, (h + 1) * 512)
                    dve.wait_ge(*is_full(out_stage, f"{rows_}{b}"))
                    dve.tensor_tensor(x[:, t, sl], ps[:, b, :], x[:, t, sl], ALU.add).then_inc(drained[b], 1)

            def sum_and_norm(out_stage, rows_, stg, gain, where, post=None, post_gain=None):
                x_ready = after_post(post.name) if post else after_sum(out_stage.name, rows_)
                for t in range(TOK):
                    if post:
                        post_tile(post, out_stage, rows_, post_gain, t)
                    else:
                        sum_tile(out_stage, rows_, t)
                    if t == 0:
                        splits(out_stage, where[0])
                    norm_mean(stg, t)
                    norm_scale(stg, x_ready, t)
                    splits(out_stage, where[1 + t])
                turned(stg, gain, out_stage, where[3])
                splits(out_stage, where[4])

            def first_split(slot):
                dve.wait_ge(hi_done[slot], 1)
                dve.tensor_tensor(w_lo[:, slot, :], w_in[:, slot, :], w_hi[:, slot, :].bitcast(F32),
                                  ALU.subtract).then_inc(lo_done[slot], 1)

            def attention(stg, units, i):
                units = list(units)
                n = len(units)
                for u in range(n + 2):
                    if u < n:
                        un = units[u]
                        dve.wait_ge(*is_full(stg, f"s{u}", i))
                        if u >= 2:
                            dve.wait_ge(s["prob"], at(stg, "prob", u - 1, i))
                        b = bank(stg, f"s{u}")
                        dve.sem_inc(s["unit"], 1)
                        for g, (c, W, mask) in enumerate(un["segments"]):
                            last = dve.tensor_tensor_reduce(
                                out=sm[:, u % 2, c:c + W], in0=ps[:, b, c:c + W], in1=mask, scale=1.0, scalar=BIG,
                                op0=ALU.add, op1=ALU.min, accum_out=stat(f"nmax{u % 2}", 2)[:, g:g + 1])
                        last.then_inc(drained[b], 1)
                        if u == 0:
                            splits(stg, range(len(stg.quarters) - 1, len(stg.quarters)), i)
                    if 1 <= u <= n:
                        v = u - 1
                        nseg = len(units[v]["segments"])
                        dve.wait_ge(s["prob"], at(stg, "prob", v + 1, i))
                        if v >= 2:
                            dve.wait_ge(*is_drained(stg, f"o{v - 2}", i))
                        link(dve.reciprocal(stat(f"rden{v % 2}", 2)[:, 0:nseg], stat(f"den{v % 2}", 2)[:, 0:nseg]))
                    if u >= 2:
                        v = u - 2
                        un = units[v]
                        dve.wait_ge(*is_full(stg, f"o{v}", i))
                        b = bank(stg, f"o{v}")
                        for g, c, oc in un["outs"]:
                            if stg.trips > 1:
                                dst = o_sb[:, un["tok"], bass.ds(i * 512 + oc, HD)]
                            last = dve.tensor_scalar(dst, ps[:, b, c:c + HD], stat(f"rden{v % 2}", 2)[:, g:g + 1],
                                                     None, ALU.mult)
                        last.then_inc(drained[b], 1)

            def sum_square(un, v, counted):
                dve.wait_ge(*is_drained(st["mix"], f"o{v}"))
                o = o_sb[:, un["tok"], un["head"] * P:(un["head"] + 1) * P]
                j = un["tok"] * 8 + un["head"]
                if v >= 2:
                    dve.wait_ge(s["oms"], at(st["mix"], "oms", counted[v - 2]))
                dve.tensor_tensor_reduce(out=rt[:, v % 2, :], in0=o, in1=o, scale=1.0 / VD, scalar=0.0, op0=ALU.mult,
                                         op1=ALU.add, accum_out=stat("oms", 16)[:, j:j + 1]).then_inc(s["oms"], 1)

            rtmp = xq[:, 0, 0:S]

            S_ = st["load"]
            chain.enter(S_, 0)
            dve.wait_ge(s["cols_in"], 16)
            for t in range(TOK):
                norm_mean(st["norm_in1"], t)
                norm_scale(st["norm_in1"], [[(s[f"x_in{t}"], 16)] * 2 for t in range(TOK)], t)
            first_split(0)
            turned(st["norm_in1"], col("g_mix"))
            for slot in range(1, SLOTS):
                first_split(slot)
            dve.wait_ge(s["gate_w"], 1)
            dve.tensor_tensor(gt_lo[:], gt_in[:], gt_hi[:].bitcast(F32), ALU.subtract).then_inc(s["gate_w"], 1)
            dve.wait_ge(s["const_in"], 32)
            lam = row("lambda").rearrange("p (v d) -> p v d", v=4)
            for j in range(2):
                last = dve.tensor_tensor_reduce(out=rt[:, j, 0:HD], in0=lam[:, 2 * j, :], in1=lam[:, 2 * j + 1, :],
                                                scale=1.0, scalar=0.0, op0=ALU.mult, op1=ALU.add,
                                                accum_out=stat("dots", 2)[:, j:j + 1])
            last.then_inc(s["lam"], 1)
            g = col("gains")
            link(dve.tensor_scalar(gq[:], g, col("unrotated", 0), col("rotated", 0), ALU.mult, ALU.add))
            gq2 = gq[:].rearrange("p (g c) -> p g c", c=2)
            link(dve.tensor_scalar(gq2[:, :, 0:1], gq2[:, :, 0:1], -(HD ** -0.5), None, ALU.mult))
            link(dve.tensor_scalar(col("g_heads", 0, 4), col("g_heads", 0, 4), 1.0 - LAMBDA_INIT, None, ALU.mult))
            grow = row("gain_rows").rearrange("p (g d) -> p g d", d=ROT)
            for j in range(8):
                dve.tensor_tensor(tabs[:, j, :, :, :].rearrange("p t c d -> p (t c) d"),
                                  const("rope_a" if j < 6 else "rope_b", "p (c d) -> p c d", dict(d=ROT)),
                                  grow[:, j:j + 1, :].broadcast_to([P, 2 * TOK, ROT]), ALU.mult)
            dve.wait_ge(s["lam"], 2)
            e = stat("elam", 2)
            link(dve.tensor_tensor(stat("dlam"), e[:, 1:2], e[:, 0:1], ALU.subtract))
            link(dve.tensor_scalar(stat("neglam"), stat("dlam"), LAMBDA_INIT, None, ALU.subtract))
            chain.leave()

            S_ = st["in1"]
            chain.enter(S_, 0)

            def rotate_full(names, t, dst):
                dve.wait_ge(*is_full(S_, names[t]))
                b = bank(S_, names[t])
                v = rope_view(ps[:, b, :], 8, 2, 32)
                a = rope_view(dst[:, t, :], 8, 2, 32)
                w = rope_view(sqb[:, t, :], 8, 2, 32)
                rp = const("rope1", "p (c t d) -> p c t d", dict(c=2, t=TOK))
                cos, sin = (rp[:, c, t, :].unsqueeze(1) for c in range(2))
                dve.tensor_tensor(dst[:, t, :].rearrange("p (h d) -> p h d", d=32),
                                  ps[:, b, :].rearrange("p (h d) -> p h d", d=32),
                                  cos.broadcast_to([P, 16, 32]), ALU.mult)
                dve.tensor_tensor(w[:, :, 0, :], v[:, :, 1, :], sin.broadcast_to([P, 8, 32]), ALU.mult)
                dve.tensor_tensor(w[:, :, 1, :], v[:, :, 0, :], sin.broadcast_to([P, 8, 32]), ALU.mult)\
                    .then_inc(drained[b], 1)
                dve.wait_ge(drained[b], filled(S_, names[t]))
                dve.tensor_tensor(a[:, :, 0, :], a[:, :, 0, :], w[:, :, 0, :], ALU.subtract)
                dve.tensor_tensor(a[:, :, 1, :], a[:, :, 1, :], w[:, :, 1, :], ALU.add).then_inc(s["rot"], 1)

            splits(S_, range(0, 4))
            for t in range(TOK):
                rotate_full(("dq0", "dq1"), t, xq)
            splits(S_, range(4, 8))
            dve.wait_ge(*is_full(S_, "gate_t"))
            link(dve.tensor_scalar(gi[:], ps[0:4, 7, 0:S], col("b_i", 0)[0:4, :], None, ALU.add))
            dve.tensor_scalar(gm[0:4, 7, :], ps[0:4, 7, S:2 * S], col("b_f", 0)[0:4, :], None, ALU.add)\
                .then_inc(drained[7], 1)
            dve.wait_ge(*is_drained(S_, "gate_t"))
            dve.tensor_scalar(gm[0:4, 0, :], gm[0:4, 7, :], 0.0, None, ALU.min).then_inc(s["gates"], 1)
            link(dve.tensor_scalar(gm[0:4, 6, :], gm[0:4, 7, :], 0.0, None, ALU.max))
            dve.tensor_tensor(gm[0:4, 1, :], gm[0:4, 0, :], gm[0:4, 6, :], ALU.subtract).then_inc(s["gates"], 1)
            for t in range(TOK):
                rotate_full(("dk0", "dk1"), t, turned_keys)
            splits(S_, range(8, 12))
            dve.wait_ge(s["lnf"], at(S_, "lnf", 2))
            link(dve.tensor_tensor(gm[0:4, 3, :], gm[0:4, 0, :], gm[0:4, 3, :], ALU.subtract))
            dve.tensor_tensor_scan(gm[0:4, 4, :], gm[0:4, 3, :], gm[0:4, 3, :], 0.0, ALU.add, ALU.bypass)\
                .then_inc(s["gates"], 1)
            dve.wait_ge(s["gates"], at(S_, "gates", 3))
            link(dve.tensor_tensor(gm[0:4, 5, :], gi[:], gm[0:4, 4, :], ALU.subtract))
            dve.tensor_tensor_scan(gm[0:4, 6, :], gm[0:4, 5, :], gm[0:4, 5, :], 0.0, ALU.max, ALU.bypass)\
                .then_inc(s["gates"], 1)
            dve.wait_ge(s["gates"], at(S_, "gates", 4))
            dve.tensor_tensor(gm[0:4, 7, :], gm[0:4, 4, :], gm[0:4, 6, :], ALU.add).then_inc(s["gates"], 1)
            for f in range(4):
                dve.wait_ge(s["cv"], at(S_, "cv", f + 1))
                for back in (1, 2, 3):
                    ins_ = dve.scalar_tensor_tensor(out=hid[:, f, back:S], in0=ps[:, 4 + f, 0:S - back],
                                                    scalar=col("cw1", f * 4 + 3 - back), in1=hid[:, f, back:S],
                                                    op0=ALU.mult, op1=ALU.add)
                    if back < 3:
                        link(ins_)
                    else:
                        ins_.then_inc(drained[4 + f], 1)
            dve.wait_ge(drained[7], filled(S_, "mqk3"))
            splits(S_, range(12, 16))
            dve.wait_ge(s["ecv"], at(S_, "ecv", 1))
            for j, sc in enumerate((HD ** -0.5, 1.0)):
                dve.scalar_tensor_tensor(out=mqkT[:, 2 * j:2 * j + 2, :].rearrange("p a b -> p (a b)"),
                                         in0=hid[:, 2 * j:2 * j + 2, :].rearrange("p a b -> p (a b)"), scalar=sc,
                                         in1=u32[:, j * 512:(j + 1) * 512], op0=ALU.mult, op1=ALU.mult)\
                    .then_inc(s["mqk"], 1)
            splits(S_, range(16, 20))
            chain.leave()

            S_ = st["mix"]
            chain.enter(S_, 0)
            ct = const("causal_t")

            def mlstm_head(g):
                dve.wait_ge(*is_full(S_, f"lo{g}"))
                v = ps[:, 6, :].rearrange("p (t c) -> p t c", t=2)
                den = v[:, :, VD:VD + 1]
                nd, dm = (stat(n, 2).rearrange("p (t c) -> p t c", t=2) for n in ("nd", "dm"))
                em = atok[:, 1, :, g:g + 1]
                link(dve.tensor_scalar(nd, den, -1.0, None, ALU.mult))
                link(dve.tensor_tensor(nd, nd, em, ALU.max))
                link(dve.tensor_tensor(dm, den, nd, ALU.max))
                link(dve.reciprocal(dm, dm))
                for t in range(TOK):
                    last = dve.tensor_scalar(o_sb[:, t, 512 + g * P:512 + (g + 1) * P], v[:, t, 0:VD],
                                             stat("dm", 2)[:, t:t + 1], None, ALU.mult)
                last.then_inc(drained[6], 1)
                dve.wait_ge(*is_drained(S_, f"lo{g}"))
                for t in range(TOK):
                    o = o_sb[:, t, 512 + g * P:512 + (g + 1) * P]
                    j = t * 8 + 4 + g
                    last = dve.tensor_tensor_reduce(out=xq[:, 1, t * P:(t + 1) * P], in0=o, in1=o, scale=1.0 / VD,
                                                    scalar=0.0, op0=ALU.mult, op1=ALU.add,
                                                    accum_out=stat("oms", 16)[:, j:j + 1])
                last.then_inc(s["oms"], 1)

            units = list(units_diff())
            n = len(units)
            n_oms, counted = 0, []
            for u in range(n + 4):
                if u < n:
                    dve.wait_ge(*is_full(S_, f"s{u}"))
                    if u >= 2:
                        dve.wait_ge(s["prob"], at(S_, "prob", u - 1))
                    b = bank(S_, f"s{u}")
                    dve.sem_inc(s["unit"], 1)
                    for g, (c, W, mask) in enumerate(units[u]["segments"]):
                        last = dve.tensor_tensor_reduce(
                            out=sm[:, u % 2, c:c + W], in0=ps[:, b, c:c + W], in1=mask, scale=1.0, scalar=BIG,
                            op0=ALU.add, op1=ALU.min, accum_out=stat(f"nmax{u % 2}", 2)[:, g:g + 1])
                    last.then_inc(drained[b], 1)
                h, odd = divmod(u, 2)
                if h < NH1 and not odd:
                    dve.wait_ge(*is_full(S_, f"m{h}"))
                    if h >= 2:
                        dve.wait_ge(*is_full(S_, f"lo{h - 2}"))
                    dve.tensor_tensor(lsm[:, h % 2, 0:S], ps[:, 6, 0:S], ct, ALU.add)
                    dve.tensor_tensor(lsm[:, h % 2, S:S + P], ps[:, 6, P:S], ct[:, 0:P], ALU.add)\
                        .then_inc(drained[6], 1)
                if 1 <= u <= n:
                    v = u - 1
                    r = stat(f"rden{v % 2}", 2)
                    W = units[v]["segments"][0][1]
                    dve.wait_ge(s["prob"], at(S_, "prob", v + 1))
                    link(dve.reciprocal(r, stat(f"den{v % 3}", 2)))
                    link(dve.tensor_scalar(stat("rlam"), r[:, 1:2], stat("neglam"), None, ALU.mult))
                    if v >= 3:
                        dve.wait_ge(*is_full(S_, f"p{v - 3}"))
                    link(dve.tensor_scalar(rtmp[:, 0:W], prob[:, v % 3, W:2 * W], stat("rlam"), None, ALU.mult))
                    dve.scalar_tensor_tensor(out=pdf[:, v % 3, 0:W], in0=prob[:, v % 3, 0:W], scalar=r[:, 0:1],
                                             in1=rtmp[:, 0:W], op0=ALU.mult, op1=ALU.add).then_inc(s["pd"], 1)
                if h < NH1 and odd:
                    dve.wait_ge(*is_full(S_, f"ls{h}"))
                    dve.wait_ge(s["wm"], at(S_, "wm", h + 1))
                    dve.tensor_tensor(lsm[:, h % 2, 0:S + P], ps[:, 7, 0:S + P], wmat[:, h % 2, 0:S + P], ALU.mult)\
                        .then_inc(drained[7], 1)
                if u >= 4:
                    sum_square(units[u - 4], u - 4, counted)
                    n_oms += 1
                    counted.append(n_oms)
                if odd and 1 <= h <= NH1:
                    mlstm_head(h - 1)
                    n_oms += 1
                    assert n_oms == oms_at_head(h - 1)
                if u in MO_STEPS:
                    split(S_, MO_STEPS.index(u))
            dve.wait_ge(s["orstd"], at(S_, "orstd", 1))
            dve.wait_ge(s["gated"], at(S_, "gated", 4))
            for t, h0 in ((0, 0), (1, 4)):
                ov = o_sb[:, t, h0 * P:].rearrange("p (h c) -> p h c", c=P)
                r = stat("orstd", 16)[:, t * 8 + h0:t * 8 + 8]
                dve.tensor_tensor(ov, ov, r.unsqueeze(2).broadcast_to([P, 8 - h0, P]), ALU.mult).then_inc(s["osq"], 1)
            chain.leave()
            turned(st["turn_mix"], col("g_heads"))
            splits(st["out1"], range(4))
            sum_and_norm(st["out1"], "r", st["norm_mlp"], col("g_mlp"), OUT_SPLITS, st["post_mix"], row("mix_post"))

            def square(stg, i, n, before):
                for f in range(4):
                    dve.wait_ge(*is_drained(stg, before[f], i))
                if stg is not st["mlp_head"] or n > 1:
                    dve.wait_ge(s["uhi"], at(stg, "uhi", n - 1, i))
                    dve.wait_ge(s["ulo"], at(stg, "ulo", n - 1, i))
                dve.tensor_tensor(u32[:], hid[:].rearrange("p a b -> p (a b)"), hid[:].rearrange("p a b -> p (a b)"),
                                  ALU.mult).then_inc(s["u"], 1)

            def hidden_lo(stg, i, n, W=4 * S):
                dve.wait_ge(s["uhi"], at(stg, "uhi", n, i))
                dve.tensor_tensor(u_lo[:, 0:W], u32[:, 0:W], u_hi[:, 0:W].bitcast(F32), ALU.subtract)\
                    .then_inc(s["ulo"], 1)

            A4, B4 = [f"a{f}" for f in range(4)], [f"b{f}" for f in range(4)]
            S_ = st["mlp_head"]
            splits(S_, range(0, 4))
            square(S_, 0, 1, A4)
            hidden_lo(S_, 0, 1)
            splits(S_, range(4, 8))
            square(S_, 0, 2, B4)
            splits(S_, range(8, 12))
            hidden_lo(S_, 0, 2)
            S_ = st["mlp_loop"]
            with trips(dve, S_) as i:
                splits(S_, range(0, 4), i)
                square(S_, i, 1, A4)
                splits(S_, range(4, 7), i)
                hidden_lo(S_, i, 1)
                splits(S_, range(7, 8), i)

            def project_heads(S_, i, groups, layer):
                n = [0]

                def head_norms(names, which, j):
                    for t in range(TOK):
                        dve.wait_ge(s["sq"], at(S_, "sq", n[0] + 1, i))
                        dve.tensor_reduce(stat(f"ms8{t}", 8), sqb[:, t, :].rearrange("p (h d) -> p h d", d=HD),
                                          AX.X, ALU.add).then_inc(s["ms8"], 1)
                        n[0] += 1
                        dve.wait_ge(s["rs8"], at(S_, "rs8", n[0], i))
                        b = bank(S_, names[t])
                        xv = xq[:, t, :].rearrange("p (h d) -> p h d", d=HD)
                        dve.tensor_tensor(xv, ps[:, b, :].rearrange("p (h d) -> p h d", d=HD),
                                          stat(f"rs8{t}", 8).unsqueeze(2).broadcast_to([P, 8, HD]),
                                          ALU.mult).then_inc(drained[b], 1)
                        dve.wait_ge(*is_drained(S_, names[t], i))
                        T = tabs[:, j, t, :, :]
                        r1, r2 = (rt[:, c, :].rearrange("p (h d) -> p h d", d=ROT) for c in range(2))
                        dve.tensor_tensor(r1, xv[:, :, 0:ROT], T[:, 0, :].unsqueeze(1).broadcast_to([P, 8, ROT]), ALU.mult)
                        link(dve.tensor_tensor(r2, xv[:, :, 0:ROT], T[:, 1, :].unsqueeze(1).broadcast_to([P, 8, ROT]), ALU.mult))
                        dve.tensor_tensor(xv[:, :, 0:8], r1[:, :, 0:8], r2[:, :, 8:16], ALU.add)
                        dve.tensor_tensor(xv[:, :, 8:16], r1[:, :, 8:16], r2[:, :, 0:8], ALU.add)\
                            .then_inc(s["rot"], 1)
                for g in range(groups):
                    q0 = g * 12
                    splits(S_, range(q0, q0 + 4), i)
                    if g > 0:
                        for j in range(2):
                            dve.wait_ge(*is_full(S_, f"kt{g - 1}{j}", i))
                    head_norms((f"q{g}0", f"q{g}1"), 0, (layer * 3 + g) * 2)
                    splits(S_, range(q0 + 4, q0 + 8), i)
                    for j in range(2):
                        dve.wait_ge(*is_full(S_, f"qt{g}{j}", i))
                    head_norms((f"k{g}0", f"k{g}1"), 1, (layer * 3 + g) * 2 + 1)
                    splits(S_, range(q0 + 8, q0 + 11 if g == groups - 1 else q0 + 12), i)

            def ffn(tag):
                W = 2 * S
                cw = col(f"cw2{tag}").rearrange("p (j c) -> p j c", c=16)

                def convolve(stg, i, names, j, n):
                    for f in range(4):
                        dve.wait_ge(s["cv"], at(stg, "cv", 4 * (n - 1) + f + 1, i))
                        for back in (1, 2):
                            sc = cw[:, bass.ds(j, 1), 4 * f + 2 - back:4 * f + 3 - back].rearrange("p a b -> p (a b)")
                            ins_ = dve.scalar_tensor_tensor(out=hid[:, f, back:S], in0=ps[:, 4 + f, 0:S - back],
                                                            scalar=sc, in1=hid[:, f, back:S], op0=ALU.mult, op1=ALU.add)
                            if back < 2:
                                link(ins_)
                            else:
                                ins_.then_inc(drained[4 + f], 1)
                    dve.wait_ge(*is_drained(stg, names[3], i))
                    dve.wait_ge(s["silu"], at(stg, "silu", n, i))
                    dve.wait_ge(s["uhi"], at(stg, "uhi", n - 1, i))
                    dve.wait_ge(s["ulo"], at(stg, "ulo", n - 1, i))
                    dve.tensor_tensor(u32[:, 0:W], u32[:, W:2 * W], hid[:, 2:4, :].rearrange("p a b -> p (a b)"),
                                      ALU.mult).then_inc(s["u"], 1)
                S_ = st[f"ffn_{tag}_head"]
                chain.enter(S_, 0)
                splits(S_, range(0, 3))
                convolve(S_, 0, A4, 0, 1)
                splits(S_, range(3, 4))
                hidden_lo(S_, 0, 1, W)
                splits(S_, range(4, 7))
                convolve(S_, 0, B4, 1, 2)
                splits(S_, range(7, 10))
                hidden_lo(S_, 0, 2, W)
                chain.leave()
                S_ = st[f"ffn_{tag}_loop"]
                with trips(dve, S_) as i:
                    chain.enter(S_, i)
                    splits(S_, range(0, 3), i)
                    convolve(S_, i, A4, i * 2 + 2, 1)
                    splits(S_, range(3, 6), i)
                    hidden_lo(S_, i, 1, W)
                    splits(S_, range(6, 9), i)
                    convolve(S_, i, B4, i * 2 + 3, 2)
                    splits(S_, range(9, 12), i)
                    hidden_lo(S_, i, 2, W)
                    chain.leave()
                S_ = st[f"ffn_{tag}_tail"]
                chain.enter(S_, 0)
                splits(S_, range(0, 3))
                convolve(S_, 0, A4, U2 - 1, 1)
                splits(S_, range(3, 4))
                hidden_lo(S_, 0, 1, W)
                splits(S_, range(4, 6))
                chain.leave()

            sum_and_norm(st["mlp_tail"], "acc", st["norm_a"], col("g_a"), MLP_SPLITS, st["post_mlp"],
                         row("mlp_post"))
            S_ = st["half_a"]
            with trips(dve, S_) as i:
                chain.enter(S_, i)
                project_heads(S_, i, NG, 0)
                attention(S_, units_a(), i)
                chain.leave()
            turned(st["turn_a"], None)
            splits(st["out_a"], range(4))
            sum_and_norm(st["out_a"], "r", st["norm_ffn_a"], col("g_fa"), OUT_SPLITS)
            ffn("a")
            sum_and_norm(st["ffn_a_tail"], "acc", st["norm_b"], col("g_b"), FFN_SPLITS)
            S_ = st["half_b"]
            with trips(dve, S_) as i:
                chain.enter(S_, i)
                project_heads(S_, i, 1, 1)
                attention(S_, units_b(), i)
                chain.leave()
            turned(st["turn_b"], None)
            splits(st["out_b"], range(4))
            sum_and_norm(st["out_b"], "r", st["norm_ffn_b"], col("g_fb"), OUT_SPLITS)
            ffn("b")
            for t in range(TOK):
                sum_tile(st["ffn_b_tail"], "acc", t)


def lay_out(inputs):
    def feat(a):
        return np.asarray(a, np.float32).reshape(-1, P).T

    def twice(a):
        return np.concatenate([a, a], 0)
    unit = {n: np.asarray(v) for n, v in inputs.items()}
    gains = [unit["a_q_norm_2"][0], unit["a_k_norm_2"][0]]
    g = [gains[c][j] for j in range(NG) for c in range(2)] + [unit["b_q_norm_2"][0], unit["b_k_norm_2"][0]]
    rot = (np.arange(P) % HD < ROT).astype(np.float32)[:, None]

    def pad4(a):
        return np.concatenate([a.reshape(4, 1), np.zeros((P - 4, 1), np.float32)], 0)
    cols = {
        "g_mix": feat(unit["norm_mix_pre"]), "g_mlp": feat(unit["norm_mlp_pre"]),
        "g_a": feat(unit["attn_norm_2"][0]), "g_b": feat(unit["attn_norm_2"][1]),
        "g_fa": feat(unit["ffn_norm_2"][0]), "g_fb": feat(unit["ffn_norm_2"][1]),
        "g_heads": np.concatenate([feat(unit["diff_norm"])] * NH1 + [feat(unit["mlstm_norm"])], 1),
        "cw1": unit["conv_w"][0].reshape(CONV1, 4, P).transpose(2, 1, 0),
        "cb1": unit["conv_b"][0].reshape(4, P).T,
        "b_i": pad4(unit["b_igate"]), "b_f": pad4(unit["b_fgate"]),
        "gains": np.stack([twice(v) for v in g], 1),
        "rotated": rot, "unrotated": 1 - rot,
    }
    for layer, tag in enumerate("ab"):
        w = np.concatenate([unit["ffn_conv_w_2"][layer], unit["ffn_conv_b_2"][layer][None]], 0)
        w = w.reshape(4, 2, U2, 2, P)
        cols[f"cw2{tag}"] = w.transpose(4, 2, 1, 3, 0)
    rows = {
        "mix_post": unit["norm_mix_post"][0], "mlp_post": unit["norm_mlp_post"][0],
        "lambda": np.concatenate([unit[f"lambda_{n}"][0] for n in ("q1", "k1", "q2", "k2")]),
        "gain_rows": np.concatenate([v[:ROT] for v in g]),
    }
    packed, at_col = pack(cols)
    at_row, n = {}, 0
    for name, a in rows.items():
        at_row[name] = (n, a.size)
        n += a.size
    return packed, at_col, np.ascontiguousarray(np.concatenate(list(rows.values()))[None], dtype=np.float32), at_row


def kernel(**inputs):
    import concourse.bacc as _bacc
    from concourse.bass_utils import run_bass_kernel_spmd as _run

    nc = _bacc.Bacc("TRN2", target_bir_lowering=False, num_devices=1)
    consts, at_const = pack(constant_tables())
    cols, at_col, rows, at_row = lay_out(inputs)
    arrays = {"consts": consts, "cols": cols, "rows": rows}
    for name in ("x", "w_in", "w_out", "w_up", "w_down"):
        arrays[name] = np.ascontiguousarray(inputs[name])
    for name in ("a_w_qkv", "a_w_o", "b_w_qkv", "b_w_o", "ffn_w_up", "ffn_w_down"):
        arrays[name] = np.ascontiguousarray(inputs[name + "_2"])
    up = arrays["ffn_w_up"]
    arrays["ffn_w_up"] = np.ascontiguousarray(
        up.reshape(2, D, 2, U2, 256).transpose(0, 1, 3, 2, 4).reshape(2, D, 2 * FF2))
    args = {n: nc.dram_tensor(f"in_{n}", a.shape, mybir.dt.from_np(a.dtype), kind="ExternalInput").ap()
            for n, a in arrays.items()}
    out = nc.dram_tensor("out_0", (1, S, D), F32, kind="ExternalOutput").ap()
    blocks_kernel(nc, args, out, at_const, at_col, at_row)
    r = _run(nc, [{f"in_{n}": a for n, a in arrays.items()}], core_ids=[0])
    return r.results[0]["out_0"]
```
